# Optimizing a Trainium2 kernel written in Bass

```python
import jax, jax.numpy as jnp
from jax import lax
import numpy as np
import math

D_MODEL = 1024
BATCH = 1
SEQ = 1024
DEPTH = 1

GLA_HEADS = 4
GLA_DK = 64
GLA_DV = 128
GLA_RANK = 16
GLA_TAU = 16.0
GLA_CHUNK = 64
SGU_GROUPS = 4
SGU_DC = 128
SGU_CHUNK = 128
D_FF = 4 * D_MODEL
EPS = 1e-6

GLA_QK = GLA_HEADS * GLA_DK
GLA_V = GLA_HEADS * GLA_DV
SGU_W = SGU_GROUPS * SGU_DC
D_MIX = GLA_V + SGU_W
IN_SIZES = (GLA_QK, GLA_QK, GLA_V, GLA_V, GLA_RANK, GLA_RANK, SGU_W, SGU_W)
D_IN = GLA_QK * 2 + GLA_V * 2 + GLA_RANK * 2 + SGU_W * 2
SPLIT_POINTS = (GLA_QK, 2 * GLA_QK, 2 * GLA_QK + GLA_V, 2 * GLA_QK + 2 * GLA_V,
                2 * GLA_QK + 2 * GLA_V + GLA_RANK, 2 * GLA_QK + 2 * GLA_V + 2 * GLA_RANK,
                2 * GLA_QK + 2 * GLA_V + 2 * GLA_RANK + SGU_W)


def rmsnorm(x, g):
    xf = x.astype(jnp.float32)
    y = xf * lax.rsqrt(jnp.mean(xf * xf, axis=-1, keepdims=True) + EPS)
    return (y * g.astype(jnp.float32)).astype(x.dtype)

def gla_one_direction(q, k, v, log_a, strict):
    B, S, H, K = q.shape
    V = v.shape[-1]
    C = GLA_CHUNK
    N = S // C
    q = q.reshape(B, N, C, H, K)
    k = k.reshape(B, N, C, H, K)
    v = v.reshape(B, N, C, H, V)
    b = jnp.cumsum(log_a.reshape(B, N, C, H, K), axis=2)
    b_mid = b[:, :, C // 2:C // 2 + 1]
    q_in = q * jnp.exp(b - b_mid)
    k_in = k * jnp.exp(b_mid - b)
    scores = jnp.einsum('bnchk,bnjhk->bnhcj', q_in, k_in)
    idx = jnp.arange(C)
    mask = (idx[:, None] > idx[None, :]) if strict else (idx[:, None] >= idx[None, :])
    scores = jnp.where(mask, scores, 0.0)
    o_intra = jnp.einsum('bnhcj,bnjhv->bnchv', scores, v)
    b_last = b[:, :, -1]
    kv = jnp.einsum('bnchk,bnchv->bnhkv', k * jnp.exp(b_last[:, :, None] - b), v)

    def step(state, inp):
        dec, kv_n = inp
        return dec[..., None] * state + kv_n, state

    init = jnp.zeros((B, H, K, V), q.dtype)
    _, s_in = lax.scan(step, init, (jnp.moveaxis(jnp.exp(b_last), 1, 0), jnp.moveaxis(kv, 1, 0)))
    s_in = jnp.moveaxis(s_in, 0, 1)
    o_inter = jnp.einsum('bnchk,bnhkv->bnchv', q * jnp.exp(b), s_in)
    return (o_intra + o_inter).reshape(B, S, H, V)

def gla_mixer(q, k, v, g, a_f, a_b, w_a2_f, b_a_f, w_a2_b, b_a_b, norm_g):
    B, S, _ = q.shape
    f32 = jnp.float32
    q = q.astype(f32).reshape(B, S, GLA_HEADS, GLA_DK) * (GLA_DK ** -0.5)
    k = k.astype(f32).reshape(B, S, GLA_HEADS, GLA_DK)
    v = v.astype(f32).reshape(B, S, GLA_HEADS, GLA_DV)
    log_a_f = (jax.nn.log_sigmoid(a_f.astype(f32) @ w_a2_f.astype(f32) + b_a_f.astype(f32)) / GLA_TAU
               ).reshape(B, S, GLA_HEADS, GLA_DK)
    log_a_b = (jax.nn.log_sigmoid(a_b.astype(f32) @ w_a2_b.astype(f32) + b_a_b.astype(f32)) / GLA_TAU
               ).reshape(B, S, GLA_HEADS, GLA_DK)
    o_f = gla_one_direction(q, k, v, log_a_f, False)
    flip = lambda t: jnp.flip(t, axis=1)
    o_b = flip(gla_one_direction(flip(q), flip(k), flip(v), flip(log_a_b), True))
    o = o_f + o_b
    o = o * lax.rsqrt(jnp.mean(o * o, axis=-1, keepdims=True) + EPS) * norm_g.astype(f32)
    return o.reshape(B, S, GLA_V) * jax.nn.silu(g.astype(f32))

def sgu_mixer(u, v, norm_g, w_s, b_s):
    B, S, _ = u.shape
    f32 = jnp.float32
    N = S // SGU_CHUNK
    v = v.astype(f32).reshape(B, N, SGU_CHUNK, SGU_GROUPS, SGU_DC)
    v = v * lax.rsqrt(jnp.mean(v * v, axis=-1, keepdims=True) + EPS) * norm_g.astype(f32)
    mixed = jnp.einsum('gpq,bnqgc->bnpgc', w_s.astype(f32), v) + b_s.astype(f32).T[:, :, None]
    return u.astype(f32) * mixed.reshape(B, S, SGU_W)

def first_inputs(seed: int = 0) -> dict:
    key = jax.random.key(seed)
    ks = jax.random.split(key, 20)
    nrm = lambda k, shape, s: jax.random.normal(k, shape, jnp.float32) * s
    L = DEPTH
    return {
        "x": nrm(ks[0], (BATCH, SEQ, D_MODEL), 1.0),
        "norm_mix_g": 1.0 + nrm(ks[1], (L, D_MODEL), 0.02),
        "w_in": nrm(ks[2], (L, D_MODEL, D_IN), D_MODEL ** -0.5),
        "w_a2_fwd": nrm(ks[3], (L, GLA_RANK, GLA_QK), GLA_RANK ** -0.5),
        "b_a_fwd": 1.5 + nrm(ks[4], (L, GLA_QK), 1.0),
        "w_a2_bwd": nrm(ks[5], (L, GLA_RANK, GLA_QK), GLA_RANK ** -0.5),
        "b_a_bwd": 1.5 + nrm(ks[6], (L, GLA_QK), 1.0),
        "gla_norm_g": 1.0 + nrm(ks[7], (L, GLA_HEADS, GLA_DV), 0.02),
        "sgu_norm_g": 1.0 + nrm(ks[8], (L, SGU_GROUPS, SGU_DC), 0.02),
        "w_s": nrm(ks[9], (L, SGU_GROUPS, SGU_CHUNK, SGU_CHUNK), SGU_CHUNK ** -0.5),
        "b_s": 1.0 + nrm(ks[10], (L, SGU_GROUPS, SGU_CHUNK), 0.1),
        "w_out": nrm(ks[11], (L, D_MIX, D_MODEL), D_MIX ** -0.5),
        "norm_mlp_g": 1.0 + nrm(ks[12], (L, D_MODEL), 0.02),
        "w_mlp1": nrm(ks[13], (L, D_MODEL, D_FF), D_MODEL ** -0.5),
        "w_mlp2": nrm(ks[14], (L, D_FF, D_MODEL), D_FF ** -0.5),
        "final_norm_g": 1.0 + nrm(ks[15], (D_MODEL,), 0.02),
    }

def first_block(x, norm_mix_g, w_in, w_a2_fwd, b_a_fwd, w_a2_bwd, b_a_bwd, gla_norm_g,
              sgu_norm_g, w_s, b_s, w_out, norm_mlp_g, w_mlp1, w_mlp2, final_norm_g):
    for l in range(DEPTH):
        h = rmsnorm(x, norm_mix_g[l])
        z = h @ w_in[l]
        q, k, v, g, a_f, a_b, su, sv = jnp.split(z, SPLIT_POINTS, axis=-1)
        o_gla = gla_mixer(q, k, v, g, a_f, a_b, w_a2_fwd[l], b_a_fwd[l],
                          w_a2_bwd[l], b_a_bwd[l], gla_norm_g[l]).astype(x.dtype)
        o_sgu = sgu_mixer(jax.nn.gelu(su, approximate=False), jax.nn.gelu(sv, approximate=False),
                          sgu_norm_g[l], w_s[l], b_s[l]).astype(x.dtype)
        x = x + jnp.concatenate([o_gla, o_sgu], axis=-1) @ w_out[l]
        h = rmsnorm(x, norm_mlp_g[l])
        x = x + jnp.square(jax.nn.relu(h @ w_mlp1[l])) @ w_mlp2[l]
    return rmsnorm(x, final_norm_g)


_first_inputs = first_inputs


def first_inputs(seed=0):
    import zlib

    import numpy as np

    out = dict(_first_inputs(seed))
    spreads = {}
    factors = {}
    for name, (base, spread) in spreads.items():
        noise = np.random.default_rng([zlib.crc32(name.encode()), seed]).standard_normal(out[name].shape)
        drawn = base * np.exp(spread * noise) if base else spread * noise
        out[name] = __import__('jax').numpy.asarray(drawn.astype(out[name].dtype))
    for name, factor in factors.items():
        out[name] = (out[name] * factor).astype(out[name].dtype)
    return out


_narrow_inputs = first_inputs


def first_inputs(seed=0):

    out = dict(_narrow_inputs(seed))
    wider = {'gla_norm_g': 8.98, 'sgu_norm_g': 8.66, 'norm_mlp_g': 4.05, 'final_norm_g': 3.2}
    for name, times in wider.items():
        mean = out[name].mean()
        out[name] = (mean + times * (out[name] - mean)).astype(out[name].dtype)
    return out


D_MIX_2 = 2 * D_MODEL
D_SSM = D_MIX_2 // 2
SSM_HEAD_DIM = 64
SSM_HEADS = D_SSM // SSM_HEAD_DIM
SSM_GROUPS = 2
SSM_HEADS_PER_GROUP = SSM_HEADS // SSM_GROUPS
D_STATE = 128
D_CONV = 5
CHUNK = 128
D_XBC = D_SSM + 2 * SSM_GROUPS * D_STATE
D_ATTN = D_MIX_2 - D_SSM
ATTN_HEADS = 8
ATTN_HEAD_DIM = D_ATTN // ATTN_HEADS // 2
ATTN_V_DIM = 2 * ATTN_HEAD_DIM
Q_BLOCK = 128
D_IN_PROJ = D_SSM + D_XBC + 2 * SSM_HEADS + 4 * D_ATTN
ALPHA = (2.0 * DEPTH) ** 0.25
BETA = (8.0 * DEPTH) ** -0.25
LN_EPS = 1e-5
RMS_EPS = 1e-5


def layer_norm(x, g, b):
    xf = x.astype(jnp.float32)
    mu = jnp.mean(xf, axis=-1, keepdims=True)
    var = jnp.mean(jnp.square(xf - mu), axis=-1, keepdims=True)
    return ((xf - mu) * lax.rsqrt(var + LN_EPS) * g + b).astype(x.dtype)

def rms_norm(x, g):
    xf = x.astype(jnp.float32)
    ms = jnp.mean(jnp.square(xf), axis=-1, keepdims=True)
    return (xf * lax.rsqrt(ms + RMS_EPS) * g).astype(x.dtype)

def centred_dwconv(u, w, b):
    out = lax.conv_general_dilated(
        u, w[:, None, :].astype(u.dtype), window_strides=(1,),
        padding=[(D_CONV // 2, D_CONV // 2)],
        dimension_numbers=("NWC", "WIO", "NWC"),
        feature_group_count=u.shape[-1])
    return out + b.astype(u.dtype)

def ssd_chunked(x, dt, A, Bm, Cm):
    b, s, g, j, p = x.shape
    n = Bm.shape[-1]
    nc = s // CHUNK
    x = x.reshape(b, nc, CHUNK, g, j, p)
    dt = dt.reshape(b, nc, CHUNK, g, j)
    Bm = Bm.reshape(b, nc, CHUNK, g, n)
    Cm = Cm.reshape(b, nc, CHUNK, g, n)
    a_cs = jnp.cumsum(dt * A, axis=2)
    xdt = x * dt[..., None]
    lower = jnp.tril(jnp.ones((CHUNK, CHUNK), dtype=bool))[None, None, :, :, None, None]
    seg = a_cs[:, :, :, None] - a_cs[:, :, None, :]
    decay = jnp.exp(jnp.where(lower, seg, -jnp.inf))
    cb = jnp.einsum("bclgn,bcsgn->bclsg", Cm, Bm)
    y_diag = jnp.einsum("bclsgj,bcsgjp->bclgjp", cb[..., None] * decay, xdt)
    decay_to_end = jnp.exp(a_cs[:, :, -1:] - a_cs)
    chunk_states = jnp.einsum("bclgn,bclgjp->bcgjpn", Bm, xdt * decay_to_end[..., None])
    chunk_decay = jnp.exp(a_cs[:, :, -1])

    def step(h, inp):
        st, dec = inp
        return dec[..., None, None] * h + st, h

    h0 = jnp.zeros((b, g, j, p, n), x.dtype)
    _, prev = lax.scan(step, h0, (jnp.moveaxis(chunk_states, 1, 0),
                                  jnp.moveaxis(chunk_decay, 1, 0)))
    prev = jnp.moveaxis(prev, 0, 1)
    y_off = jnp.einsum("bclgn,bcgjpn->bclgjp", Cm, prev) * jnp.exp(a_cs)[..., None]
    return (y_diag + y_off).reshape(b, s, g, j, p)

def bidirectional_ssd(xs, dt_f, dt_b, Bm, Cm, A_log_f, A_log_b, dt_bias_f, dt_bias_b, D):
    b, s = xs.shape[:2]
    shp = (SSM_GROUPS, SSM_HEADS_PER_GROUP)
    A_f = -jnp.exp(A_log_f.astype(jnp.float32)).reshape(shp)
    A_b = -jnp.exp(A_log_b.astype(jnp.float32)).reshape(shp)
    dtf = jax.nn.softplus(dt_f.astype(jnp.float32) + dt_bias_f.astype(jnp.float32)).reshape(b, s, *shp)
    dtb = jax.nn.softplus(dt_b.astype(jnp.float32) + dt_bias_b.astype(jnp.float32)).reshape(b, s, *shp)
    xf, Bf, Cf = xs.astype(jnp.float32), Bm.astype(jnp.float32), Cm.astype(jnp.float32)
    flip = lambda t: jnp.flip(t, axis=1)
    y_fwd = ssd_chunked(xf, dtf, A_f, Bf, Cf)
    y_bwd = flip(ssd_chunked(flip(xf), flip(dtb), A_b, flip(Bf), flip(Cf)))
    y = y_fwd + y_bwd + D.astype(jnp.float32).reshape(*shp, 1) * xf
    return y.astype(xs.dtype)

def diff_attention(q, k, v, lam, slopes):
    b, s, h, _, d = q.shape
    nb = s // Q_BLOCK
    scale = ATTN_HEAD_DIM ** -0.5
    k_pos = jnp.arange(s)
    qb = jnp.moveaxis(q.reshape(b, nb, Q_BLOCK, h, 2, d), 1, 0)
    starts = jnp.arange(nb) * Q_BLOCK

    def block(args):
        qi, start = args
        scores = jnp.einsum("bqhrd,bshrd->bhrqs", qi, k).astype(jnp.float32) * scale
        dist = jnp.abs((start + jnp.arange(Q_BLOCK))[:, None] - k_pos[None, :]).astype(jnp.float32)
        scores = scores - slopes[None, :, None, None, None] * dist[None, None, None]
        probs = jax.nn.softmax(scores, axis=-1)
        w = probs[:, :, 0] - lam * probs[:, :, 1]
        return jnp.einsum("bhqs,bshe->bqhe", w.astype(v.dtype), v)

    o = lax.map(block, (qb, starts))
    return jnp.moveaxis(o, 0, 1).reshape(b, s, h, v.shape[-1])

def hybrid_layer(h, layer_idx, w_in, conv_w, conv_b, A_log_f, A_log_b, dt_bias_f, dt_bias_b,
                 D, ssm_norm_g, lq1, lk1, lq2, lk2, subln_g, w_out, ln_g, ln_b):
    b, s, _ = h.shape
    proj = jnp.einsum("bsd,de->bse", h, w_in.astype(h.dtype))
    offs = np.cumsum([D_SSM, D_XBC, SSM_HEADS, SSM_HEADS, D_ATTN, D_ATTN, D_ATTN, D_ATTN])[:-1].tolist()
    z, xbc, dt_f, dt_b, q, k, v, g = jnp.split(proj, offs, axis=-1)

    xbc = jax.nn.silu(centred_dwconv(xbc, conv_w, conv_b))
    xs, Bm, Cm = jnp.split(xbc, [D_SSM, D_SSM + SSM_GROUPS * D_STATE], axis=-1)
    xs = xs.reshape(b, s, SSM_GROUPS, SSM_HEADS_PER_GROUP, SSM_HEAD_DIM)
    Bm = Bm.reshape(b, s, SSM_GROUPS, D_STATE)
    Cm = Cm.reshape(b, s, SSM_GROUPS, D_STATE)
    y = bidirectional_ssd(xs, dt_f, dt_b, Bm, Cm, A_log_f, A_log_b, dt_bias_f, dt_bias_b, D)
    y = y.reshape(b, s, SSM_GROUPS, D_SSM // SSM_GROUPS)
    zg = jax.nn.silu(z).reshape(b, s, SSM_GROUPS, D_SSM // SSM_GROUPS)
    y_ssm = rms_norm(y * zg, ssm_norm_g.reshape(SSM_GROUPS, -1)).reshape(b, s, D_SSM)

    q = q.reshape(b, s, ATTN_HEADS, 2, ATTN_HEAD_DIM)
    k = k.reshape(b, s, ATTN_HEADS, 2, ATTN_HEAD_DIM)
    v = v.reshape(b, s, ATTN_HEADS, ATTN_V_DIM)
    lam_init = 0.8 - 0.6 * math.exp(-0.3 * layer_idx)
    lam = (jnp.exp(jnp.sum(lq1.astype(jnp.float32) * lk1.astype(jnp.float32)))
           - jnp.exp(jnp.sum(lq2.astype(jnp.float32) * lk2.astype(jnp.float32))) + lam_init)
    slopes = jnp.exp2(-8.0 * (jnp.arange(ATTN_HEADS, dtype=jnp.float32) + 1.0) / ATTN_HEADS)
    o = diff_attention(q, k, v, lam, slopes)
    o = rms_norm(o, subln_g) * (1.0 - lam_init)
    y_attn = o.reshape(b, s, D_ATTN) * jax.nn.silu(g)

    mix = jnp.einsum("bse,ed->bsd", jnp.concatenate([y_ssm, y_attn], axis=-1), w_out.astype(h.dtype))
    return layer_norm(ALPHA * h + mix, ln_g, ln_b)

def second_inputs(seed: int = 0) -> dict:
    key = jax.random.key(seed)
    ks = jax.random.split(key, 24)
    f32 = jnp.float32
    x = jax.random.normal(ks[0], (BATCH, SEQ, D_MODEL), f32)
    ln_emb_g = 1.0 + 0.02 * jax.random.normal(ks[1], (D_MODEL,), f32)
    ln_emb_b = 0.02 * jax.random.normal(ks[2], (D_MODEL,), f32)
    x_start = D_SSM
    v_start = D_SSM + D_XBC + 2 * SSM_HEADS + 2 * D_ATTN
    col_scale = (jnp.ones((D_IN_PROJ,), f32)
                 .at[x_start:x_start + D_SSM].set(BETA)
                 .at[v_start:v_start + D_ATTN].set(BETA))
    w_in = jax.random.normal(ks[3], (DEPTH, D_MODEL, D_IN_PROJ), f32) * (D_MODEL ** -0.5) * col_scale
    conv_w = jax.random.normal(ks[4], (DEPTH, D_CONV, D_XBC), f32) * (D_CONV ** -0.5)
    conv_b = 0.01 * jax.random.normal(ks[5], (DEPTH, D_XBC), f32)
    A_log_fwd = jnp.log(jax.random.uniform(ks[6], (DEPTH, SSM_HEADS), f32, 1.0, 16.0))
    A_log_bwd = jnp.log(jax.random.uniform(ks[7], (DEPTH, SSM_HEADS), f32, 1.0, 16.0))
    dt_f0 = jnp.exp(jax.random.uniform(ks[8], (DEPTH, SSM_HEADS), f32, math.log(1e-3), math.log(1e-1)))
    dt_b0 = jnp.exp(jax.random.uniform(ks[9], (DEPTH, SSM_HEADS), f32, math.log(1e-3), math.log(1e-1)))
    dt_bias_fwd = dt_f0 + jnp.log(-jnp.expm1(-dt_f0))
    dt_bias_bwd = dt_b0 + jnp.log(-jnp.expm1(-dt_b0))
    D_skip = 1.0 + 0.1 * jax.random.normal(ks[10], (DEPTH, SSM_HEADS), f32)
    ssm_norm_g = 1.0 + 0.02 * jax.random.normal(ks[11], (DEPTH, D_SSM), f32)
    lambda_q1 = 0.1 * jax.random.normal(ks[12], (DEPTH, ATTN_HEAD_DIM), f32)
    lambda_k1 = 0.1 * jax.random.normal(ks[13], (DEPTH, ATTN_HEAD_DIM), f32)
    lambda_q2 = 0.1 * jax.random.normal(ks[14], (DEPTH, ATTN_HEAD_DIM), f32)
    lambda_k2 = 0.1 * jax.random.normal(ks[15], (DEPTH, ATTN_HEAD_DIM), f32)
    subln_g = 1.0 + 0.02 * jax.random.normal(ks[16], (DEPTH, ATTN_V_DIM), f32)
    w_out = jax.random.normal(ks[17], (DEPTH, D_MIX_2, D_MODEL), f32) * (D_MIX_2 ** -0.5) * BETA
    ln_g = 1.0 + 0.02 * jax.random.normal(ks[18], (DEPTH, D_MODEL), f32)
    ln_b = 0.02 * jax.random.normal(ks[19], (DEPTH, D_MODEL), f32)
    return {"x": x, "ln_emb_g": ln_emb_g, "ln_emb_b": ln_emb_b, "w_in": w_in,
            "conv_w": conv_w, "conv_b": conv_b, "A_log_fwd": A_log_fwd, "A_log_bwd": A_log_bwd,
            "dt_bias_fwd": dt_bias_fwd, "dt_bias_bwd": dt_bias_bwd, "D_skip": D_skip,
            "ssm_norm_g": ssm_norm_g, "lambda_q1": lambda_q1, "lambda_k1": lambda_k1,
            "lambda_q2": lambda_q2, "lambda_k2": lambda_k2, "subln_g": subln_g,
            "w_out": w_out, "ln_g": ln_g, "ln_b": ln_b}

def second_block(x, ln_emb_g, ln_emb_b, w_in, conv_w, conv_b, A_log_fwd, A_log_bwd,
              dt_bias_fwd, dt_bias_bwd, D_skip, ssm_norm_g, lambda_q1, lambda_k1,
              lambda_q2, lambda_k2, subln_g, w_out, ln_g, ln_b):
    h = layer_norm(x, ln_emb_g, ln_emb_b)
    for l in range(DEPTH):
        h = hybrid_layer(h, l, w_in[l], conv_w[l], conv_b[l], A_log_fwd[l], A_log_bwd[l],
                         dt_bias_fwd[l], dt_bias_bwd[l], D_skip[l], ssm_norm_g[l],
                         lambda_q1[l], lambda_k1[l], lambda_q2[l], lambda_k2[l],
                         subln_g[l], w_out[l], ln_g[l], ln_b[l])
    return h


_first_inputs_2 = second_inputs


def second_inputs(seed=0):
    import zlib

    import numpy as np

    out = dict(_first_inputs_2(seed))
    spreads = {}
    factors = {'conv_b': 5.483,
     'D_skip': 2.94,
     'ssm_norm_g': 26.879,
     'lambda_q1': 5.092,
     'lambda_q2': 64.0,
     'lambda_k2': 3.921,
     'subln_g': 54.109,
     'ln_g': 8.436,
     'ln_b': 8.255}
    for name, (base, spread) in spreads.items():
        noise = np.random.default_rng([zlib.crc32(name.encode()), seed]).standard_normal(out[name].shape)
        drawn = base * np.exp(spread * noise) if base else spread * noise
        out[name] = __import__('jax').numpy.asarray(drawn.astype(out[name].dtype))
    for name, factor in factors.items():
        out[name] = (out[name] * factor).astype(out[name].dtype)
    return out


_narrow_inputs_2 = second_inputs


def second_inputs(seed=0):

    out = dict(_narrow_inputs_2(seed))
    wider = {'ssm_norm_g': 4.48, 'subln_g': 4.53, 'ln_g': 3.27, 'ln_b': 3.27}
    for name, times in wider.items():
        mean = out[name].mean()
        out[name] = (mean + times * (out[name] - mean)).astype(out[name].dtype)
    return out


PLE_DIM = 256
W_CONV = D_MODEL
CONV_GROUPS = 8
CONV_K = 31
HG_HEAD_DIM = 128
W_HGRN = D_MODEL
HG_HEADS = W_HGRN // HG_HEAD_DIM
W_MIX = W_CONV + W_HGRN
CHUNK_3 = 64
W_IN_COLS = 3 * W_CONV + 4 * W_HGRN


def rms_norm_3(x, g):
    xf = x.astype(jnp.float32)
    y = xf * lax.rsqrt(jnp.mean(xf * xf, axis=-1, keepdims=True) + EPS)
    return (y * g.astype(jnp.float32)).astype(x.dtype)

def group_layer_norm(x, g, b, n_groups):
    shp = x.shape
    xf = x.astype(jnp.float32).reshape(shp[:-1] + (n_groups, shp[-1] // n_groups))
    mu = jnp.mean(xf, axis=-1, keepdims=True)
    var = jnp.mean(jnp.square(xf - mu), axis=-1, keepdims=True)
    y = ((xf - mu) * lax.rsqrt(var + EPS)).reshape(shp)
    return (y * g.astype(jnp.float32) + b.astype(jnp.float32)).astype(x.dtype)

def conformer_conv_branch(z_val, z_glu, z_gate, conv_w, conv_b, cn_g, cn_b, w_pw2, b_pw2):
    v = z_val * jax.nn.sigmoid(z_glu)
    y = lax.conv_general_dilated(
        v, conv_w[:, None, :].astype(v.dtype),
        window_strides=(1,), padding=[(CONV_K - 1, 0)],
        dimension_numbers=("NWC", "WIO", "NWC"),
        feature_group_count=W_CONV) + conv_b.astype(v.dtype)
    y = jax.nn.silu(group_layer_norm(y, cn_g, cn_b, CONV_GROUPS))
    y = y @ w_pw2.astype(y.dtype) + b_pw2.astype(y.dtype)
    return y * jax.nn.silu(z_gate)

def _gla_chunk_step(S, inp):
    q, k, v, lf = inp
    b = jnp.cumsum(lf, axis=2)
    o_inter = jnp.einsum("bhck,bhkv->bhcv", q * jnp.exp(b), S)
    t_idx = jnp.arange(CHUNK_3)
    causal = (t_idx[:, None] >= t_idx[None, :])[None, None, :, :, None]
    diff = b[:, :, :, None, :] - b[:, :, None, :, :]
    decay = jnp.exp(jnp.where(causal, diff, -jnp.inf))
    A = jnp.einsum("bhtsk,bhsk->bhts", q[:, :, :, None, :] * decay, k)
    o_intra = jnp.einsum("bhts,bhsv->bhtv", A, v)
    b_last = b[:, :, -1, :]
    k_dec = k * jnp.exp(b_last[:, :, None, :] - b)
    S_new = jnp.exp(b_last)[..., None] * S + jnp.einsum("bhsk,bhsv->bhkv", k_dec, v)
    return S_new, o_inter + o_intra

def hgrn2_branch(zq, zf, zi, zg, lb, onorm_g):
    B, T, _ = zq.shape
    n_chunks = T // CHUNK_3
    lbf = lb.astype(jnp.float32)
    zf32 = zf.astype(jnp.float32)
    f = lbf + (1.0 - lbf) * jax.nn.sigmoid(zf32)
    log_f = jnp.log(f)
    k = (1.0 - lbf) * jax.nn.sigmoid(-zf32)
    q = jax.nn.silu(zq.astype(jnp.float32))
    v = zi.astype(jnp.float32)

    def to_chunks(t):
        return t.reshape(B, n_chunks, CHUNK_3, HG_HEADS, HG_HEAD_DIM).transpose(1, 0, 3, 2, 4)

    S0 = jnp.zeros((B, HG_HEADS, HG_HEAD_DIM, HG_HEAD_DIM), jnp.float32)
    _, o = lax.scan(_gla_chunk_step, S0,
                    (to_chunks(q), to_chunks(k), to_chunks(v), to_chunks(log_f)))
    o = o.transpose(1, 0, 3, 2, 4).reshape(B, T, HG_HEADS, HG_HEAD_DIM)
    o = rms_norm_3(o, onorm_g.reshape(HG_HEADS, HG_HEAD_DIM))
    o = o.reshape(B, T, W_HGRN).astype(zq.dtype)
    return o * jax.nn.silu(zg)

def third_inputs(seed: int = 0) -> dict:
    key = jax.random.key(seed)
    ks = jax.random.split(key, 20)
    f32 = jnp.float32
    nrm = lambda k, s, sc: (jax.random.normal(k, s, f32) * sc).astype(f32)
    return {
        "x": jax.random.normal(ks[0], (BATCH, SEQ, D_MODEL), f32),
        "p": jax.random.normal(ks[1], (DEPTH, BATCH, SEQ, PLE_DIM), f32),
        "ln_g": 1.0 + nrm(ks[2], (DEPTH, D_MODEL), 0.02),
        "w_in": nrm(ks[3], (DEPTH, D_MODEL, W_IN_COLS), D_MODEL ** -0.5),
        "conv_w": nrm(ks[4], (DEPTH, CONV_K, W_CONV), CONV_K ** -0.5),
        "conv_b": nrm(ks[5], (DEPTH, W_CONV), 0.01),
        "cnorm_g": 1.0 + nrm(ks[6], (DEPTH, W_CONV), 0.02),
        "cnorm_b": nrm(ks[7], (DEPTH, W_CONV), 0.01),
        "w_pw2": nrm(ks[8], (DEPTH, W_CONV, W_CONV), W_CONV ** -0.5),
        "b_pw2": nrm(ks[9], (DEPTH, W_CONV), 0.01),
        "lb_logits": nrm(ks[10], (DEPTH + 1, W_HGRN), 0.1),
        "onorm_g": 1.0 + nrm(ks[11], (DEPTH, W_HGRN), 0.02),
        "w_out": nrm(ks[12], (DEPTH, W_MIX, D_MODEL), W_MIX ** -0.5),
        "pe_norm_g": 1.0 + nrm(ks[13], (DEPTH, D_MODEL), 0.02),
        "w_pg": nrm(ks[14], (DEPTH, D_MODEL, D_MODEL), D_MODEL ** -0.5),
        "w_pp": nrm(ks[15], (DEPTH, PLE_DIM, D_MODEL), PLE_DIM ** -0.5),
        "final_g": 1.0 + nrm(ks[16], (D_MODEL,), 0.02),
    }

def third_block(x, p, ln_g, w_in, conv_w, conv_b, cnorm_g, cnorm_b, w_pw2, b_pw2,
              lb_logits, onorm_g, w_out, pe_norm_g, w_pg, w_pp, final_g):
    lbs = jnp.cumsum(jax.nn.softmax(lb_logits.astype(jnp.float32), axis=0), axis=0)
    h = x
    split_pts = [W_CONV, 2 * W_CONV, 3 * W_CONV,
                 3 * W_CONV + W_HGRN, 3 * W_CONV + 2 * W_HGRN, 3 * W_CONV + 3 * W_HGRN]
    for i in range(DEPTH):
        u = rms_norm_3(h, ln_g[i])
        z = u @ w_in[i].astype(u.dtype)
        c_val, c_glu, c_gate, hq, hf, hi, hg = jnp.split(z, split_pts, axis=-1)
        y_conv = conformer_conv_branch(c_val, c_glu, c_gate, conv_w[i], conv_b[i],
                                       cnorm_g[i], cnorm_b[i], w_pw2[i], b_pw2[i])
        y_hgrn = hgrn2_branch(hq, hf, hi, hg, lbs[i], onorm_g[i])
        y = jnp.concatenate([y_conv, y_hgrn.astype(y_conv.dtype)], axis=-1)
        h = h + y @ w_out[i].astype(y.dtype)
        pe = p[i] @ w_pp[i].astype(p.dtype)
        gate = jax.nn.sigmoid(rms_norm_3(h, pe_norm_g[i]) @ w_pg[i].astype(h.dtype))
        h = h + gate * pe.astype(h.dtype)
    return rms_norm_3(h, final_g)


_first_inputs_3 = third_inputs


def third_inputs(seed=0):
    import zlib

    import numpy as np

    out = dict(_first_inputs_3(seed))
    spreads = {}
    factors = {'ln_g': 4.682,
     'conv_b': 27.575,
     'cnorm_g': 147.001,
     'cnorm_b': 200.0,
     'b_pw2': 200.0,
     'lb_logits': 8.0,
     'onorm_g': 109.316,
     'pe_norm_g': 200.0,
     'final_g': 23.508,
     'w_pg': 22.904,
     'p': 7.119,
     'w_pp': 7.141}
    for name, (base, spread) in spreads.items():
        noise = np.random.default_rng([zlib.crc32(name.encode()), seed]).standard_normal(out[name].shape)
        drawn = base * np.exp(spread * noise) if base else spread * noise
        out[name] = __import__('jax').numpy.asarray(drawn.astype(out[name].dtype))
    for name, factor in factors.items():
        out[name] = (out[name] * factor).astype(out[name].dtype)
    return out


_narrow_inputs_3 = third_inputs


def third_inputs(seed=0):

    out = dict(_narrow_inputs_3(seed))
    wider = {'cnorm_g': 3.85,
     'cnorm_b': 5.66,
     'b_pw2': 4.14,
     'onorm_g': 3.86,
     'pe_norm_g': 6.46,
     'final_g': 3.22}
    for name, times in wider.items():
        mean = out[name].mean()
        out[name] = (mean + times * (out[name] - mean)).astype(out[name].dtype)
    return out


def setup_inputs(seed=0):
    out = dict(first_inputs(seed))
    for name, value in second_inputs(seed + 1).items():
        if name != "x":
            out[name + "_2"] = value
    for name, value in third_inputs(seed + 2).items():
        if name != "x":
            out[name + "_3"] = value
    return out


def reference(
    x, norm_mix_g, w_in, w_a2_fwd, b_a_fwd, w_a2_bwd, b_a_bwd, gla_norm_g, sgu_norm_g, w_s, b_s,
    w_out, norm_mlp_g, w_mlp1, w_mlp2, final_norm_g, ln_emb_g_2, ln_emb_b_2, w_in_2, conv_w_2,
    conv_b_2, A_log_fwd_2, A_log_bwd_2, dt_bias_fwd_2, dt_bias_bwd_2, D_skip_2, ssm_norm_g_2,
    lambda_q1_2, lambda_k1_2, lambda_q2_2, lambda_k2_2, subln_g_2, w_out_2, ln_g_2, ln_b_2, p_3,
    ln_g_3, w_in_3, conv_w_3, conv_b_3, cnorm_g_3, cnorm_b_3, w_pw2_3, b_pw2_3, lb_logits_3,
    onorm_g_3, w_out_3, pe_norm_g_3, w_pg_3, w_pp_3, final_g_3,
):
    x = first_block(
        x, norm_mix_g, w_in, w_a2_fwd, b_a_fwd, w_a2_bwd, b_a_bwd, gla_norm_g, sgu_norm_g, w_s,
        b_s, w_out, norm_mlp_g, w_mlp1, w_mlp2, final_norm_g,
    )
    x = second_block(
        x, ln_emb_g_2, ln_emb_b_2, w_in_2, conv_w_2, conv_b_2, A_log_fwd_2, A_log_bwd_2,
        dt_bias_fwd_2, dt_bias_bwd_2, D_skip_2, ssm_norm_g_2, lambda_q1_2, lambda_k1_2,
        lambda_q2_2, lambda_k2_2, subln_g_2, w_out_2, ln_g_2, ln_b_2,
    )
    return third_block(
        x, p_3, ln_g_3, w_in_3, conv_w_3, conv_b_3, cnorm_g_3, cnorm_b_3, w_pw2_3, b_pw2_3,
        lb_logits_3, onorm_g_3, w_out_3, pe_norm_g_3, w_pg_3, w_pp_3, final_g_3,
    )


_drawn_inputs = setup_inputs


def setup_inputs(seed=0):
    import zlib

    import numpy as np

    out = dict(_drawn_inputs(seed))
    spreads = {}
    factors = {}
    for name, (base, spread) in spreads.items():
        noise = np.random.default_rng([zlib.crc32(name.encode()), seed]).standard_normal(out[name].shape)
        drawn = base * np.exp(spread * noise) if base else spread * noise
        out[name] = __import__('jax').numpy.asarray(drawn.astype(out[name].dtype))
    for name, factor in factors.items():
        out[name] = (out[name] * factor).astype(out[name].dtype)
    return out
```

```python
import math
from contextlib import ExitStack

import numpy as np
import concourse.bass as bass
from concourse import mybir

F32 = mybir.dt.float32
F32R = mybir.dt.float32r
I32 = mybir.dt.int32
ALU = mybir.AluOpType
ACT = mybir.ActivationFunctionType
AX = mybir.AxisListType
ADD, SUB, MUL, MAX, MIN = ALU.add, ALU.subtract, ALU.mult, ALU.max, ALU.min
ALPHA = 2.0 ** 0.25
S = 1024
NT = 8


class Queue:

    def __init__(self, sem):
        self.sem, self.n, self.items = sem, 0, []

    def __call__(self, fn, *a, w=(), inc=True, **k):
        self.n += inc
        self.items.append((fn, a, k, list(w), self.sem if inc else None, 1))
        return (self.sem, self.n)

    def dma(self, fn, out, in_, sem, w=()):
        self.items.append((fn, (out, in_), {}, list(w), sem, 16))

    def later(self, fn):
        self.items.append((fn, None, None, [], None, 0))

    def now(self):
        return (self.sem, self.n)

    def emit(self, eng):
        seen = {}

        def wait(w):
            for sem, v in w:
                if v > 0 and seen.get(id(sem), 0) < v:
                    eng.wait_ge(sem, v)
                    seen[id(sem)] = v
        for fn, a, k, w, sem, by in self.items:
            if a is None:
                fn(wait)
                continue
            wait(w)
            ins = fn(*a, **k)
            if sem is not None:
                ins.then_inc(sem, by)


class Slot:

    def __init__(self, t):
        self.t, self.w = t, []


class Ring:
    def __init__(self, ts):
        self.s, self.i = [Slot(t) for t in ts], -1

    def get(self):
        self.i = (self.i + 1) % len(self.s)
        return self.s[self.i]


def bc(ap, shape):
    return ap.broadcast_to(shape)


def build(nc, A, out, upto=3, tap=None):
    ctx = ExitStack()
    with ctx:
        program(nc, A, out, ctx, upto, tap)


def program(nc, A, out, ctx, upto, tap):
    names = [0]

    def sbt(c, shape, dt=F32):
        names[0] += 1
        return c.enter_context(nc.sbuf_tensor(f"t{names[0]}", shape, dt))

    def sem(name):
        return ctx.enter_context(nc.semaphore(name))

    PE, AC, DV, PO = (Queue(sem(n)) for n in ("s_pe", "s_ac", "s_dv", "s_po"))
    SP = Queue(sem("s_sp"))
    T, V, G, C = nc.tensor, nc.vector, nc.gpsimd, nc.scalar
    dram = nc.dram_tensor
    YM = dram("ym_scratch", [2048, S], F32, kind="Internal").ap()
    XD = dram("x_scratch", [S, 1024], F32, kind="Internal").ap()
    ZG = dram("zg_scratch", [1024, S], F32, kind="Internal").ap()
    YC = dram("yc_scratch", [1024, S], F32, kind="Internal").ap()

    dsem = [[sem(f"s_d{i}"), 0] for i in range(24)]
    dcount = [0]
    stores = {}

    def dma(q, out_, in_, w=()):
        d = dsem[dcount[0] % len(dsem)]
        dcount[0] += 1
        before = [(d[0], d[1])] if d[1] else []
        d[1] += 16
        fn = {id(SP): nc.sync.dma_start, id(PO): G.dma_start, id(AC): C.dma_start}[id(q)]
        q.dma(fn, out_, in_, d[0], w=list(w) + before)
        return (d[0], d[1])

    HTh = sbt(ctx, [128, 8, S], F32R)
    HTl = sbt(ctx, [128, 8, S], F32R)
    WR = [sbt(ctx, [128, 2048]) for _ in range(2)]
    WH = [sbt(ctx, [128, 2048], F32R) for _ in range(2)]
    WL = [sbt(ctx, [128, 2048], F32R) for _ in range(2)]
    ident = sbt(ctx, [128, 128])
    Uinc = sbt(ctx, [128, 128])
    Linc = sbt(ctx, [128, 128])
    ones = sbt(ctx, [128, 128])
    nhalf = sbt(ctx, [128, 64])
    PC = sbt(ctx, [128, 4 * 128])
    ss = sbt(ctx, [128, 64])
    st = sbt(ctx, [128, 64])

    PD = Ring([ctx.enter_context(nc.psum_tensor(f"pd{i}", [128, 512], F32)) for i in range(4)])
    PQt = [ctx.enter_context(nc.psum_tensor(f"pq{i}", [128, 1024], F32)) for i in range(2)]
    PB = Ring([PQt[0][:, 0:512], PQt[0][:, 512:1024], PQt[1][:, 0:512], PQt[1][:, 512:1024]])

    NR = 2
    s_wr = [sem(f"s_wr{i}") for i in range(NR)]
    s_wh, s_wl = sem("s_wh"), sem("s_wl")
    units = []
    freed = []

    def load_unit(i):
        def go(wait):
            if i >= len(units):
                return
            if i >= NR:
                wait([(s_wh, i - NR + 1), (s_wl, i - NR + 1)])
            sz, pieces = units[i]
            for k, (o, src) in enumerate(pieces):
                ins = nc.sync.dma_start(o(WR[i % NR]), src)
                ins.then_inc(s_wr[i % NR], 16)
        SP.later(go)

    def need(i):
        return (s_wr[i % NR], sum(16 * len(units[j][1]) for j in range(i % NR, i + 1, NR)))

    def split_unit(i):
        def hi(wait):
            if i < len(units):
                wait([need(i)] + ([freed[i - 2]] if i >= 2 else []))
                n = units[i][0]
                C.activation(WH[i % 2][:, 0:n], WR[i % NR][:, 0:n], ACT.Copy).then_inc(s_wh, 1)

        def lo(wait):
            if i < len(units):
                wait([need(i), (s_wh, i + 1)])
                n = units[i][0]
                V.tensor_tensor(WL[i % 2][:, 0:n], WR[i % NR][:, 0:n],
                                WH[i % 2][:, 0:n].bitcast(F32), SUB).then_inc(s_wl, 1)
        AC.later(hi)
        DV.later(lo)

    class Unit:
        def __init__(self, pieces, k, c):
            i = len(units)
            units.append((k * c, pieces))
            freed.append(None)
            if i == 0:
                for j in range(NR):
                    load_unit(j)
                split_unit(0)
            else:
                load_unit(i + NR - 1)
            split_unit(i + 1)
            self.i = i
            self.h = WH[i % 2][:, 0:k * c].rearrange("p (k c) -> p k c", k=k)
            self.l = WL[i % 2][:, 0:k * c].rearrange("p (k c) -> p k c", k=k)
            self.w = [(s_wh, i + 1), (s_wl, i + 1)]

        def done(self):
            freed[self.i] = PE.now()

    def unit(W, parts, k0=0, k=8):
        c = sum(n for _, n in parts)
        pieces, o = [], 0
        for c0, n in parts:
            src = W[k0 * 128:(k0 + k) * 128, c0:c0 + n].rearrange("(k p) c -> p k c", p=128)

            def dst(t, o=o, n=n):
                return t[:, 0:k * c].rearrange("p (k c) -> p k c", k=k)[:, :, o:o + n]
            pieces.append((dst, src))
            o += n
        return Unit(pieces, k, c)

    def mms(out_, pairs, w, first=True, last=True, inc=True, start=None):
        n = len(pairs)
        tok = None
        for j, (l, r) in enumerate(pairs):
            s_ = (first and j == 0) if start is None else (start and j == 0)
            tok = PE(T.matmul, out_, l, r, start=s_, stop=(last and j == n - 1),
                     skip_group_check=True, w=w if j == 0 else (), inc=(inc and j == n - 1))
        return tok

    def three(lh, ll, rh, rl):
        return [(lh, rh), (lh, rl), (ll, rh)]

    HT = Slot(None)
    HT.r = []

    def fm(u, m0, th, kk=8, w=()):
        b = PD.get()
        sl = slice(th * 512, th * 512 + 512)
        pairs = []
        for k in range(kk):
            pairs += three(u.h[:, k, m0:m0 + 128], u.l[:, k, m0:m0 + 128], HTh[:, k, sl], HTl[:, k, sl])
        t = mms(b.t[:, :], pairs, b.w + u.w + HT.w + list(w))
        return b, t

    def tm(u, c0, n, tts, kk=8):
        b = PD.get()
        t = None
        for j, tt in enumerate(tts):
            sl = slice(tt * 128, tt * 128 + 128)
            pairs = []
            for k in range(kk):
                pairs += three(HTh[:, k, sl], HTl[:, k, sl], u.h[:, k, c0:c0 + n], u.l[:, k, c0:c0 + n])
            t = mms(b.t[:, j * n:(j + 1) * n], pairs, b.w + u.w + HT.w, inc=(j == len(tts) - 1))
        return b, t

    def fence(extra=()):
        w = [q.now() for q in (PE, AC, DV, PO)] + list(extra) + [(d[0], d[1]) for d in dsem if d[1]]
        for q in (PE, AC, DV, PO, SP):
            q.later(lambda wait, w=w: wait(w))

    t = PO(G.memset, ident[:, :], 0.0)
    t = PO(G.affine_select, out=ident[:, :], in_=ident[:, :], compare_op=ALU.not_equal, fill=1.0,
           base=0, pattern=[[-1, 128]], channel_multiplier=1, w=[t])
    t = PO(G.memset, ones[:, :], 1.0)
    PO(G.memset, nhalf[:, :], -0.5)
    PO(G.affine_select, out=Uinc[:, :], in_=ones[:, :], compare_op=ALU.is_ge, fill=0.0,
       base=0, pattern=[[1, 128]], channel_multiplier=-1, w=[t])
    CST = PO(G.affine_select, out=Linc[:, :], in_=ones[:, :], compare_op=ALU.is_ge, fill=0.0,
             base=0, pattern=[[-1, 128]], channel_multiplier=1)

    def rsqrt(dst, src, scale, eps, w):
        n = src.shape[-1]
        t = DV(V.tensor_scalar, dst, src, scale, eps, MUL, ADD, w=w)
        return PO(G.tensor_tensor, dst, dst, nhalf[:, 0:n], ALU.pow, w=[t])

    col = {}

    def columns(c, n0, parts):
        PR = sbt(c, [128, 128])
        z = PO(G.memset, PR[:, :], 0.0)
        r, toks = 0, []
        for name, ap in parts:
            k = ap.shape[0]
            toks.append(dma(SP, PR[r:r + k, :], ap, w=[z]))
            col[name] = n0 + r
            r += k
        assert r <= 128
        b = PB.get()
        t = PE(T.transpose, b.t[:, 0:128], PR[:, :], ident[:, :], w=b.w + toks + [CST])
        t = DV(V.tensor_copy, PC[:, n0:n0 + 128], b.t[:, 0:128], w=[t])
        b.w = [t]
        return t

    def vec(ap):
        return ap.rearrange("(k p) -> k p", p=128)

    def pc(name, i=0):
        c = col[name] + i
        return PC[:, c:c + 1]

    lam = sbt(ctx, [128, 4])
    ph = ExitStack()
    toks = []
    toks.append(columns(ph, 0, [
        ("g_mix", vec(A["norm_mix_g"][0])), ("g_mlp", vec(A["norm_mlp_g"][0])),
        ("ba0", vec(A["b_a_fwd"][0])), ("ba1", vec(A["b_a_bwd"][0])),
        ("gla_g", A["gla_norm_g"][0]), ("sgu_g", A["sgu_norm_g"][0]),
        ("cw2", A["conv_w_2"][0].rearrange("j (k p) -> (j k) p", p=128)),
        ("cb2", vec(A["conv_b_2"][0])), ("ssm_g", vec(A["ssm_norm_g_2"][0])),
        ("subln", A["subln_g_2"])]))
    toks.append(columns(ph, 128, [
        ("cw3a", A["conv_w_3"][0, 0:16, :].rearrange("j (k p) -> (j k) p", p=128))]))
    toks.append(columns(ph, 256, [
        ("cw3b", A["conv_w_3"][0, 16:31, :].rearrange("j (k p) -> (j k) p", p=128))]))
    toks.append(columns(ph, 384, [
        ("g3", vec(A["ln_g_3"][0])), ("cb3", vec(A["conv_b_3"][0])),
        ("cng", vec(A["cnorm_g_3"][0])), ("cnb", vec(A["cnorm_b_3"][0])),
        ("bpw", vec(A["b_pw2_3"][0])), ("lb0", vec(A["lb_logits_3"][0])),
        ("lb1", vec(A["lb_logits_3"][1])), ("ong", vec(A["onorm_g_3"][0])),
        ("peg", vec(A["pe_norm_g_3"][0]))]))
    PCt = toks

    lv = sbt(ph, [128, 5, 64])
    toks = [dma(SP, lv[:, i, :], A[n].partition_broadcast(128).rearrange("p a d -> p (a d)"))
            for i, n in enumerate(("lambda_q1_2", "lambda_k1_2", "lambda_q2_2", "lambda_k2_2"))]
    for i in range(2):
        t = DV(V.tensor_tensor, lv[:, 4, :], lv[:, 2 * i, :], lv[:, 2 * i + 1, :], MUL, w=toks + [DV.now()])
        t = DV(V.tensor_reduce, lam[:, i:i + 1], lv[:, 4, :], AX.X, ADD, w=[t])
    t = AC(C.activation, lam[:, 0:2], lam[:, 0:2], ACT.Exp, w=[t])
    t = DV(V.tensor_tensor, lam[:, 2:3], lam[:, 1:2], lam[:, 0:1], SUB, w=[t])
    t = DV(V.tensor_scalar, lam[:, 3:4], lam[:, 2:3], -(0.8 - 0.6 * math.exp(0.0)), None, ADD, w=[t])
    t = DV(V.tensor_scalar, pc("subln"), pc("subln"), 1.0 - (0.8 - 0.6 * math.exp(0.0)), None, MUL, w=PCt)
    PCt = PCt + [t]
    fence(PCt)
    ph.close()

    def row_bcast(c, ap):
        n = ap.shape[-1]
        r = sbt(c, [128, n])
        return r, dma(SP, r[:, :], ap.partition_broadcast(128))

    def load_X(X, src):
        v = src.rearrange("(t p) d -> p t d", p=128)
        return [dma(SP, X[:, tt, :], v[:, tt, :]) for tt in range(NT)]

    def store_X(X, dst, w):
        v = dst.rearrange("(t p) d -> p t d", p=128)
        return [dma(SP, v[:, tt, :], X[:, tt, :], w=w[tt] if isinstance(w[0], list) else w) for tt in range(NT)]

    def split_HT(k, sl, src, scale, w):
        if scale is None:
            t1 = AC(C.activation, HTh[:, k, sl], src, ACT.Copy, w=w)
            t2 = DV(V.tensor_tensor, HTl[:, k, sl], src, HTh[:, k, sl].bitcast(F32), SUB, w=[t1] + w)
        else:
            t1 = AC(C.activation, HTh[:, k, sl], src, ACT.Copy, scale=scale, w=w)
            t2 = DV(V.scalar_tensor_tensor, HTl[:, k, sl], src, scale, HTh[:, k, sl].bitcast(F32), MUL, SUB,
                    w=[t1] + w)
        return t1, t2

    def rms_rows(X, w, junk):
        for tt in range(NT):
            ww = w[tt] if isinstance(w, dict) else w
            t = AC(C.activation, junk[:, :], X[:, tt, :], ACT.Square, accum_out=ss[:, tt:tt + 1],
                   w=list(ww) + [AC.now()])
        return rsqrt(st[:, 0:8], ss[:, 0:8], 1.0 / 1024, 1e-6, [t])

    def to_HT(c, X, w, rs, gname):
        XN = sbt(c, [128, 4, 1024]) if rs is not None else None
        reads = [PE.now()]
        toks = []
        wr = []
        for th in range(2):
            if rs is not None:
                srcs = []
                for j in range(4):
                    t = DV(V.tensor_scalar, XN[:, j, :], X[:, th * 4 + j, :], st[:, th * 4 + j:th * 4 + j + 1],
                           None, MUL, w=list(w) + [rs] + wr)
                    srcs.append(t)
            for k in range(8):
                b = PD.get()
                for j in range(4):
                    src = XN[:, j, k * 128:(k + 1) * 128] if rs is not None else \
                        X[:, th * 4 + j, k * 128:(k + 1) * 128]
                    t = PE(T.transpose, b.t[:, j * 128:(j + 1) * 128], src, ident[:, :],
                           w=b.w + (srcs if rs is not None else list(w)), inc=(j == 3))
                scale = pc(gname, k) if gname else None
                t1, t2 = split_HT(k, slice(th * 512, th * 512 + 512), b.t[:, :], scale, [t] + reads)
                b.w = [t1, t2]
            wr = [PE.now()]
        HT.w = [t1, t2]

    def rms_heads(O, n, d, sq, w, eps, name_scale=None):
        t = PO(G.tensor_tensor, sq, O, O, MUL, w=w)
        t = DV(V.tensor_reduce, ss[:, 0:n], sq, AX.X, ADD, w=[t])
        t = rsqrt(st[:, 0:n], ss[:, 0:n], 1.0 / d, eps, [t])
        return DV(V.tensor_tensor, O, O, bc(st[:, 0:n].unsqueeze(2), [128, n, d]), MUL, w=[t])

    def out_proj(X, W, kgroups, wX, stage, ytoks):
        for kg in kgroups:
            reads = [PE.now()]
            for k in range(8):
                s = stage.get()
                r = (kg * 8 + k) * 128
                td = dma(SP, s.t[:, :], YM[r:r + 128, :], w=s.w + ytoks)
                t1 = AC(C.activation, HTh[:, k, :], s.t[:, :], ACT.Copy, w=[td] + reads)
                t2 = DV(V.tensor_tensor, HTl[:, k, :], s.t[:, :], HTh[:, k, :].bitcast(F32), SUB, w=[t1, td] + reads)
                s.w = [t1, t2]
            HT.w = [t1, t2]
            for n in range(4):
                u = unit(W, [(n * 256, 256)], k0=kg * 8)
                for t4 in range(4):
                    b, t = tm(u, 0, 256, [2 * t4, 2 * t4 + 1])
                    o = X[:, 2 * t4:2 * t4 + 2, n * 256:(n + 1) * 256]
                    t = DV(V.tensor_tensor, o, b.t[:, :].rearrange("p (a c) -> p a c", a=2), o, ADD, w=[t] + wX)
                    b.w = [t]
                u.done()
        return t

    x_in = A["x"][0]
    ph = ExitStack()
    X = sbt(ph, [128, NT, 1024])
    xt = load_X(X, x_in)
    junk = sbt(ph, [128, 1024])
    rs = rms_rows(X, xt, junk)
    to_HT(ph, X, xt, rs, "g_mix")
    fence()
    ph.close()

    W = A["w_in"][0]
    ph = ExitStack()
    M64 = sbt(ph, [128, S])
    aT = sbt(ph, [32, S])
    wa = [sbt(ph, [32, 256]) for _ in range(2)]
    qT, kT, bb = sbt(ph, [128, S]), sbt(ph, [128, S]), sbt(ph, [128, S])
    DE = sbt(ph, [128, 2, S])
    qin, kin, qx = sbt(ph, [128, S]), sbt(ph, [128, S]), sbt(ph, [128, S])
    vt = sbt(ph, [128, NT, 256])
    kdt = sbt(ph, [128, NT, 128])
    Am = sbt(ph, [128, 2, NT, 128])
    Sg = sbt(ph, [128, 16, 128])
    O = sbt(ph, [128, NT, 2, 128])
    dec = sbt(ph, [128, 16])
    mk = sbt(ph, [128, 2, 64])
    t = PO(G.memset, M64[:, :], 1.0)
    t = PO(G.memset, M64[:, :].rearrange("p (c t) -> p c t", t=64)[:, :, 0:1], 0.0, w=[t])
    PO(G.memset, Am[:, :, :, :], 0.0)
    t = PO(G.memset, mk[:, :, :], 1.0)
    for half in range(2):
        r = slice(64 * half, 64 * half + 64)
        PO(G.affine_select, out=mk[r, 0, :], in_=mk[r, 0, :], compare_op=ALU.is_ge, fill=0.0,
           base=0, pattern=[[1, 64]], channel_multiplier=-1, w=[t])
        PO(G.affine_select, out=mk[r, 1, :], in_=mk[r, 1, :], compare_op=ALU.is_gt, fill=0.0,
           base=0, pattern=[[-1, 64]], channel_multiplier=1, w=[t])
    PO(G.memset, wa[0][:, :], 0.0)
    t = PO(G.memset, wa[1][:, :], 0.0)
    g0 = t
    wat = [dma(SP, wa[0][0:16, :], A["w_a2_fwd"][0], w=[t]), dma(SP, wa[1][16:32, :], A["w_a2_bwd"][0], w=[t])]
    u = unit(W, [(1536, 128)])
    for th in range(2):
        b, t = fm(u, 0, th)
        t = AC(C.copy, aT[:, th * 512:th * 512 + 512], b.t[0:32, :], w=[t])
        b.w = [t]
    u.done()
    at = t
    ysp = []
    prev = []
    for pt in range(2):
        u = unit(W, [(pt * 128, 128), (256 + pt * 128, 128)])
        for th in range(2):
            sl = slice(th * 512, th * 512 + 512)
            b, t = fm(u, 0, th)
            tq = AC(C.mul, qT[:, sl], b.t[:, :], 0.125, w=[t] + prev)
            b.w = [tq]
            b, t = fm(u, 128, th)
            tk = DV(V.tensor_copy, kT[:, sl], b.t[:, :], w=[t] + prev)
            b.w = [tk]
        u.done()
        u = unit(W, [(512 + pt * 256, 256)])
        for t4 in range(4):
            b, t = tm(u, 0, 256, [2 * t4, 2 * t4 + 1])
            tv = AC(C.copy, vt[:, 2 * t4:2 * t4 + 2, :], b.t[:, :].rearrange("p (a c) -> p a c", a=2), w=[t] + prev)
            b.w = [tv]
        u.done()
        for d in range(2):
            D, E = DE[:, 0, :], DE[:, 1, :]
            for th in range(2):
                sl = slice(th * 512, th * 512 + 512)
                b = PB.get()
                t = mms(b.t[:, :], [(wa[d][:, pt * 128:(pt + 1) * 128], aT[:, sl])], b.w + [at] + wat)
                t = AC(C.activation, D[:, sl], b.t[:, :], ACT.Identity, bias=pc(f"ba{d}", pt), w=[t] + prev + [DV.now(), PE.now()])
                b.w = [t]
            t1 = AC(C.activation, E, D, ACT.Abs, w=[t])
            t1 = AC(C.activation, E, E, ACT.Exp, scale=-1.0, w=[t1])
            t1 = AC(C.activation, E, E, ACT.Ln, bias=1.0, w=[t1])
            t = DV(V.tensor_scalar, D, D, 0.0, 1.0 / 16, MIN, MUL, w=[t, t1])
            t = DV(V.scalar_tensor_tensor, D, E, -1.0 / 16, D, MUL, ADD, w=[t])
            if d == 0:
                t = DV(V.tensor_tensor_scan, bb[:, :], M64[:, :], D, 0.0, op0=MUL, op1=ADD, w=[t, g0])
            else:
                t = DV(V.tensor_tensor_scan, bb[:, ::-1], M64[:, :], DE[:, 0, ::-1], 0.0, op0=MUL, op1=ADD, w=[t])
            bv = bb[:, :].rearrange("p (c t) -> p c t", t=64)
            Dv = D.rearrange("p (c t) -> p c t", t=64)
            mid, end = (32, 63) if d == 0 else (31, 0)
            t = DV(V.tensor_tensor, Dv, bv, bc(bv[:, :, mid:mid + 1], [128, 16, 64]), SUB, w=[t])
            t1 = AC(C.activation, E, D, ACT.Exp, w=[t])
            t = DV(V.tensor_tensor, qin[:, :], qT[:, :], E, MUL, w=[t1, tq])
            t2 = AC(C.activation, E, D, ACT.Exp, scale=-1.0, w=[t])
            ti = DV(V.tensor_tensor, kin[:, :], kT[:, :], E, MUL, w=[t2, tk])
            t3 = DV(V.tensor_tensor, Dv, bc(bv[:, :, end:end + 1], [128, 16, 64]), bv, SUB, w=[t2])
            t3 = AC(C.activation, D, D, ACT.Exp, w=[t3])
            tkd = DV(V.tensor_tensor, D, kT[:, :], D, MUL, w=[t3])
            t4_ = AC(C.activation, E, bb[:, :], ACT.Exp, w=[ti])
            tdec = AC(C.activation, dec[:, :], bv[:, :, end], ACT.Exp, w=[DV.now()])
            tqx = DV(V.tensor_tensor, qx[:, :], qT[:, :], E, MUL, w=[t4_])
            for th in range(2):
                b = PB.get()
                for j in range(4):
                    tt = th * 4 + j
                    t = PE(T.transpose, b.t[:, j * 128:(j + 1) * 128], D[:, tt * 128:(tt + 1) * 128], ident[:, :],
                           w=b.w + [tkd], inc=(j == 3))
                tkt = AC(C.copy, kdt[:, th * 4:th * 4 + 4, :], b.t[:, :].rearrange("p (a c) -> p a c", a=4), w=[t])
                b.w = [tkt]
            banks = [PB.get(), PB.get()]
            for hh in range(2):
                r = slice(64 * hh, 64 * hh + 64)
                b = banks[hh]
                for c in range(16):
                    half, cs = c % 2, slice(64 * c, 64 * c + 64)
                    t = mms(b.t[64 * half:64 * half + 64, 64 * (c // 2):64 * (c // 2) + 64],
                            [(kin[r, cs], qin[r, cs])], b.w + [ti], inc=(c == 15))
                for half in range(2):
                    p = slice(64 * half, 64 * half + 64)
                    ta = DV(V.tensor_tensor, Am[p, hh, :, 64 * half:64 * half + 64],
                            b.t[p, :].rearrange("p (a c) -> p a c", a=8),
                            bc(mk[p, d:d + 1, :], [64, 8, 64]), MUL, w=[t, g0])
                b.w = [ta]
            order = list(range(16)) if d == 0 else list(range(15, -1, -1))
            t = DV(V.memset, Sg[:, order[0], :], 0.0, w=[PE.now()])
            ts = t
            for q4 in range(4):
                cs = order[q4 * 4:q4 * 4 + 4]
                banks = [PB.get(), PB.get()]
                for j, c in enumerate(cs):
                    half, tt = c % 2, c // 2
                    r = slice(64 * half, 64 * half + 64)
                    for hh in range(2):
                        t = mms(banks[half].t[64 * hh:64 * hh + 64, (j // 2) * 128:(j // 2) * 128 + 128],
                                [(kdt[r, tt, 64 * hh:64 * hh + 64], vt[r, tt, hh * 128:hh * 128 + 128])],
                                banks[half].w + [tkt, tv], inc=(j == 3 and hh == 1))
                for j, c in enumerate(cs):
                    i = q4 * 4 + j
                    if i < 15:
                        ts = DV(V.scalar_tensor_tensor, Sg[:, order[i + 1], :], Sg[:, c, :], dec[:, c:c + 1],
                                banks[c % 2].t[:, (j // 2) * 128:(j // 2) * 128 + 128], MUL, ADD, w=[t, ts, tdec])
                for b in banks:
                    b.w = [ts]
            for hh in range(2):
                r = slice(64 * hh, 64 * hh + 64)
                for th in range(2):
                    b = PB.get()
                    for j in range(4):
                        tt = th * 4 + j
                        o = b.t[:, j * 128:(j + 1) * 128]
                        mms(o, [(Am[:, hh, tt, :], vt[:, tt, hh * 128:(hh + 1) * 128])], b.w + [ta, tv, ts, tqx],
                            last=False, inc=False)
                        for half in range(2):
                            c = 2 * tt + half
                            t = mms(b.t[64 * half:64 * half + 64, j * 128:(j + 1) * 128],
                                    [(qx[r, 64 * c:64 * c + 64], Sg[r, c, :])], (), first=False,
                                    inc=(half == 1))
                    ov = O[:, th * 4:th * 4 + 4, hh, :]
                    bvw = b.t[:, :].rearrange("p (a c) -> p a c", a=4)
                    if d == 0:
                        to = DV(V.tensor_copy, ov, bvw, w=[t] + prev)
                    else:
                        to = DV(V.tensor_tensor, ov, bvw, ov, ADD, w=[t, DV.now()])
                    b.w = [to]
        u = unit(W, [(1024 + pt * 256, 256)])
        gw = [PE.now(), AC.now(), DV.now()]
        for hh in range(2):
            for th in range(2):
                b, t = fm(u, hh * 128, th)
                tg = AC(C.activation, DE[:, hh, th * 512:th * 512 + 512], b.t[:, :], ACT.Silu, w=[t] + gw)
                b.w = [tg]
        u.done()
        Of = O[:, :, :, :].rearrange("p a b c -> p (a b) c")
        t = rms_heads(Of, 16, 128, Sg[:, :, :], [to, PE.now()], 1e-6)
        for hh in range(2):
            for th in range(2):
                b = PB.get()
                for j in range(4):
                    tt_ = PE(T.transpose, b.t[:, j * 128:(j + 1) * 128], O[:, th * 4 + j, hh, :], ident[:, :],
                             w=b.w + [t], inc=(j == 3))
                gs = DE[:, hh, th * 512:th * 512 + 512]
                ty = DV(V.scalar_tensor_tensor, gs, b.t[:, :], pc("gla_g", pt * 2 + hh), gs, MUL, MUL, w=[tt_, tg])
                b.w = [ty]
            r = (pt * 2 + hh) * 128
            ysp.append(dma(SP, YM[r:r + 128, :], DE[:, hh, :], w=[ty]))
        prev = [PE.now(), AC.now(), DV.now()] + ysp[-2:]
    fence()
    ph.close()

    ph = ExitStack()
    wsr = sbt(ph, [128, 4, 128])
    wsT = sbt(ph, [128, 4, 128])
    bsr, bst = row_bcast(ph, A["b_s"][0].rearrange("g p -> (g p)"))
    wst = dma(SP, wsr[:, :, :], A["w_s"][0].rearrange("g p q -> p g q"))
    b = PB.get()
    for g in range(4):
        t = PE(T.transpose, b.t[:, g * 128:(g + 1) * 128], wsr[:, g, :], ident[:, :], w=b.w + [wst], inc=(g == 3))
    twT = AC(C.copy, wsT[:, :, :], b.t[:, :].rearrange("p (a c) -> p a c", a=4), w=[t])
    b.w = [twT]
    VS = Ring([sbt(ph, [128, NT, 2, 128]) for _ in range(2)])
    UT = Ring([sbt(ph, [128, 2, S]) for _ in range(2)])
    sq = sbt(ph, [128, 16, 128])
    for gp in range(2):
        vs, ut = VS.get(), UT.get()
        u = unit(W, [(2080 + gp * 256, 256)])
        for t4 in range(4):
            b, t = tm(u, 0, 256, [2 * t4, 2 * t4 + 1])
            tv = AC(C.activation, vs.t[:, 2 * t4:2 * t4 + 2, :, :].rearrange("p a g c -> p (a g c)"), b.t[:, :],
                    ACT.Gelu, w=[t])
            b.w = [tv]
        u.done()
        tv = rms_heads(vs.t[:, :, :, :].rearrange("p a g c -> p (a g) c"), 16, 128, sq[:, :, :],
                       [tv, DV.now()], 1e-6)
        u = unit(W, [(1568 + gp * 256, 256)])
        for g in range(2):
            for th in range(2):
                b, t = fm(u, g * 128, th)
                tu = AC(C.activation, ut.t[:, g, th * 512:th * 512 + 512], b.t[:, :], ACT.Gelu, w=[t])
                b.w = [tu]
        u.done()
        for g in range(2):
            gg = gp * 2 + g
            for th in range(2):
                b = PB.get()
                for j in range(4):
                    t = mms(b.t[:, j * 128:(j + 1) * 128], [(vs.t[:, th * 4 + j, g, :], wsT[:, gg, :])],
                            b.w + [tv, twT], inc=(j == 3))
                mixed = sq[:, 0:4, :]
                t = DV(V.scalar_tensor_tensor, mixed, b.t[:, :].rearrange("p (a c) -> p a c", a=4),
                       pc("sgu_g", gg),
                       bc(bsr[:, gg * 128:(gg + 1) * 128].unsqueeze(1), [128, 4, 128]), MUL, ADD,
                       w=[t, bst, DV.now()])
                b.w = [t]
                o = ut.t[:, g, th * 512:th * 512 + 512]
                t = DV(V.tensor_tensor, o, o, mixed.rearrange("p a c -> p (a c)"), MUL, w=[t, tu])
            r = (4 + gg) * 128
            ysp.append(dma(SP, YM[r:r + 128, :], ut.t[:, g, :], w=[t]))
    fence()
    ph.close()

    ph = ExitStack()
    X = sbt(ph, [128, NT, 1024])
    ph2 = ExitStack()
    stage = Ring([sbt(ph2, [128, S]) for _ in range(3)])
    xt = load_X(X, x_in)
    t = out_proj(X, A["w_out"][0], [0], xt, stage, ysp)
    fence()
    ph2.close()
    ph2 = ExitStack()
    junk = sbt(ph2, [128, 1024])
    rs = rms_rows(X, [t], junk)
    to_HT(ph2, X, [], rs, "g_mlp")
    fence()
    ph2.close()
    ph2 = ExitStack()
    Uh = [sbt(ph2, [128, 2, S], F32R) for _ in range(2)]
    Ul = [sbt(ph2, [128, 2, S], F32R) for _ in range(2)]
    rr = Ring([sbt(ph2, [128, 512]) for _ in range(3)])
    qq = Ring([sbt(ph2, [128, 512]) for _ in range(3)])
    W1, W2 = A["w_mlp1"][0], A["w_mlp2"][0]
    utok, uread = {}, {}

    def up(j):
        u = unit(W1, [(j * 256, 256)])
        toks = []
        for m in range(2):
            for th in range(2):
                sl = slice(th * 512, th * 512 + 512)
                b, t = fm(u, m * 128, th)
                r, q = rr.get(), qq.get()
                t = AC(C.activation, r.t[:, :], b.t[:, :], ACT.Relu, w=[t] + r.w)
                b.w = [t]
                tq = PO(G.tensor_tensor, q.t[:, :], r.t[:, :], r.t[:, :], MUL, w=[t] + q.w)
                th_ = AC(C.activation, Uh[j % 2][:, m, sl], r.t[:, :], ACT.Square, w=[t] + uread.get(j - 2, []))
                tl = DV(V.tensor_tensor, Ul[j % 2][:, m, sl], q.t[:, :], Uh[j % 2][:, m, sl].bitcast(F32), SUB,
                        w=[tq, th_])
                r.w, q.w = [tq, th_], [tl]
                toks += [th_, tl]
        u.done()
        utok[j] = toks

    def down(j):
        u = unit(W2, [(0, 1024)], k0=2 * j, k=2)
        for tt in range(NT):
            sl = slice(tt * 128, tt * 128 + 128)
            for nh in range(2):
                cs = slice(nh * 512, nh * 512 + 512)
                b = PD.get()
                pairs = []
                for k in range(2):
                    pairs += three(Uh[j % 2][:, k, sl], Ul[j % 2][:, k, sl], u.h[:, k, cs], u.l[:, k, cs])
                t = mms(b.t[:, :], pairs, b.w + u.w + utok[j])
                t = DV(V.tensor_tensor, X[:, tt, cs], b.t[:, :], X[:, tt, cs], ADD, w=[t])
                b.w = [t]
        u.done()
        uread[j] = [PE.now()]
        return t

    up(0)
    for j in range(16):
        if j < 15:
            up(j + 1)
        t = down(j)
    fence()
    ph2.close()

    def layernorm(X, gr, br, w):
        toks = []
        mv = st[:, 32:48]
        for tt in range(NT):
            t1 = DV(V.bn_stats, ss[:, 0:6], X[:, tt, 0:512], w=w + [DV.now()])
            t2 = DV(V.bn_stats, ss[:, 6:12], X[:, tt, 512:1024])
            t3 = DV(V.bn_aggr, mv[:, 2 * tt:2 * tt + 2], ss[:, 0:12], w=[t2])
        var = mv.rearrange("p (t c) -> p t c", c=2)
        t = DV(V.tensor_scalar, st[:, 0:8], var[:, :, 1], 1.0, 1e-5, MUL, ADD, w=[t3])
        t = PO(G.tensor_tensor, st[:, 0:8], st[:, 0:8], nhalf[:, 0:8], ALU.pow, w=[t])
        for tt in range(NT):
            t1 = DV(V.tensor_scalar, X[:, tt, :], X[:, tt, :], mv[:, 2 * tt:2 * tt + 1], st[:, tt:tt + 1],
                    SUB, MUL, w=[t])
            t2 = DV(V.tensor_tensor, X[:, tt, :], X[:, tt, :], gr[:, :], MUL, w=[t1])
            toks.append(PO(G.tensor_tensor, X[:, tt, :], X[:, tt, :], br[:, :], ADD, w=[t2]))
        return toks

    ph2 = ExitStack()
    junk = sbt(ph2, [128, 1024])
    fg, t1 = row_bcast(ph2, A["final_norm_g"])
    eg, t2 = row_bcast(ph2, A["ln_emb_g_2"])
    eb, t3 = row_bcast(ph2, A["ln_emb_b_2"])
    rs = rms_rows(X, [t], junk)
    for tt in range(NT):
        t = DV(V.scalar_tensor_tensor, X[:, tt, :], X[:, tt, :], st[:, tt:tt + 1], fg[:, :], MUL, MUL, w=[rs, t1])
    if upto == 1:
        stx = store_X(X, out[0], [t])
        ph2.close()
        ph.close()
        finish(nc, ctx, PE, AC, DV, PO, SP, stx)
        return
    toks = layernorm(X, eg, eb, [t, t2, t3])
    stx = store_X(X, XD, [[x] for x in toks])
    to_HT(ph2, X, [toks[-1]], None, None)
    fence()
    ph2.close()
    ph.close()
    W = A["w_in_2"][0]
    ph = ExitStack()
    dt_, dA, acs, wd, ea, dcy = (sbt(ph, [128, NT, 32]) for _ in range(6))
    dbr = sbt(ph, [128, 32])
    Ar = sbt(ph, [128, 32])
    Dr = sbt(ph, [128, 16])
    ct = [dma(SP, dbr[:, 0:16], A["dt_bias_fwd_2"][0].partition_broadcast(128)),
          dma(SP, dbr[:, 16:32], A["dt_bias_bwd_2"][0].partition_broadcast(128)),
          dma(SP, Ar[:, 0:16], A["A_log_fwd_2"][0].partition_broadcast(128)),
          dma(SP, Ar[:, 16:32], A["A_log_bwd_2"][0].partition_broadcast(128)),
          dma(SP, Dr[:, :], A["D_skip_2"][0].partition_broadcast(128))]
    u = unit(W, [(2560, 32)])
    b, t = tm(u, 0, 32, list(range(8)))
    u.done()
    flat = (lambda x: x[:, :, :].rearrange("p a b -> p (a b)"))
    t = DV(V.tensor_tensor, dt_[:, :, :], b.t[:, 0:256].rearrange("p (a b) -> p a b", a=8),
           bc(dbr[:, :].unsqueeze(1), [128, 8, 32]), ADD, w=[t] + ct)
    b.w = [t]
    t1 = AC(C.activation, flat(wd), flat(dt_), ACT.Abs, w=[t])
    t1 = AC(C.activation, flat(wd), flat(wd), ACT.Exp, scale=-1.0, w=[t1])
    t1 = AC(C.activation, flat(wd), flat(wd), ACT.Ln, bias=1.0, w=[t1])
    tA = AC(C.activation, Ar[:, :], Ar[:, :], ACT.Exp, w=ct)
    t = DV(V.scalar_tensor_tensor, dt_[:, :, :], dt_[:, :, :], 0.0, wd[:, :, :], MAX, ADD, w=[t1])
    t = DV(V.scalar_tensor_tensor, dA[:, :, :], dt_[:, :, :], -1.0, bc(Ar[:, :].unsqueeze(1), [128, 8, 32]),
           MUL, MUL, w=[t, tA])
    b = PB.get()
    bvv = b.t[:, 0:256].rearrange("p (a b) -> p a b", a=8)
    mms(bvv[:, :, 0:16], [(Uinc[:, :], dA[:, :, 0:16])], b.w + [t], inc=False)
    mms(bvv[:, :, 16:32], [(Linc[:, :], dA[:, :, 16:32])], (), inc=False)
    t = mms(b.t[:, 256:512], [(ones[:, :], flat(dA))], ())
    t1 = DV(V.tensor_copy, acs[:, :, :], bvv, w=[t])
    t1 = DV(V.tensor_tensor, flat(wd), b.t[:, 256:512], flat(acs), SUB, w=[t1])
    t2 = AC(C.activation, flat(dcy), b.t[:, 256:512], ACT.Exp, w=[t1])
    b.w = [t2, t1]
    t3 = AC(C.activation, flat(wd), flat(wd), ACT.Exp, w=[t1])
    t4_ = AC(C.activation, flat(ea), flat(acs), ACT.Exp, w=[t1])
    tw = DV(V.tensor_tensor, flat(wd), flat(wd), flat(dt_), MUL, w=[t3])
    small = [tw, t4_, t2, t1]
    xs = sbt(ph, [128, NT, 512])
    y = sbt(ph, [128, NT, 512])
    BT, CT, Bt = sbt(ph, [128, S]), sbt(ph, [128, S]), sbt(ph, [128, NT, 128])
    PR = [sbt(ph, [128, S + 4]) for _ in range(2)]
    for p in PR:
        PO(G.memset, p[:, 0:2], 0.0)
        t = PO(G.memset, p[:, S + 2:S + 4], 0.0)
    pz = t
    Pad = Ring(PR)
    Acc = Ring([sbt(ph, [128, S]) for _ in range(2)])
    Er = Ring([sbt(ph, [128, 4, 128]) for _ in range(2)])
    Gr = Ring([sbt(ph, [128, 4, 128]) for _ in range(2)])
    Tr = Ring([sbt(ph, [128, 512]) for _ in range(2)])
    Xw = Ring([sbt(ph, [128, 512]) for _ in range(2)])
    Cb = Ring([sbt(ph, [128, 128]) for _ in range(2)])
    St = sbt(ph, [128, 512])
    ysp = []
    prev = []
    for g in range(2):
        tiles = []
        for n in range(3):
            if n < 2:
                u = unit(W, [(1024 + g * 512 + n * 256, 256)])
                ms = [4 * g + 2 * n, 4 * g + 2 * n + 1]
            else:
                u = unit(W, [(2048 + g * 128, 128), (2304 + g * 128, 128)])
                ms = [8 + g, 10 + g]
            for mi, m in enumerate(ms):
                p = Pad.get()
                for th in range(2):
                    b, t = fm(u, mi * 128, th)
                    tp = AC(C.copy, p.t[:, 2 + th * 512:2 + th * 512 + 512], b.t[:, :], w=[t, pz] + p.w)
                    b.w = [tp]
                a = Acc.get()
                t = AC(C.activation, a.t[:, :], p.t[:, 0:S], ACT.Identity, scale=pc("cw2", m), bias=pc("cb2", m),
                       w=[tp] + a.w)
                for j in range(1, 5):
                    t = DV(V.scalar_tensor_tensor, a.t[:, :], p.t[:, j:j + S], pc("cw2", 12 * j + m), a.t[:, :],
                           MUL, ADD, w=[t])
                p.w = [t]
                dst = {8 + g: BT, 10 + g: CT}.get(m)
                if dst is None:
                    t = AC(C.activation, a.t[:, :], a.t[:, :], ACT.Silu, w=[t])
                    src = a.t
                else:
                    t = AC(C.activation, dst[:, :], a.t[:, :], ACT.Silu, w=[t] + prev)
                    a.w = [t]
                    src = dst
                    tBC = t
                if m < 8 or m == 8 + g:
                    for th in range(2):
                        b = PB.get()
                        for j in range(4):
                            tt = th * 4 + j
                            t_ = PE(T.transpose, b.t[:, j * 128:(j + 1) * 128], src[:, tt * 128:(tt + 1) * 128],
                                    ident[:, :], w=b.w + [t], inc=(j == 3))
                        o = xs[:, th * 4:th * 4 + 4, (m % 4) * 128:(m % 4) * 128 + 128] if m < 8 else \
                            Bt[:, th * 4:th * 4 + 4, :]
                        t2 = DV(V.tensor_copy, o, b.t[:, :].rearrange("p (a c) -> p a c", a=4), w=[t_] + prev)
                        b.w = [t2]
                    if m < 8:
                        a.w = [t_]
                    txs = t2
            u.done()
        h8 = [128, 8, 64]

        def hv(x):
            return x.rearrange("p (h d) -> p h d", h=8)
        ty = None
        for tt in range(NT):
            ty = PO(G.tensor_tensor, hv(y[:, tt, :]), hv(xs[:, tt, :]),
                    bc(Dr[:, g * 8:g * 8 + 8].unsqueeze(2), h8), MUL, w=[txs, ct[4]] + prev)
        for d in range(2):
            order = list(range(8)) if d == 0 else list(range(7, -1, -1))
            ts = None
            for i, tt in enumerate(order):
                sl = slice(tt * 128, tt * 128 + 128)
                b = PB.get()
                t = mms(b.t[:, 0:128], [(BT[:, sl], CT[:, sl])], b.w + [tBC, txs])
                cb = Cb.get()
                tcb = DV(V.tensor_tensor, cb.t[:, :], b.t[:, 0:128], (Uinc if d == 0 else Linc)[:, :], MUL,
                         w=[t] + cb.w)
                b.w = [tcb]
                Y = PD.get()
                for q4 in range(2):
                    b = PB.get()
                    h0 = d * 16 + g * 8 + q4 * 4
                    for j in range(4):
                        t = mms(b.t[:, j * 128:(j + 1) * 128],
                                [(bc(dA[:, tt, h0 + j:h0 + j + 1], [128, 128]), (Uinc if d == 0 else Linc)[:, :])],
                                b.w + small, inc=(j == 3))
                    e, gr = Er.get(), Gr.get()
                    for j in range(4):
                        te = DV(V.tensor_scalar, e.t[:, j, :], b.t[:, j * 128:(j + 1) * 128],
                                acs[:, tt, h0 + j:h0 + j + 1], 0.0, SUB, MIN, w=[t] + e.w)
                    b.w = [te]
                    te = AC(C.activation, e.t[:, :, :], e.t[:, :, :], ACT.Exp, w=[te])
                    for j in range(4):
                        tg = DV(V.scalar_tensor_tensor, gr.t[:, j, :], e.t[:, j, :], dt_[:, tt, h0 + j:h0 + j + 1],
                                cb.t[:, :], MUL, MUL, w=[te, tcb] + gr.w)
                    e.w = [tg]
                    for j in range(4):
                        hh = q4 * 4 + j
                        t = mms(Y.t[:, hh * 64:hh * 64 + 64], [(gr.t[:, j, :], xs[:, tt, hh * 64:hh * 64 + 64])],
                                Y.w + [tg], inc=(j == 3))
                    gr.w = [t]
                cb.w = [tg]
                ty = DV(V.tensor_tensor, y[:, tt, :], Y.t[:, :], y[:, tt, :], ADD, w=[t, ty, DV.now()])
                Y.w = [ty]
                hs = slice(d * 16 + g * 8, d * 16 + g * 8 + 8)
                if i > 0:
                    Z = PD.get()
                    t = mms(Z.t[:, :], [(CT[:, sl], St[:, :])], Z.w + [ts, tBC])
                    tz = t
                    tr = Tr.get()
                    t = DV(V.tensor_tensor, hv(tr.t[:, :]), hv(Z.t[:, :]), bc(ea[:, tt, hs].unsqueeze(2), h8), MUL,
                           w=[t] + small + tr.w)
                    Z.w = [t]
                    ty = DV(V.tensor_tensor, y[:, tt, :], y[:, tt, :], tr.t[:, :], ADD, w=[t])
                    tr.w = [ty]
                if i < 7:
                    xw = Xw.get()
                    t = PO(G.tensor_tensor, hv(xw.t[:, :]), hv(xs[:, tt, :]), bc(wd[:, tt, hs].unsqueeze(2), h8), MUL,
                           w=[txs] + small + xw.w)
                    b = PD.get()
                    t = mms(b.t[:, :], [(Bt[:, tt, :], xw.t[:, :])], b.w + [t, txs])
                    xw.w = [t]
                    if i == 0:
                        ts = DV(V.tensor_copy, St[:, :], b.t[:, :], w=[t, PE.now()])
                    else:
                        t1 = DV(V.tensor_tensor, hv(St[:, :]), hv(St[:, :]), bc(dcy[:, tt, hs].unsqueeze(2), h8),
                                MUL, w=[tz, ts])
                        ts = DV(V.tensor_tensor, St[:, :], b.t[:, :], St[:, :], ADD, w=[t, t1])
                    b.w = [ts]
        for n in range(2):
            u = unit(W, [(g * 512 + n * 256, 256)])
            for t4 in range(4):
                b, t = tm(u, 0, 256, [2 * t4, 2 * t4 + 1])
                tr = Tr.get()
                t = AC(C.activation, tr.t[:, :], b.t[:, :], ACT.Silu, w=[t] + tr.w)
                b.w = [t]
                o = y[:, 2 * t4:2 * t4 + 2, n * 256:(n + 1) * 256]
                ty = DV(V.tensor_tensor, o, o, tr.t[:, :].rearrange("p (a c) -> p a c", a=2), MUL, w=[t, ty])
                tr.w = [ty]
            u.done()
        t = rms_heads(y[:, :, :], 8, 512, xs[:, :, :], [ty, PE.now()], 1e-5)
        for m in range(4):
            a = Acc.get()
            for th in range(2):
                b = PB.get()
                for j in range(4):
                    t_ = PE(T.transpose, b.t[:, j * 128:(j + 1) * 128], y[:, th * 4 + j, m * 128:(m + 1) * 128],
                            ident[:, :], w=b.w + [t], inc=(j == 3))
                ty = AC(C.mul, a.t[:, th * 512:th * 512 + 512], b.t[:, :], pc("ssm_g", g * 4 + m), w=[t_] + a.w)
                b.w = [ty]
            r = (g * 4 + m) * 128
            ysp.append(dma(SP, YM[r:r + 128, :], a.t[:, :], w=[ty]))
            a.w = [ysp[-1]]
        prev = [PE.now(), AC.now(), DV.now(), PO.now()]
    fence()
    ph.close()

    ph = ExitStack()
    WD = 1920
    dist = sbt(ph, [128, WD])
    bias = sbt(ph, [128, WD])
    qT, kT, gT = (sbt(ph, [128, 2, S]) for _ in range(3))
    vt = sbt(ph, [128, NT, 256])
    SR = Ring([sbt(ph, [128, 2, S]) for _ in range(2)])
    WT = Ring([sbt(ph, [128, 8, 128]) for _ in range(2)])
    O = sbt(ph, [128, NT, 128])
    sm = Ring([sbt(ph, [128, 8]) for _ in range(4)])
    PQ = [Slot(PQt[0]), Slot(PQt[1])]
    t = PO(G.iota, dist[:, :], pattern=[[-1, WD]], base=896, channel_multiplier=1,
           allow_small_or_imprecise_dtypes=True)
    tdist = AC(C.activation, dist[:, :], dist[:, :], ACT.Abs, w=[t])
    prev = []
    for b in PB.s:
        PQ[0].w = PQ[0].w + b.w
        PQ[1].w = PQ[1].w + b.w
    for hp in range(4):
        for dst, c0 in ((qT, 2592), (kT, 3616)):
            u = unit(W, [(c0 + hp * 256, 256)])
            for m in range(2):
                for th in range(2):
                    b, t = fm(u, m * 128, th)
                    t = AC(C.copy, dst[:, m, th * 512:th * 512 + 512], b.t[:, :], w=[t] + prev)
                    b.w = [t]
            u.done()
        tqk = t
        u = unit(W, [(4640 + hp * 256, 256)])
        for t4 in range(4):
            b, t = tm(u, 0, 256, [2 * t4, 2 * t4 + 1])
            tv = AC(C.copy, vt[:, 2 * t4:2 * t4 + 2, :], b.t[:, :].rearrange("p (a c) -> p a c", a=2), w=[t] + prev)
            b.w = [tv]
        u.done()
        u = unit(W, [(5664 + hp * 256, 256)])
        for m in range(2):
            for th in range(2):
                b, t = fm(u, m * 128, th)
                tg = AC(C.activation, gT[:, m, th * 512:th * 512 + 512], b.t[:, :], ACT.Silu, w=[t] + prev)
                b.w = [tg]
        u.done()
        for m in range(2):
            h = hp * 2 + m
            tb = AC(C.mul, bias[:, :], dist[:, :], -8.0 * 2.0 ** (-(h + 1.0)), w=[tdist, DV.now()])

            def scores(tt):
                s, x = SR.get(), sm.get()
                toks = []
                for r in range(2):
                    p = PQ[r]
                    rows = slice(64 * r, 64 * r + 64)
                    for sh in range(2):
                        t = mms(p.t[:, sh * 512:sh * 512 + 512],
                                [(qT[rows, m, tt * 128:tt * 128 + 128], kT[rows, m, sh * 512:sh * 512 + 512])],
                                p.w + [tqk], inc=(sh == 1))
                    t = DV(V.tensor_tensor_reduce, out=s.t[:, r, :], in0=p.t[:, :],
                           in1=bias[:, 896 - 128 * tt:896 - 128 * tt + 1024], scale=0.125, scalar=-3.0e38,
                           op0=ADD, op1=MAX, accum_out=x.t[:, r:r + 1], w=[t, tb] + s.w + x.w)
                    p.w = [t]
                t = DV(V.tensor_scalar, x.t[:, 2:4], x.t[:, 0:2], -1.0, None, MUL, w=[t])
                for r in range(2):
                    t2 = AC(C.activation, s.t[:, r, :], s.t[:, r, :], ACT.Exp, bias=x.t[:, 2 + r:3 + r],
                            accum_out=x.t[:, 4 + r:5 + r], w=[t])
                t = DV(V.reciprocal, x.t[:, 6:8], x.t[:, 4:6], w=[t2])
                t = DV(V.scalar_tensor_tensor, x.t[:, 5:6], x.t[:, 4:5], lam[:, 3:4], x.t[:, 7:8], MUL, MUL, w=[t])
                t = DV(V.scalar_tensor_tensor, s.t[:, 0, :], s.t[:, 1, :], x.t[:, 5:6], s.t[:, 0, :], MUL, ADD,
                       w=[t])
                return tt, s, x, t

            def values(tt, s, x, t):
                wt = WT.get()
                toks = []
                for th in range(2):
                    b = PD.get()
                    for j in range(4):
                        t_ = PE(T.transpose, b.t[:, j * 128:(j + 1) * 128],
                                s.t[:, 0, (th * 4 + j) * 128:(th * 4 + j + 1) * 128], ident[:, :], w=b.w + [t],
                                inc=(j == 3))
                    if th == 0:
                        t2 = AC(C.copy, wt.t[:, 0:4, :], b.t[:, :].rearrange("p (a c) -> p a c", a=4),
                                w=[t_] + wt.w)
                    else:
                        t2 = DV(V.tensor_copy, wt.t[:, 4:8, :], b.t[:, :].rearrange("p (a c) -> p a c", a=4),
                                w=[t_] + wt.w)
                    b.w = [t2]
                    toks.append(t2)
                s.w = [t_]
                b = PD.get()
                t_ = mms(b.t[:, 0:128], [(wt.t[:, j, :], vt[:, j, m * 128:(m + 1) * 128]) for j in range(8)],
                         b.w + toks + [tv])
                wt.w = [t_]
                t2 = AC(C.mul, O[:, tt, :], b.t[:, 0:128], x.t[:, 6:7], w=[t_] + ow)
                b.w = [t2]
                x.w = [t2]
                return t2

            ow = [PE.now()]
            pend = scores(0)
            for tt in range(NT):
                nxt = scores(tt + 1) if tt < 7 else None
                to = values(*pend)
                pend = nxt
            s = SR.get()
            t = rms_heads(O[:, :, :], 8, 128, s.t[:, 0, :].rearrange("p (a c) -> p a c", a=8), [to] + s.w, 1e-5)
            s.w = [t]
            for th in range(2):
                b = PD.get()
                for j in range(4):
                    t_ = PE(T.transpose, b.t[:, j * 128:(j + 1) * 128], O[:, th * 4 + j, :], ident[:, :],
                            w=b.w + [t], inc=(j == 3))
                gs = gT[:, m, th * 512:th * 512 + 512]
                ty = DV(V.scalar_tensor_tensor, gs, b.t[:, :], pc("subln"), gs, MUL, MUL, w=[t_, tg])
                b.w = [ty]
            r = (8 + h) * 128
            ysp.append(dma(SP, YM[r:r + 128, :], gT[:, m, :], w=[ty]))
        prev = [PE.now(), AC.now(), DV.now()] + ysp[-2:]
    fence()
    ph.close()

    ph = ExitStack()
    X = sbt(ph, [128, NT, 1024])
    stage = Ring([sbt(ph, [128, S]) for _ in range(3)])
    xt = load_X(X, XD)
    wX = []
    for tt in range(NT):
        wX.append(AC(C.mul, X[:, tt, :], X[:, tt, :], ALPHA, w=[xt[tt]] + stx))
    t = out_proj(X, A["w_out_2"][0], [0, 1], wX[-1:], stage, ysp)
    gr, t1 = row_bcast(ph, A["ln_g_2"][0])
    br, t2 = row_bcast(ph, A["ln_b_2"][0])
    toks = layernorm(X, gr, br, [t, t1, t2])
    if upto == 2:
        stx = store_X(X, out[0], [[x] for x in toks])
        ph.close()
        finish(nc, ctx, PE, AC, DV, PO, SP, stx)
        return
    stx = store_X(X, XD, [[x] for x in toks])
    fence()
    ph2 = ExitStack()
    junk = sbt(ph2, [128, 1024])
    rs = rms_rows(X, [toks[-1]], junk)
    to_HT(ph2, X, [], rs, "g3")
    fence()
    ph2.close()
    ph.close()
    W = A["w_in_3"][0]
    ph = ExitStack()
    PR = [sbt(ph, [128, S + 30]) for _ in range(2)]
    for p in PR:
        pz = PO(G.memset, p[:, 0:30], 0.0)
    Pad = Ring(PR)
    Acc = Ring([sbt(ph, [128, S]) for _ in range(2)])
    Sg_ = Ring([sbt(ph, [128, S]) for _ in range(3)])
    o128 = sbt(ph, [128, 128])
    to128 = DV(V.memset, o128[:, :], 1.0 / 128)
    eps = sbt(ph, [128, 1])
    teps = DV(V.memset, eps[:, :], 1e-6)
    ycs = []

    def taps(k, g):
        return pc("cw3a", 8 * k + g) if k < 16 else pc("cw3b", 8 * (k - 16) + g)

    for g in range(8):
        u = unit(W, [(g * 128, 128), (1024 + g * 128, 128)])
        p, sg, a = Pad.get(), Sg_.get(), Acc.get()
        for th in range(2):
            sl = slice(th * 512, th * 512 + 512)
            b1, t1 = fm(u, 128, th)
            t1 = AC(C.activation, sg.t[:, sl], b1.t[:, :], ACT.Sigmoid, w=[t1] + sg.w)
            b1.w = [t1]
            b2, t2 = fm(u, 0, th)
            tp = DV(V.tensor_tensor, p.t[:, 30 + th * 512:30 + th * 512 + 512], b2.t[:, :], sg.t[:, sl], MUL,
                    w=[t2, t1, pz] + p.w)
            b2.w = [tp]
        u.done()
        t = AC(C.activation, a.t[:, :], p.t[:, 0:S], ACT.Identity, scale=taps(0, g), bias=pc("cb3", g),
               w=[tp] + a.w)
        for k in range(1, 31):
            t = DV(V.scalar_tensor_tensor, a.t[:, :], p.t[:, k:k + S], taps(k, g), a.t[:, :], MUL, ADD, w=[t])
        p.w = [t]
        for th in range(2):
            sl = slice(th * 512, th * 512 + 512)
            b = PB.get()
            t1 = mms(b.t[:, :], [(o128[:, :], a.t[:, sl])], b.w + [t, to128])
            t1 = DV(V.tensor_tensor, a.t[:, sl], a.t[:, sl], b.t[:, :], SUB, w=[t1])
            b.w = [t1]
            t2 = AC(C.activation, sg.t[:, sl], a.t[:, sl], ACT.Square, w=[t1])
            b = PB.get()
            t2 = mms(b.t[:, :], [(o128[:, :], sg.t[:, sl])], b.w + [t2])
            t2 = AC(C.activation, sg.t[:, sl], b.t[:, :], ACT.Ln, bias=eps[:, 0:1], w=[t2, teps])
            b.w = [t2]
            t2 = AC(C.activation, sg.t[:, sl], sg.t[:, sl], ACT.Exp, scale=-0.5, w=[t2])
            t1 = DV(V.tensor_tensor, a.t[:, sl], a.t[:, sl], sg.t[:, sl], MUL, w=[t1, t2])
            t1 = AC(C.activation, sg.t[:, sl], a.t[:, sl], ACT.Silu, scale=pc("cng", g), bias=pc("cnb", g), w=[t1])
        a.w = [t1]
        ycs.append(dma(SP, YC[g * 128:(g + 1) * 128, :], sg.t[:, :], w=[t1]))
        sg.w = [ycs[-1]]
    zgs = []
    for n in range(4):
        u = unit(W, [(2048 + n * 256, 256)])
        for m in range(2):
            sg = Sg_.get()
            for th in range(2):
                b, t = fm(u, m * 128, th)
                t = AC(C.activation, sg.t[:, th * 512:th * 512 + 512], b.t[:, :], ACT.Silu, w=[t] + sg.w)
                b.w = [t]
            r = (n * 2 + m) * 128
            zgs.append(dma(SP, ZG[r:r + 128, :], sg.t[:, :], w=[t]))
            sg.w = [zgs[-1]]
        u.done()
    fence()
    ph.close()

    ph = ExitStack()
    M128 = sbt(ph, [128, S])
    lb, lb1 = sbt(ph, [128, 8]), sbt(ph, [128, 8])
    Mi = sbt(ph, [128, 8, 128], I32)
    Mf = sbt(ph, [128, 128])
    t = PO(G.memset, M128[:, :], 1.0)
    tM = PO(G.memset, M128[:, :].rearrange("p (c t) -> p c t", t=128)[:, :, 0:1], 0.0, w=[t])
    LV = [64, 32, 16, 8, 4, 2, 1]
    tm_ = []
    for l, w_ in enumerate(LV):
        nb = 64 // w_
        mfv = Mf[:, :].rearrange("p (b h t) -> p b h t", b=nb, h=2)
        t = PO(G.memset, Mf[:, :], 0.0, w=[DV.now(), PO.now()])
        t = PO(G.memset, mfv[:, :, 1, :], 1.0, w=[t])
        t = PO(G.affine_select, out=Mf[:, :], in_=Mf[:, :], compare_op=ALU.is_ge, fill=0.0, base=0,
               pattern=[[-2 * w_, nb], [0, 2 * w_]], channel_multiplier=1, w=[t])
        t = PO(G.affine_select, out=Mf[:, :], in_=Mf[:, :], compare_op=ALU.is_ge, fill=0.0, base=w_ - 1,
               pattern=[[2 * w_, nb], [0, 2 * w_]], channel_multiplier=-1, w=[t])
        tMi = DV(V.tensor_copy, Mi[:, l, :], Mf[:, :], w=[t])
    tMi = DV(V.tensor_copy, Mi[:, 7, :], ident[:, :])
    l0 = PC[:, col["lb0"]:col["lb0"] + 8]
    l1 = PC[:, col["lb1"]:col["lb1"] + 8]
    t = DV(V.tensor_tensor, lb1[:, :], l0, l1, MAX)
    t = DV(V.tensor_tensor, lb[:, :], l0, lb1[:, :], SUB, w=[t])
    t = DV(V.tensor_tensor, lb1[:, :], l1, lb1[:, :], SUB, w=[t])
    t = AC(C.activation, lb[:, :], lb[:, :], ACT.Exp, w=[t])
    t = AC(C.activation, lb1[:, :], lb1[:, :], ACT.Exp, w=[t])
    t = DV(V.tensor_tensor, lb1[:, :], lb[:, :], lb1[:, :], ADD, w=[t])
    t = DV(V.reciprocal, lb1[:, :], lb1[:, :], w=[t])
    t = DV(V.tensor_tensor, lb[:, :], lb[:, :], lb1[:, :], MUL, w=[t])
    tlb = DV(V.tensor_scalar, lb1[:, :], lb[:, :], -1.0, 1.0, MUL, ADD, w=[t])
    qT, kT, bT, gT = (sbt(ph, [128, 2, S]) for _ in range(4))
    vt = sbt(ph, [128, NT, 256])
    Dr_ = Ring([sbt(ph, [128, S]) for _ in range(2)])
    Zr = Ring([sbt(ph, [128, S]) for _ in range(2)])
    At = sbt(ph, [128, NT, 128])
    tAz = PO(G.memset, At[:, :, :], 0.0)
    kdt = sbt(ph, [128, NT, 128])
    O = sbt(ph, [128, NT, 128])
    Sr = Ring([sbt(ph, [128, 128]) for _ in range(2)])
    dec = sbt(ph, [128, 8])
    prev = []
    yh = []
    for hp in range(4):
        u = unit(W, [(3072 + hp * 256, 256)])
        for m in range(2):
            for th in range(2):
                b, t = fm(u, m * 128, th)
                tq = AC(C.activation, qT[:, m, th * 512:th * 512 + 512], b.t[:, :], ACT.Silu, w=[t] + prev)
                b.w = [tq]
        u.done()
        u = unit(W, [(4096 + hp * 256, 256)])
        for m in range(2):
            for th in range(2):
                sl = slice(th * 512, th * 512 + 512)
                b, t = fm(u, m * 128, th)
                tf = AC(C.activation, bT[:, m, sl], b.t[:, :], ACT.Sigmoid, w=[t] + prev)
                tk = AC(C.activation, kT[:, m, sl], b.t[:, :], ACT.Sigmoid, scale=-1.0, w=[t] + prev)
                b.w = [tk]
        u.done()
        u = unit(W, [(5120 + hp * 256, 256)])
        for t4 in range(4):
            b, t = tm(u, 0, 256, [2 * t4, 2 * t4 + 1])
            tv = AC(C.copy, vt[:, 2 * t4:2 * t4 + 2, :], b.t[:, :].rearrange("p (a c) -> p a c", a=2), w=[t] + prev)
            b.w = [tv]
        u.done()
        u = unit(W, [(6144 + hp * 256, 256)])
        for m in range(2):
            for th in range(2):
                b, t = fm(u, m * 128, th)
                tg = AC(C.activation, gT[:, m, th * 512:th * 512 + 512], b.t[:, :], ACT.Silu, w=[t] + prev)
                b.w = [tg]
        u.done()
        for m in range(2):
            h = hp * 2 + m
            q, k, bb, v = qT[:, m, :], kT[:, m, :], bT[:, m, :], vt[:, :, m * 128:(m + 1) * 128]
            t = DV(V.tensor_scalar, bb, bb, lb1[:, h:h + 1], lb[:, h:h + 1], MUL, ADD, w=[tf, tlb])
            tk2 = DV(V.tensor_scalar, k, k, lb1[:, h:h + 1], None, MUL, w=[tk, tlb])
            dd = Dr_.get()
            t = DV(V.tensor_scalar, bb, bb, 2.0 ** -63, None, MAX, w=[t])
            t = AC(C.activation, dd.t[:, :], bb, ACT.Ln, w=[t] + dd.w)
            tb = DV(V.tensor_tensor_scan, bb, M128[:, :], dd.t[:, :], 0.0, op0=MUL, op1=ADD, w=[t, tM])
            dd.w = [tb]
            tAs = [tAz, tAz]
            for l in range(8):
                if l < 7:
                    w_ = LV[l]
                    nb = S // (2 * w_)
                    dd, z = Dr_.get(), Zr.get()
                    v4 = (lambda x, w_=w_: x.rearrange("p (b h t) -> p b h t", h=2, t=w_))
                    ref = v4(bb)[:, :, 0, w_ - 1:w_]
                    t1 = DV(V.tensor_tensor, v4(dd.t[:, :])[:, :, 0, :], bc(ref, [128, nb, w_]), v4(bb)[:, :, 0, :],
                            SUB, w=[tb] + dd.w)
                    t1 = DV(V.tensor_tensor, v4(dd.t[:, :])[:, :, 1, :], v4(bb)[:, :, 1, :], bc(ref, [128, nb, w_]),
                            SUB)
                    t1 = AC(C.activation, dd.t[:, :], dd.t[:, :], ACT.Exp, w=[t1])
                    t2 = PO(G.tensor_tensor, v4(z.t[:, :])[:, :, 0, :], v4(k)[:, :, 0, :],
                            v4(dd.t[:, :])[:, :, 0, :], MUL, w=[t1, tk2] + z.w)
                    t2 = PO(G.tensor_tensor, v4(z.t[:, :])[:, :, 1, :], v4(q)[:, :, 1, :],
                            v4(dd.t[:, :])[:, :, 1, :], MUL, w=[tq])
                    dd.w = [t2]
                    zl, zr, tz = z.t, z.t, t2
                for th in range(2):
                    b = PB.get()
                    for j in range(4):
                        sl = slice((th * 4 + j) * 128, (th * 4 + j) * 128 + 128)
                        l_, r_ = (z.t[:, sl], z.t[:, sl]) if l < 7 else (kT[:, m, sl], qT[:, m, sl])
                        t = mms(b.t[:, j * 128:(j + 1) * 128], [(l_, r_)], b.w + [tz, tk2, tq], inc=(j == 3))
                    tA = DV(V.copy_predicated, At[:, th * 4:th * 4 + 4, :],
                            bc(Mi[:, l:l + 1, :], [128, 4, 128]),
                            b.t[:, :].rearrange("p (a c) -> p a c", a=4),
                            w=[t, tMi, tAz, tAs[th]] + ([ow] if h else []))
                    tAs[th] = tA
                    b.w = [tA]
                if l < 7:
                    z.w = [t]
            bv = bb.rearrange("p (c t) -> p c t", t=128)
            dd = Dr_.get()
            t1 = DV(V.tensor_tensor, dd.t[:, :].rearrange("p (c t) -> p c t", t=128),
                    bc(bv[:, :, 127:128], [128, 8, 128]), bv, SUB, w=[tb] + dd.w)
            t1 = AC(C.activation, dd.t[:, :], dd.t[:, :], ACT.Exp, w=[t1])
            tkd = DV(V.tensor_tensor, dd.t[:, :], k, dd.t[:, :], MUL, w=[t1, tk2])
            tdec = AC(C.activation, dec[:, :], bv[:, :, 127], ACT.Exp, w=[DV.now()])
            z = Zr.get()
            t1 = AC(C.activation, z.t[:, :], bb, ACT.Exp, w=[tb] + z.w)
            tqx = DV(V.tensor_tensor, z.t[:, :], q, z.t[:, :], MUL, w=[t1])
            for th in range(2):
                b = PB.get()
                for j in range(4):
                    tt = th * 4 + j
                    t = PE(T.transpose, b.t[:, j * 128:(j + 1) * 128], dd.t[:, tt * 128:(tt + 1) * 128],
                           ident[:, :], w=b.w + [tkd], inc=(j == 3))
                tkt = AC(C.copy, kdt[:, th * 4:th * 4 + 4, :], b.t[:, :].rearrange("p (a c) -> p a c", a=4), w=[t])
                b.w = [tkt]
            dd.w = [t]
            so = None
            for th in range(2):
                kvb = PB.get()
                for j in range(4):
                    tt = th * 4 + j
                    tkv = mms(kvb.t[:, j * 128:(j + 1) * 128], [(kdt[:, tt, :], v[:, tt, :])],
                              kvb.w + [tkt, tv], inc=(j == 3))
                ob = PD.get()
                for j in range(4):
                    tt = th * 4 + j
                    o = ob.t[:, j * 128:(j + 1) * 128]
                    t = mms(o, [(At[:, tt, :], v[:, tt, :])] +
                            ([(z.t[:, tt * 128:(tt + 1) * 128], so.t[:, :])] if so else []),
                            ob.w + [tA, tv, tqx] + ([tso] if so else []))
                    if tt < 7:
                        sn = Sr.get()
                        kv = kvb.t[:, j * 128:(j + 1) * 128]
                        if so is None:
                            tso = DV(V.tensor_copy, sn.t[:, :], kv, w=[tkv] + sn.w)
                        else:
                            tso = DV(V.scalar_tensor_tensor, sn.t[:, :], so.t[:, :], dec[:, tt:tt + 1], kv, MUL,
                                     ADD, w=[tkv, tso, tdec] + sn.w)
                            so.w = [t, tso]
                        so = sn
                    else:
                        so.w = [t]
                kvb.w = [tso]
                to = AC(C.copy, O[:, th * 4:th * 4 + 4, :], ob.t[:, :].rearrange("p (a c) -> p a c", a=4),
                        w=[t, PE.now()])
                ob.w = [to]
            ow = t
            z.w = [t]
            s = Dr_.get()
            t = rms_heads(O[:, :, :], 8, 128, s.t[:, :].rearrange("p (a c) -> p a c", a=8), [to] + s.w, 1e-6)
            s.w = [t]
            for th in range(2):
                b = PB.get()
                for j in range(4):
                    t_ = PE(T.transpose, b.t[:, j * 128:(j + 1) * 128], O[:, th * 4 + j, :], ident[:, :],
                            w=b.w + [t], inc=(j == 3))
                gs = gT[:, m, th * 512:th * 512 + 512]
                ty = DV(V.scalar_tensor_tensor, gs, b.t[:, :], pc("ong", h), gs, MUL, MUL, w=[t_, tg])
                b.w = [ty]
            r = (8 + h) * 128
            yh.append(dma(SP, YM[r:r + 128, :], gT[:, m, :], w=[ty]))
        prev = [PE.now(), AC.now(), DV.now(), PO.now()] + yh[-2:]
    fence()
    ph.close()

    ph = ExitStack()
    X = sbt(ph, [128, NT, 1024])
    ph3 = ExitStack()
    stage = Ring([sbt(ph3, [128, S]) for _ in range(3)])
    gst = Ring([sbt(ph3, [128, S]) for _ in range(3)])
    xt = load_X(X, XD)
    for k in range(8):
        s = stage.get()
        td = dma(SP, s.t[:, :], YC[k * 128:(k + 1) * 128, :], w=s.w + ycs)
        t1 = AC(C.activation, HTh[:, k, :], s.t[:, :], ACT.Copy, w=[td])
        t2 = DV(V.tensor_tensor, HTl[:, k, :], s.t[:, :], HTh[:, k, :].bitcast(F32), SUB, w=[t1, td])
        s.w = [t1, t2]
    HT.w = [t1, t2]
    yc2 = []
    for n in range(4):
        u = unit(A["w_pw2_3"][0], [(n * 256, 256)])
        for m in range(2):
            r = (n * 2 + m) * 128
            g_ = gst.get()
            td = dma(SP, g_.t[:, :], ZG[r:r + 128, :], w=g_.w + zgs)
            for th in range(2):
                b, t = fm(u, m * 128, th)
                o = g_.t[:, th * 512:th * 512 + 512]
                t = DV(V.scalar_tensor_tensor, o, b.t[:, :], pc("bpw", n * 2 + m), o, ADD, MUL, w=[t, td])
                b.w = [t]
            yc2.append(dma(SP, YM[r:r + 128, :], g_.t[:, :], w=[t]))
            g_.w = [yc2[-1]]
        u.done()
    t = out_proj(X, A["w_out_3"][0], [1, 0], xt, stage, yc2 + yh)
    fence()
    ph3.close()
    ph2 = ExitStack()
    junk = sbt(ph2, [128, 1024])
    rs = rms_rows(X, [t], junk)
    to_HT(ph2, X, [], rs, "peg")
    fence()
    ph2.close()
    ph2 = ExitStack()
    pin = sbt(ph2, [128, NT, 256])
    Ph = sbt(ph2, [128, 2, S], F32R)
    Pl = sbt(ph2, [128, 2, S], F32R)
    gtr = Ring([sbt(ph2, [128, 512]) for _ in range(8)])
    tp = dma(SP, pin[:, :, :], A["p_3"][0, 0].rearrange("(t p) d -> p t d", p=128))
    for k in range(2):
        for th in range(2):
            b = PB.get()
            for j in range(4):
                t = PE(T.transpose, b.t[:, j * 128:(j + 1) * 128], pin[:, th * 4 + j, k * 128:(k + 1) * 128],
                       ident[:, :], w=b.w + [tp], inc=(j == 3))
            sl = slice(th * 512, th * 512 + 512)
            t1 = AC(C.activation, Ph[:, k, sl], b.t[:, :], ACT.Copy, w=[t])
            tP = DV(V.tensor_tensor, Pl[:, k, sl], b.t[:, :], Ph[:, k, sl].bitcast(F32), SUB, w=[t1])
            b.w = [t1, tP]
    for n in range(4):
        u = unit(A["w_pg_3"][0], [(n * 256, 256)])
        gts = []
        for t4 in range(4):
            b, t = tm(u, 0, 256, [2 * t4, 2 * t4 + 1])
            gt = gtr.get()
            t = AC(C.activation, gt.t[:, :], b.t[:, :], ACT.Sigmoid, w=[t] + gt.w)
            b.w = [t]
            gts.append((gt, t))
        u.done()
        u = unit(A["w_pp_3"][0], [(n * 256, 256)], k=2)
        for t4 in range(4):
            gt, tg = gts[t4]
            b = PD.get()
            for j in range(2):
                sl = slice((2 * t4 + j) * 128, (2 * t4 + j) * 128 + 128)
                pairs = []
                for k in range(2):
                    pairs += three(Ph[:, k, sl], Pl[:, k, sl], u.h[:, k, :], u.l[:, k, :])
                t = mms(b.t[:, j * 256:(j + 1) * 256], pairs, b.w + u.w + [tP], inc=(j == 1))
            t = DV(V.tensor_tensor, gt.t[:, :], b.t[:, :], gt.t[:, :], MUL, w=[t, tg])
            b.w = [t]
            o = X[:, 2 * t4:2 * t4 + 2, n * 256:(n + 1) * 256]
            t = PO(G.tensor_tensor, o, o, gt.t[:, :].rearrange("p (a c) -> p a c", a=2), ADD, w=[t])
            gt.w = [t]
        u.done()
    fence()
    ph2.close()
    ph2 = ExitStack()
    junk = sbt(ph2, [128, 1024])
    fg, t1 = row_bcast(ph2, A["final_g_3"])
    rs = rms_rows(X, [t], junk)
    toks = []
    for tt in range(NT):
        toks.append([DV(V.scalar_tensor_tensor, X[:, tt, :], X[:, tt, :], st[:, tt:tt + 1], fg[:, :], MUL, MUL,
                        w=[rs, t1])])
    stx = store_X(X, out[0], toks)
    ph2.close()
    ph.close()
    finish(nc, ctx, PE, AC, DV, PO, SP, stx)


def finish(nc, ctx, PE, AC, DV, PO, SP, last):
    SP.later(lambda wait: wait(last))
    block = ctx.enter_context(nc.Block())

    @block.sync
    def _(e):
        SP.emit(e)

    @block.tensor
    def _(e):
        PE.emit(e)

    @block.vector
    def _(e):
        DV.emit(e)

    @block.scalar
    def _(e):
        AC.emit(e)

    @block.gpsimd
    def _(e):
        PO.emit(e)


_INS = [
    "x", "norm_mix_g", "w_in", "w_a2_fwd", "b_a_fwd", "w_a2_bwd", "b_a_bwd", "gla_norm_g", "sgu_norm_g", "w_s",
    "b_s", "w_out", "norm_mlp_g", "w_mlp1", "w_mlp2", "final_norm_g", "ln_emb_g_2", "ln_emb_b_2", "w_in_2",
    "conv_w_2", "conv_b_2", "A_log_fwd_2", "A_log_bwd_2", "dt_bias_fwd_2", "dt_bias_bwd_2", "D_skip_2",
    "ssm_norm_g_2", "lambda_q1_2", "lambda_k1_2", "lambda_q2_2", "lambda_k2_2", "subln_g_2", "w_out_2", "ln_g_2",
    "ln_b_2", "p_3", "ln_g_3", "w_in_3", "conv_w_3", "conv_b_3", "cnorm_g_3", "cnorm_b_3", "w_pw2_3", "b_pw2_3",
    "lb_logits_3", "onorm_g_3", "w_out_3", "pe_norm_g_3", "w_pg_3", "w_pp_3", "final_g_3",
]


def kernel(**inputs):
    import numpy as _np
    import concourse.bacc as _bacc
    from concourse import mybir as _mybir
    from concourse.bass_utils import run_bass_kernel_spmd as _run

    nc = _bacc.Bacc("TRN2", target_bir_lowering=False, num_devices=1)
    arrays, args = {}, {}
    for name in _INS:
        a = _np.ascontiguousarray(inputs[name])
        arrays[f"in_{name}_dram"] = a
        args[name] = nc.dram_tensor(f"in_{name}_dram", a.shape, _mybir.dt.from_np(a.dtype),
                                    kind="ExternalInput").ap()
    o = nc.dram_tensor("out_0_dram", (1, 1024, 1024), F32, kind="ExternalOutput").ap()
    build(nc, args, o)
    r = _run(nc, [arrays], core_ids=[0])
    return r.results[0]["out_0_dram"]
```

```python
import math
from contextlib import ExitStack

import numpy as np
import concourse.bass as bass
from concourse import mybir

F32 = mybir.dt.float32
F32R = mybir.dt.float32r
I32 = mybir.dt.int32
ALU = mybir.AluOpType
ACT = mybir.ActivationFunctionType
AX = mybir.AxisListType
ADD, SUB, MUL, MAX, MIN = ALU.add, ALU.subtract, ALU.mult, ALU.max, ALU.min
ALPHA = 2.0 ** 0.25
S = 1024
NT = 8


class Queue:

    def __init__(self, sem):
        self.sem, self.n, self.items = sem, 0, []

    def __call__(self, fn, *a, w=(), inc=True, **k):
        self.n += inc
        self.items.append((fn, a, k, list(w), self.sem if inc else None, 1))
        return (self.sem, self.n)

    def dma(self, fn, out, in_, sem, w=()):
        self.items.append((fn, (out, in_), {}, list(w), sem, 16))

    def later(self, fn):
        self.items.append((fn, None, None, [], None, 0))

    def now(self):
        return (self.sem, self.n)

    def emit(self, eng):
        seen = {}

        def wait(w):
            for sem, v in w:
                if v > 0 and seen.get(id(sem), 0) < v:
                    eng.wait_ge(sem, v)
                    seen[id(sem)] = v
        for fn, a, k, w, sem, by in self.items:
            if a is None:
                fn(wait)
                continue
            wait(w)
            ins = fn(*a, **k)
            if sem is not None:
                ins.then_inc(sem, by)


class Slot:

    def __init__(self, t):
        self.t, self._w, self.held = t, [], False

    @property
    def w(self):
        return self._w

    @w.setter
    def w(self, toks):
        self._w, self.held = toks, False


class Ring:
    def __init__(self, ts):
        self.s, self.i = [Slot(t) for t in ts], -1

    def get(self):
        for _ in self.s:
            self.i = (self.i + 1) % len(self.s)
            if not self.s[self.i].held:
                self.s[self.i].held = True
                return self.s[self.i]
        raise RuntimeError("no slot is free")


def weave(*parts):
    live = [[g, n, 0] for g, n in parts]
    while live:
        x = min(live, key=lambda x: (x[2] + 0.5) / x[1])
        x[2] += 1
        try:
            next(x[0])
        except StopIteration:
            live.remove(x)


def steps(g):
    for _ in g:
        pass


def bc(ap, shape):
    return ap.broadcast_to(shape)


def build(nc, A, out, upto=3, tap=None):
    ctx = ExitStack()
    with ctx:
        program(nc, A, out, ctx, upto, tap)


def program(nc, A, out, ctx, upto, tap):
    names = [0]

    def sbt(c, shape, dt=F32):
        names[0] += 1
        return c.enter_context(nc.sbuf_tensor(f"t{names[0]}", shape, dt))

    def sem(name):
        return ctx.enter_context(nc.semaphore(name))

    PE, AC, DV, PO = (Queue(sem(n)) for n in ("s_pe", "s_ac", "s_dv", "s_po"))
    SP = Queue(sem("s_sp"))
    T, V, G, C = nc.tensor, nc.vector, nc.gpsimd, nc.scalar
    dram = nc.dram_tensor
    YM = dram("ym_scratch", [2048, S], F32, kind="Internal").ap()
    XD = dram("x_scratch", [S, 1024], F32, kind="Internal").ap()
    ZG = dram("zg_scratch", [1024, S], F32, kind="Internal").ap()
    ZS = dram("zs_scratch", [8, 128, 1024], F32, kind="Internal").ap()
    YC = dram("yc_scratch", [1024, S], F32, kind="Internal").ap()

    dsem = [[sem(f"s_d{i}"), 0] for i in range(24)]
    dcount = [0]
    stores = {}

    def dma(q, out_, in_, w=()):
        d = dsem[dcount[0] % len(dsem)]
        dcount[0] += 1
        before = [(d[0], d[1])] if d[1] else []
        d[1] += 16
        fn = {id(SP): nc.sync.dma_start, id(PO): G.dma_start, id(AC): C.dma_start}[id(q)]
        q.dma(fn, out_, in_, d[0], w=list(w) + before)
        return (d[0], d[1])

    HTh = sbt(ctx, [128, 8, S], F32R)
    HTl = sbt(ctx, [128, 8, S], F32R)
    WR = [sbt(ctx, [128, 2048]) for _ in range(2)]
    WH = [sbt(ctx, [128, 2048], F32R) for _ in range(2)]
    WL = [sbt(ctx, [128, 2048], F32R) for _ in range(2)]
    ident = sbt(ctx, [128, 128])
    Uinc = sbt(ctx, [128, 128])
    Linc = sbt(ctx, [128, 128])
    ones = sbt(ctx, [128, 128])
    nhalf = sbt(ctx, [128, 64])
    PC = sbt(ctx, [128, 4 * 128])
    ss = sbt(ctx, [128, 64])
    st = sbt(ctx, [128, 64])

    PD = Ring([ctx.enter_context(nc.psum_tensor(f"pd{i}", [128, 512], F32)) for i in range(4)])
    PQt = [ctx.enter_context(nc.psum_tensor(f"pq{i}", [128, 1024], F32)) for i in range(2)]
    PB = Ring([PQt[0][:, 0:512], PQt[0][:, 512:1024], PQt[1][:, 0:512], PQt[1][:, 512:1024]])

    NR = 2
    s_wr = [sem(f"s_wr{i}") for i in range(NR)]
    s_wh, s_wl = sem("s_wh"), sem("s_wl")
    units = []
    freed = []

    def load_unit(i):
        def go(wait):
            if i >= len(units):
                return
            if i >= NR:
                wait([(s_wh, i - NR + 1), (s_wl, i - NR + 1)])
            sz, pieces = units[i]
            for k, (o, src) in enumerate(pieces):
                ins = nc.sync.dma_start(o(WR[i % NR]), src)
                ins.then_inc(s_wr[i % NR], 16)
        SP.later(go)

    def need(i):
        return (s_wr[i % NR], sum(16 * len(units[j][1]) for j in range(i % NR, i + 1, NR)))

    def split_unit(i):
        def hi(wait):
            if i < len(units):
                wait([need(i)] + ([freed[i - 2]] if i >= 2 else []))
                n = units[i][0]
                C.activation(WH[i % 2][:, 0:n], WR[i % NR][:, 0:n], ACT.Copy).then_inc(s_wh, 1)

        def lo(wait):
            if i < len(units):
                wait([need(i), (s_wh, i + 1)])
                n = units[i][0]
                V.tensor_tensor(WL[i % 2][:, 0:n], WR[i % NR][:, 0:n],
                                  WH[i % 2][:, 0:n].bitcast(F32), SUB).then_inc(s_wl, 1)
        AC.later(hi)
        DV.later(lo)

    class Unit:
        def __init__(self, pieces, k, c):
            i = len(units)
            units.append((k * c, pieces))
            freed.append(None)
            if i == 0:
                for j in range(NR):
                    load_unit(j)
                split_unit(0)
            else:
                load_unit(i + NR - 1)
            split_unit(i + 1)
            self.i = i
            self.h = WH[i % 2][:, 0:k * c].rearrange("p (k c) -> p k c", k=k)
            self.l = WL[i % 2][:, 0:k * c].rearrange("p (k c) -> p k c", k=k)
            self.w = [(s_wh, i + 1), (s_wl, i + 1)]

        def done(self):
            freed[self.i] = PE.now()

    def unit(W, parts, k0=0, k=8):
        c = sum(n for _, n in parts)
        pieces, o = [], 0
        for c0, n in parts:
            src = W[k0 * 128:(k0 + k) * 128, c0:c0 + n].rearrange("(k p) c -> p k c", p=128)

            def dst(t, o=o, n=n):
                return t[:, 0:k * c].rearrange("p (k c) -> p k c", k=k)[:, :, o:o + n]
            pieces.append((dst, src))
            o += n
        return Unit(pieces, k, c)

    def mms(out_, pairs, w, first=True, last=True, inc=True, start=None):
        n = len(pairs)
        tok = None
        for j, (l, r) in enumerate(pairs):
            s_ = (first and j == 0) if start is None else (start and j == 0)
            tok = PE(T.matmul, out_, l, r, start=s_, stop=(last and j == n - 1),
                     skip_group_check=True, w=w if j == 0 else (), inc=(inc and j == n - 1))
        return tok

    def three(lh, ll, rh, rl):
        return [(lh, rh), (lh, rl), (ll, rh)]

    HT = Slot(None)
    HT.r = []

    def fm(u, m0, th, kk=8, w=()):
        b = PD.get()
        sl = slice(th * 512, th * 512 + 512)
        pairs = []
        for k in range(kk):
            pairs += three(u.h[:, k, m0:m0 + 128], u.l[:, k, m0:m0 + 128], HTh[:, k, sl], HTl[:, k, sl])
        t = mms(b.t[:, :], pairs, b.w + u.w + HT.w + list(w))
        return b, t

    def tm(u, c0, n, tts, kk=8):
        b = PD.get()
        t = None
        for j, tt in enumerate(tts):
            sl = slice(tt * 128, tt * 128 + 128)
            pairs = []
            for k in range(kk):
                pairs += three(HTh[:, k, sl], HTl[:, k, sl], u.h[:, k, c0:c0 + n], u.l[:, k, c0:c0 + n])
            t = mms(b.t[:, j * n:(j + 1) * n], pairs, b.w + u.w + HT.w, inc=(j == len(tts) - 1))
        return b, t

    def fence(extra=()):
        w = [q.now() for q in (PE, AC, DV, PO)] + list(extra) + [(d[0], d[1]) for d in dsem if d[1]]
        for q in (PE, AC, DV, PO, SP):
            q.later(lambda wait, w=w: wait(w))

    t = PO(G.memset, ident[:, :], 0.0)
    t = PO(G.affine_select, out=ident[:, :], in_=ident[:, :], compare_op=ALU.not_equal, fill=1.0,
           base=0, pattern=[[-1, 128]], channel_multiplier=1, w=[t])
    t = PO(G.memset, ones[:, :], 1.0)
    PO(G.memset, nhalf[:, :], -0.5)
    PO(G.affine_select, out=Uinc[:, :], in_=ones[:, :], compare_op=ALU.is_ge, fill=0.0,
       base=0, pattern=[[1, 128]], channel_multiplier=-1, w=[t])
    CST = PO(G.affine_select, out=Linc[:, :], in_=ones[:, :], compare_op=ALU.is_ge, fill=0.0,
             base=0, pattern=[[-1, 128]], channel_multiplier=1)

    def rsqrt(dst, src, scale, eps, w):
        n = src.shape[-1]
        t = DV(V.tensor_scalar, dst, src, scale, eps, MUL, ADD, w=w)
        return PO(G.tensor_tensor, dst, dst, nhalf[:, 0:n], ALU.pow, w=[t])

    col = {}

    def columns(c, n0, parts):
        PR = sbt(c, [128, 128])
        z = PO(G.memset, PR[:, :], 0.0)
        r, toks = 0, []
        for name, ap in parts:
            k = ap.shape[0]
            toks.append(dma(SP, PR[r:r + k, :], ap, w=[z]))
            col[name] = n0 + r
            r += k
        assert r <= 128
        b = PB.get()
        t = PE(T.transpose, b.t[:, 0:128], PR[:, :], ident[:, :], w=b.w + toks + [CST])
        t = DV(V.tensor_copy, PC[:, n0:n0 + 128], b.t[:, 0:128], w=[t])
        b.w = [t]
        return t

    def vec(ap):
        return ap.rearrange("(k p) -> k p", p=128)

    def pc(name, i=0):
        c = col[name] + i
        return PC[:, c:c + 1]

    lam = sbt(ctx, [128, 4])
    ph = ExitStack()
    toks = []
    toks.append(columns(ph, 0, [
        ("g_mix", vec(A["norm_mix_g"][0])), ("g_mlp", vec(A["norm_mlp_g"][0])),
        ("ba0", vec(A["b_a_fwd"][0])), ("ba1", vec(A["b_a_bwd"][0])),
        ("gla_g", A["gla_norm_g"][0]), ("sgu_g", A["sgu_norm_g"][0]),
        ("cw2", A["conv_w_2"][0].rearrange("j (k p) -> (j k) p", p=128)),
        ("cb2", vec(A["conv_b_2"][0])), ("ssm_g", vec(A["ssm_norm_g_2"][0])),
        ("subln", A["subln_g_2"])]))
    toks.append(columns(ph, 128, [
        ("cw3a", A["conv_w_3"][0, 0:16, :].rearrange("j (k p) -> (j k) p", p=128))]))
    toks.append(columns(ph, 256, [
        ("cw3b", A["conv_w_3"][0, 16:31, :].rearrange("j (k p) -> (j k) p", p=128))]))
    toks.append(columns(ph, 384, [
        ("g3", vec(A["ln_g_3"][0])), ("cb3", vec(A["conv_b_3"][0])),
        ("cng", vec(A["cnorm_g_3"][0])), ("cnb", vec(A["cnorm_b_3"][0])),
        ("bpw", vec(A["b_pw2_3"][0])), ("lb0", vec(A["lb_logits_3"][0])),
        ("lb1", vec(A["lb_logits_3"][1])), ("ong", vec(A["onorm_g_3"][0])),
        ("peg", vec(A["pe_norm_g_3"][0]))]))
    PCt = toks

    lv = sbt(ph, [128, 5, 64])
    toks = [dma(SP, lv[:, i, :], A[n].partition_broadcast(128).rearrange("p a d -> p (a d)"))
            for i, n in enumerate(("lambda_q1_2", "lambda_k1_2", "lambda_q2_2", "lambda_k2_2"))]
    for i in range(2):
        t = DV(V.tensor_tensor, lv[:, 4, :], lv[:, 2 * i, :], lv[:, 2 * i + 1, :], MUL, w=toks + [DV.now()])
        t = DV(V.tensor_reduce, lam[:, i:i + 1], lv[:, 4, :], AX.X, ADD, w=[t])
    t = AC(C.activation, lam[:, 0:2], lam[:, 0:2], ACT.Exp, w=[t])
    t = DV(V.tensor_tensor, lam[:, 2:3], lam[:, 1:2], lam[:, 0:1], SUB, w=[t])
    t = DV(V.tensor_scalar, lam[:, 3:4], lam[:, 2:3], -(0.8 - 0.6 * math.exp(0.0)), None, ADD, w=[t])
    t = DV(V.tensor_scalar, pc("subln"), pc("subln"), 1.0 - (0.8 - 0.6 * math.exp(0.0)), None, MUL, w=PCt)
    PCt = PCt + [t]
    fence(PCt)
    ph.close()

    def row_bcast(c, ap):
        n = ap.shape[-1]
        r = sbt(c, [128, n])
        return r, dma(SP, r[:, :], ap.partition_broadcast(128))

    def load_X(X, src):
        v = src.rearrange("(t p) d -> p t d", p=128)
        return [dma(SP, X[:, tt, :], v[:, tt, :]) for tt in range(NT)]

    def store_X(X, dst, w):
        v = dst.rearrange("(t p) d -> p t d", p=128)
        return [dma(SP, v[:, tt, :], X[:, tt, :], w=w[tt] if isinstance(w[0], list) else w) for tt in range(NT)]

    def split_HT(k, sl, src, scale, w):
        if scale is None:
            t1 = AC(C.activation, HTh[:, k, sl], src, ACT.Copy, w=w)
            t2 = DV(V.tensor_tensor, HTl[:, k, sl], src, HTh[:, k, sl].bitcast(F32), SUB, w=[t1] + w)
        else:
            t1 = AC(C.activation, HTh[:, k, sl], src, ACT.Copy, scale=scale, w=w)
            t2 = DV(V.scalar_tensor_tensor, HTl[:, k, sl], src, scale, HTh[:, k, sl].bitcast(F32), MUL, SUB,
                    w=[t1] + w)
        return t1, t2

    def squares(X, th, wt):
        a, b = PB.s[0], PB.s[1]
        for tt in range(th * 4, th * 4 + 4):
            t = AC(C.activation, PQt[0][:, :], X[:, tt, :], ACT.Square, accum_out=ss[:, 16 + tt:17 + tt],
                   w=list(wt[tt]) + a.w + b.w + [AC.now()])
        a.w, b.w = [t], [t]
        return t

    def rstd(th, t):
        sl = slice(16 + th * 4, 20 + th * 4)
        return rsqrt(st[:, sl], ss[:, sl], 1.0 / 1024, 1e-6, [t])

    def to_HT(srcs, th, ws, gname):
        for k in range(8):
            b = PD.get()
            for j in range(4):
                t = PE(T.transpose, b.t[:, j * 128:(j + 1) * 128], srcs[j][:, k * 128:(k + 1) * 128], ident[:, :],
                       w=b.w + [ws[j]], inc=(j == 3))
            t1, t2 = split_HT(k, slice(th * 512, th * 512 + 512), b.t[:, :], pc(gname, k) if gname else None, [t])
            b.w = [t1, t2]
            yield
        HT.w = [t1, t2]

    def norm_HT(X, XN, wt, gname):
        rs = [rstd(0, squares(X, 0, wt))]
        tsq = squares(X, 1, wt)
        sl, tok = [XN.get() for _ in range(8)], [None] * 8

        def scaled(tt, r):
            c = 16 + tt
            tok[tt] = DV(V.tensor_scalar, sl[tt].t[:, :], X[:, tt, :], st[:, c:c + 1], None, MUL,
                         w=[r] + list(wt[tt]) + sl[tt].w)

        for tt in range(4):
            scaled(tt, rs[0])
        r1 = rstd(1, tsq)
        for k, _ in enumerate(to_HT([x.t for x in sl[0:4]], 0, tok[0:4], gname)):
            if k % 2 == 1:
                scaled(4 + k // 2, r1)
        steps(to_HT([x.t for x in sl[4:8]], 1, tok[4:8], gname))
        for x in sl:
            x.w = [PE.now()]

    def rms_heads(O, n, d, sq, w, eps, name_scale=None):
        t = PO(G.tensor_tensor, sq, O, O, MUL, w=w)
        t = DV(V.tensor_reduce, ss[:, 0:n], sq, AX.X, ADD, w=[t])
        t = rsqrt(st[:, 0:n], ss[:, 0:n], 1.0 / d, eps, [t])
        return DV(V.tensor_tensor, O, O, bc(st[:, 0:n].unsqueeze(2), [128, n, d]), MUL, w=[t])

    def out_proj(X, W, kgroups, wX, stage, ytoks):
        def fetch(kg):
            for k in range(8):
                s = stage.get()
                r = (kg * 8 + k) * 128
                got[kg, k] = s, dma(AC, s.t[:, :], YM[r:r + 128, :], w=s.w + ytoks[kg])

        got, last = {}, [None] * NT
        for gi, kg in enumerate(kgroups):
            if gi == 0:
                fetch(kg)
            reads = [PE.now()]
            HT.k = []
            for k in range(8):
                s, td = got[kg, k]
                t1 = AC(C.activation, HTh[:, k, :], s.t[:, :], ACT.Copy, w=[td] + reads)
                t2 = DV(V.tensor_tensor, HTl[:, k, :], s.t[:, :], HTh[:, k, :].bitcast(F32), SUB, w=[t1, td] + reads)
                s.w = [t1, t2]
                HT.k.append([t1, t2])
            HT.w = [t1, t2]
            if gi + 1 < len(kgroups):
                fetch(kgroups[gi + 1])
            for n in range(4):
                u = unit(W, [(n * 256, 256)], k0=kg * 8)
                for t4 in range(4):
                    b, t = tm(u, 0, 256, [2 * t4, 2 * t4 + 1])
                    o = X[:, 2 * t4:2 * t4 + 2, n * 256:(n + 1) * 256]
                    t = DV(V.tensor_tensor, o, b.t[:, :].rearrange("p (a c) -> p a c", a=2), o, ADD, w=[t] + wX)
                    b.w = [t]
                    last[2 * t4] = last[2 * t4 + 1] = [t]
                u.done()
        return last

    x_in = A["x"][0]
    ph = ExitStack()
    X = sbt(ph, [128, NT, 1024])
    xt = load_X(X, x_in)
    norm_HT(X, Ring([sbt(ph, [128, 1024]) for _ in range(8)]), [[x] for x in xt], "g_mix")
    fence()
    ph.close()

    W = A["w_in"][0]
    ph = ExitStack()
    M64 = sbt(ph, [128, S])
    aT = sbt(ph, [32, S])
    wa = [sbt(ph, [32, 256]) for _ in range(2)]
    qT, kT, bb = sbt(ph, [128, S]), sbt(ph, [128, S]), sbt(ph, [128, S])
    DE = sbt(ph, [128, 2, S])
    qin, kin, qx = sbt(ph, [128, S]), sbt(ph, [128, S]), sbt(ph, [128, S])
    vt = sbt(ph, [128, NT, 256])
    kdt = sbt(ph, [128, NT, 128])
    Am = sbt(ph, [128, 2, NT, 128])
    Sg = sbt(ph, [128, 16, 128])
    O = sbt(ph, [128, NT, 2, 128])
    dec = sbt(ph, [128, 16])
    mk = sbt(ph, [128, 2, 64])
    t = PO(G.memset, M64[:, :], 1.0)
    t = PO(G.memset, M64[:, :].rearrange("p (c t) -> p c t", t=64)[:, :, 0:1], 0.0, w=[t])
    PO(G.memset, Am[:, :, :, :], 0.0)
    t = PO(G.memset, mk[:, :, :], 1.0)
    for half in range(2):
        r = slice(64 * half, 64 * half + 64)
        PO(G.affine_select, out=mk[r, 0, :], in_=mk[r, 0, :], compare_op=ALU.is_ge, fill=0.0,
           base=0, pattern=[[1, 64]], channel_multiplier=-1, w=[t])
        PO(G.affine_select, out=mk[r, 1, :], in_=mk[r, 1, :], compare_op=ALU.is_gt, fill=0.0,
           base=0, pattern=[[-1, 64]], channel_multiplier=1, w=[t])
    PO(G.memset, wa[0][:, :], 0.0)
    t = PO(G.memset, wa[1][:, :], 0.0)
    g0 = t
    wat = [dma(SP, wa[0][0:16, :], A["w_a2_fwd"][0], w=[t]), dma(SP, wa[1][16:32, :], A["w_a2_bwd"][0], w=[t])]
    u = unit(W, [(1536, 128)])
    for th in range(2):
        b, t = fm(u, 0, th)
        t = AC(C.copy, aT[:, th * 512:th * 512 + 512], b.t[0:32, :], w=[t])
        b.w = [t]
    u.done()
    at = t
    ysp = []
    prev = []
    for pt in range(2):
        u = unit(W, [(pt * 128, 128), (256 + pt * 128, 128)])
        for th in range(2):
            sl = slice(th * 512, th * 512 + 512)
            b, t = fm(u, 0, th)
            tq = AC(C.mul, qT[:, sl], b.t[:, :], 0.125, w=[t] + prev)
            b.w = [tq]
            b, t = fm(u, 128, th)
            tk = DV(V.tensor_copy, kT[:, sl], b.t[:, :], w=[t] + prev)
            b.w = [tk]
        u.done()
        u = unit(W, [(512 + pt * 256, 256)])
        for t4 in range(4):
            b, t = tm(u, 0, 256, [2 * t4, 2 * t4 + 1])
            tv = AC(C.copy, vt[:, 2 * t4:2 * t4 + 2, :], b.t[:, :].rearrange("p (a c) -> p a c", a=2), w=[t] + prev)
            b.w = [tv]
        u.done()
        for d in range(2):
            D, E = DE[:, 0, :], DE[:, 1, :]
            for th in range(2):
                sl = slice(th * 512, th * 512 + 512)
                b = PB.get()
                t = mms(b.t[:, :], [(wa[d][:, pt * 128:(pt + 1) * 128], aT[:, sl])], b.w + [at] + wat)
                t = AC(C.activation, D[:, sl], b.t[:, :], ACT.Identity, bias=pc(f"ba{d}", pt), w=[t] + prev + [DV.now(), PE.now()])
                b.w = [t]
            t1 = AC(C.activation, E, D, ACT.Abs, w=[t])
            t1 = AC(C.activation, E, E, ACT.Exp, scale=-1.0, w=[t1])
            t1 = AC(C.activation, E, E, ACT.Ln, bias=1.0, w=[t1])
            t = DV(V.tensor_scalar, D, D, 0.0, 1.0 / 16, MIN, MUL, w=[t, t1])
            t = DV(V.scalar_tensor_tensor, D, E, -1.0 / 16, D, MUL, ADD, w=[t])
            if d == 0:
                t = DV(V.tensor_tensor_scan, bb[:, :], M64[:, :], D, 0.0, op0=MUL, op1=ADD, w=[t, g0])
            else:
                t = DV(V.tensor_tensor_scan, bb[:, ::-1], M64[:, :], DE[:, 0, ::-1], 0.0, op0=MUL, op1=ADD, w=[t])
            bv = bb[:, :].rearrange("p (c t) -> p c t", t=64)
            Dv = D.rearrange("p (c t) -> p c t", t=64)
            mid, end = (32, 63) if d == 0 else (31, 0)
            t = DV(V.tensor_tensor, Dv, bv, bc(bv[:, :, mid:mid + 1], [128, 16, 64]), SUB, w=[t])
            t1 = AC(C.activation, E, D, ACT.Exp, w=[t])
            t = DV(V.tensor_tensor, qin[:, :], qT[:, :], E, MUL, w=[t1, tq])
            t2 = AC(C.activation, E, D, ACT.Exp, scale=-1.0, w=[t])
            ti = DV(V.tensor_tensor, kin[:, :], kT[:, :], E, MUL, w=[t2, tk])
            t3 = DV(V.tensor_tensor, Dv, bc(bv[:, :, end:end + 1], [128, 16, 64]), bv, SUB, w=[t2])
            t3 = AC(C.activation, D, D, ACT.Exp, w=[t3])
            tkd = DV(V.tensor_tensor, D, kT[:, :], D, MUL, w=[t3])
            t4_ = AC(C.activation, E, bb[:, :], ACT.Exp, w=[ti])
            tdec = AC(C.activation, dec[:, :], bv[:, :, end], ACT.Exp, w=[DV.now()])
            tqx = DV(V.tensor_tensor, qx[:, :], qT[:, :], E, MUL, w=[t4_])
            for th in range(2):
                b = PB.get()
                for j in range(4):
                    tt = th * 4 + j
                    t = PE(T.transpose, b.t[:, j * 128:(j + 1) * 128], D[:, tt * 128:(tt + 1) * 128], ident[:, :],
                           w=b.w + [tkd], inc=(j == 3))
                tkt = AC(C.copy, kdt[:, th * 4:th * 4 + 4, :], b.t[:, :].rearrange("p (a c) -> p a c", a=4), w=[t])
                b.w = [tkt]
            banks = [PB.get(), PB.get()]
            for hh in range(2):
                r = slice(64 * hh, 64 * hh + 64)
                b = banks[hh]
                for c in range(16):
                    half, cs = c % 2, slice(64 * c, 64 * c + 64)
                    t = mms(b.t[64 * half:64 * half + 64, 64 * (c // 2):64 * (c // 2) + 64],
                            [(kin[r, cs], qin[r, cs])], b.w + [ti], inc=(c == 15))
                for half in range(2):
                    p = slice(64 * half, 64 * half + 64)
                    ta = DV(V.tensor_tensor, Am[p, hh, :, 64 * half:64 * half + 64],
                            b.t[p, :].rearrange("p (a c) -> p a c", a=8),
                            bc(mk[p, d:d + 1, :], [64, 8, 64]), MUL, w=[t, g0])
                b.w = [ta]
            order = list(range(16)) if d == 0 else list(range(15, -1, -1))
            t = DV(V.memset, Sg[:, order[0], :], 0.0, w=[PE.now()])
            ts = t
            for q4 in range(4):
                cs = order[q4 * 4:q4 * 4 + 4]
                banks = [PB.get(), PB.get()]
                for j, c in enumerate(cs):
                    half, tt = c % 2, c // 2
                    r = slice(64 * half, 64 * half + 64)
                    for hh in range(2):
                        t = mms(banks[half].t[64 * hh:64 * hh + 64, (j // 2) * 128:(j // 2) * 128 + 128],
                                [(kdt[r, tt, 64 * hh:64 * hh + 64], vt[r, tt, hh * 128:hh * 128 + 128])],
                                banks[half].w + [tkt, tv], inc=(j == 3 and hh == 1))
                for j, c in enumerate(cs):
                    i = q4 * 4 + j
                    if i < 15:
                        ts = DV(V.scalar_tensor_tensor, Sg[:, order[i + 1], :], Sg[:, c, :], dec[:, c:c + 1],
                                banks[c % 2].t[:, (j // 2) * 128:(j // 2) * 128 + 128], MUL, ADD, w=[t, ts, tdec])
                for b in banks:
                    b.w = [ts]
            for hh in range(2):
                r = slice(64 * hh, 64 * hh + 64)
                for th in range(2):
                    b = PB.get()
                    for j in range(4):
                        tt = th * 4 + j
                        o = b.t[:, j * 128:(j + 1) * 128]
                        mms(o, [(Am[:, hh, tt, :], vt[:, tt, hh * 128:(hh + 1) * 128])], b.w + [ta, tv, ts, tqx],
                            last=False, inc=False)
                        for half in range(2):
                            c = 2 * tt + half
                            t = mms(b.t[64 * half:64 * half + 64, j * 128:(j + 1) * 128],
                                    [(qx[r, 64 * c:64 * c + 64], Sg[r, c, :])], (), first=False,
                                    inc=(half == 1))
                    ov = O[:, th * 4:th * 4 + 4, hh, :]
                    bvw = b.t[:, :].rearrange("p (a c) -> p a c", a=4)
                    if d == 0:
                        to = DV(V.tensor_copy, ov, bvw, w=[t] + prev)
                    else:
                        to = DV(V.tensor_tensor, ov, bvw, ov, ADD, w=[t, DV.now()])
                    b.w = [to]
        u = unit(W, [(1024 + pt * 256, 256)])
        gw = [PE.now(), AC.now(), DV.now()]
        for hh in range(2):
            for th in range(2):
                b, t = fm(u, hh * 128, th)
                tg = AC(C.activation, DE[:, hh, th * 512:th * 512 + 512], b.t[:, :], ACT.Silu, w=[t] + gw)
                b.w = [tg]
        u.done()
        Of = O[:, :, :, :].rearrange("p a b c -> p (a b) c")
        t = rms_heads(Of, 16, 128, Sg[:, :, :], [to, PE.now()], 1e-6)
        for hh in range(2):
            for th in range(2):
                b = PB.get()
                for j in range(4):
                    tt_ = PE(T.transpose, b.t[:, j * 128:(j + 1) * 128], O[:, th * 4 + j, hh, :], ident[:, :],
                             w=b.w + [t], inc=(j == 3))
                gs = DE[:, hh, th * 512:th * 512 + 512]
                ty = DV(V.scalar_tensor_tensor, gs, b.t[:, :], pc("gla_g", pt * 2 + hh), gs, MUL, MUL, w=[tt_, tg])
                b.w = [ty]
            r = (pt * 2 + hh) * 128
            ysp.append(dma(SP, YM[r:r + 128, :], DE[:, hh, :], w=[ty]))
        prev = [PE.now(), AC.now(), DV.now()] + ysp[-2:]
    fence()
    ph.close()

    ph = ExitStack()
    wsr = sbt(ph, [128, 4, 128])
    wsT = sbt(ph, [128, 4, 128])
    bsr, bst = row_bcast(ph, A["b_s"][0].rearrange("g p -> (g p)"))
    wst = dma(SP, wsr[:, :, :], A["w_s"][0].rearrange("g p q -> p g q"))
    b = PB.get()
    for g in range(4):
        t = PE(T.transpose, b.t[:, g * 128:(g + 1) * 128], wsr[:, g, :], ident[:, :], w=b.w + [wst], inc=(g == 3))
    twT = AC(C.copy, wsT[:, :, :], b.t[:, :].rearrange("p (a c) -> p a c", a=4), w=[t])
    b.w = [twT]
    VS = Ring([sbt(ph, [128, NT, 2, 128]) for _ in range(2)])
    UT = Ring([sbt(ph, [128, 2, S]) for _ in range(2)])
    sq = sbt(ph, [128, 16, 128])
    for gp in range(2):
        vs, ut = VS.get(), UT.get()
        u = unit(W, [(2080 + gp * 256, 256)])
        for t4 in range(4):
            b, t = tm(u, 0, 256, [2 * t4, 2 * t4 + 1])
            tv = AC(C.activation, vs.t[:, 2 * t4:2 * t4 + 2, :, :].rearrange("p a g c -> p (a g c)"), b.t[:, :],
                    ACT.Gelu, w=[t])
            b.w = [tv]
        u.done()
        tv = rms_heads(vs.t[:, :, :, :].rearrange("p a g c -> p (a g) c"), 16, 128, sq[:, :, :],
                       [tv, DV.now()], 1e-6)
        u = unit(W, [(1568 + gp * 256, 256)])
        for g in range(2):
            for th in range(2):
                b, t = fm(u, g * 128, th)
                tu = AC(C.activation, ut.t[:, g, th * 512:th * 512 + 512], b.t[:, :], ACT.Gelu, w=[t])
                b.w = [tu]
        u.done()
        for g in range(2):
            gg = gp * 2 + g
            for th in range(2):
                b = PB.get()
                for j in range(4):
                    t = mms(b.t[:, j * 128:(j + 1) * 128], [(vs.t[:, th * 4 + j, g, :], wsT[:, gg, :])],
                            b.w + [tv, twT], inc=(j == 3))
                mixed = sq[:, 0:4, :]
                t = DV(V.scalar_tensor_tensor, mixed, b.t[:, :].rearrange("p (a c) -> p a c", a=4),
                       pc("sgu_g", gg),
                       bc(bsr[:, gg * 128:(gg + 1) * 128].unsqueeze(1), [128, 4, 128]), MUL, ADD,
                       w=[t, bst, DV.now()])
                b.w = [t]
                o = ut.t[:, g, th * 512:th * 512 + 512]
                t = DV(V.tensor_tensor, o, o, mixed.rearrange("p a c -> p (a c)"), MUL, w=[t, tu])
            r = (4 + gg) * 128
            ysp.append(dma(SP, YM[r:r + 128, :], ut.t[:, g, :], w=[t]))
    fence()
    ph.close()

    ph = ExitStack()
    X = sbt(ph, [128, NT, 1024])
    ph2 = ExitStack()
    stage = Ring([sbt(ph2, [128, S]) for _ in range(8)])
    xt = load_X(X, x_in)
    wt = out_proj(X, A["w_out"][0], [0], xt, stage, {0: ysp})
    norm_HT(X, stage, wt, "g_mlp")
    fence()
    ph2.close()
    ph2 = ExitStack()
    Uh = [sbt(ph2, [128, 2, S], F32R) for _ in range(2)]
    Ul = [sbt(ph2, [128, 2, S], F32R) for _ in range(2)]
    rr = Ring([sbt(ph2, [128, 512]) for _ in range(3)])
    qq = Ring([sbt(ph2, [128, 512]) for _ in range(3)])
    fg, t1 = row_bcast(ph2, A["final_norm_g"])
    eg, t2 = row_bcast(ph2, A["ln_emb_g_2"])
    eb, t3 = row_bcast(ph2, A["ln_emb_b_2"])
    W1, W2 = A["w_mlp1"][0], A["w_mlp2"][0]
    utok, uread = {}, {}

    def up(j):
        u = unit(W1, [(j * 256, 256)])
        toks = []
        for m in range(2):
            for th in range(2):
                sl = slice(th * 512, th * 512 + 512)
                b, t = fm(u, m * 128, th)
                r, q = rr.get(), qq.get()
                t = AC(C.activation, r.t[:, :], b.t[:, :], ACT.Relu, w=[t] + r.w)
                b.w = [t]
                tq = PO(G.tensor_tensor, q.t[:, :], r.t[:, :], r.t[:, :], MUL, w=[t] + q.w)
                th_ = AC(C.activation, Uh[j % 2][:, m, sl], r.t[:, :], ACT.Square, w=[t] + uread.get(j - 2, []))
                tl = DV(V.tensor_tensor, Ul[j % 2][:, m, sl], q.t[:, :], Uh[j % 2][:, m, sl].bitcast(F32), SUB,
                        w=[tq, th_])
                r.w, q.w = [tq, th_], [tl]
                toks += [th_, tl]
        u.done()
        utok[j] = toks

    def down(j):
        u = unit(W2, [(0, 1024)], k0=2 * j, k=2)
        last = []
        for tt in range(NT):
            sl = slice(tt * 128, tt * 128 + 128)
            for nh in range(2):
                cs = slice(nh * 512, nh * 512 + 512)
                b = PD.get()
                pairs = []
                for k in range(2):
                    pairs += three(Uh[j % 2][:, k, sl], Ul[j % 2][:, k, sl], u.h[:, k, cs], u.l[:, k, cs])
                t = mms(b.t[:, :], pairs, b.w + u.w + utok[j])
                t = DV(V.tensor_tensor, X[:, tt, cs], b.t[:, :], X[:, tt, cs], ADD, w=[t])
                b.w = [t]
            last.append([t])
        u.done()
        uread[j] = [PE.now()]
        return last

    up(0)
    for j in range(16):
        if j < 15:
            up(j + 1)
        wt = down(j)

    def ln_stats(X, th, wt):
        mv = st[:, 32:48]
        for tt in range(th * 4, th * 4 + 4):
            t1 = DV(V.bn_stats, ss[:, 0:6], X[:, tt, 0:512], w=list(wt[tt]) + [DV.now()])
            t2 = DV(V.bn_stats, ss[:, 6:12], X[:, tt, 512:1024])
            t3 = DV(V.bn_aggr, mv[:, 2 * tt:2 * tt + 2], ss[:, 0:12], w=[t2])
        var = mv.rearrange("p (t c) -> p t c", c=2)
        sl = slice(th * 4, th * 4 + 4)
        t = DV(V.tensor_scalar, st[:, sl], var[:, sl, 1], 1.0, 1e-5, MUL, ADD, w=[t3])
        return PO(G.tensor_tensor, st[:, sl], st[:, sl], nhalf[:, 0:4], ALU.pow, w=[t])

    def ln_apply(X, gr, br, th, w):
        mv = st[:, 32:48]
        toks = []
        for tt in range(th * 4, th * 4 + 4):
            t1 = DV(V.tensor_scalar, X[:, tt, :], X[:, tt, :], mv[:, 2 * tt:2 * tt + 1], st[:, tt:tt + 1],
                    SUB, MUL, w=w)
            t2 = DV(V.tensor_tensor, X[:, tt, :], X[:, tt, :], gr[:, :], MUL, w=[t1])
            toks.append(PO(G.tensor_tensor, X[:, tt, :], X[:, tt, :], br[:, :], ADD, w=[t2]))
        return toks

    def layernorm(X, gr, br, wt, w):
        a, b = ln_stats(X, 0, wt), ln_stats(X, 1, wt)
        return ln_apply(X, gr, br, 0, [a] + w) + ln_apply(X, gr, br, 1, [b] + w)

    def rms_scale(X, th, r, g, w):
        return [[DV(V.scalar_tensor_tensor, X[:, tt, :], X[:, tt, :], st[:, 16 + tt:17 + tt], g[:, :], MUL, MUL,
                    w=[r] + w)] for tt in range(th * 4, th * 4 + 4)]

    q0 = squares(X, 0, wt)
    q1 = squares(X, 1, wt)
    wt = rms_scale(X, 0, rstd(0, q0), fg, [t1])
    wt += rms_scale(X, 1, rstd(1, q1), fg, [t1])
    if upto == 1:
        stx = store_X(X, out[0], wt)
        ph2.close()
        ph.close()
        finish(nc, ctx, PE, AC, DV, PO, SP, stx)
        return
    toks = layernorm(X, eg, eb, wt, [t2, t3])
    stx = store_X(X, XD, [[x] for x in toks])
    for th in range(2):
        steps(to_HT([X[:, th * 4 + j, :] for j in range(4)], th, toks[th * 4:th * 4 + 4], None))
    fence()
    ph2.close()
    ph.close()
    W = A["w_in_2"][0]
    ph = ExitStack()
    dt_, dA, acs, wd, ea, dcy = (sbt(ph, [128, NT, 32]) for _ in range(6))
    dbr = sbt(ph, [128, 32])
    Ar = sbt(ph, [128, 32])
    Dr = sbt(ph, [128, 16])
    ct = [dma(SP, dbr[:, 0:16], A["dt_bias_fwd_2"][0].partition_broadcast(128)),
          dma(SP, dbr[:, 16:32], A["dt_bias_bwd_2"][0].partition_broadcast(128)),
          dma(SP, Ar[:, 0:16], A["A_log_fwd_2"][0].partition_broadcast(128)),
          dma(SP, Ar[:, 16:32], A["A_log_bwd_2"][0].partition_broadcast(128)),
          dma(SP, Dr[:, :], A["D_skip_2"][0].partition_broadcast(128))]
    XS = [sbt(ph, [128, NT, 256]) for _ in range(2)]
    BC = [[sbt(ph, [128, S]), sbt(ph, [128, S]), sbt(ph, [128, NT, 128])] for _ in range(2)]
    y = sbt(ph, [128, NT, 512])
    PR = [sbt(ph, [128, S + 4])]
    for p in PR:
        PO(G.memset, p[:, 0:2], 0.0)
        t = PO(G.memset, p[:, S + 2:S + 4], 0.0)
    pz = t
    Pad = Ring(PR)
    Acc = Ring([sbt(ph, [128, S]) for _ in range(2)])
    Er = Ring([sbt(ph, [128, 4, 128]) for _ in range(4)])
    Tr = Ring([sbt(ph, [128, 512]) for _ in range(1)])
    Xw = Ring([sbt(ph, [128, 256]) for _ in range(2)])
    Cb = Ring([sbt(ph, [128, 128]) for _ in range(3)])
    Ust, Lst = sbt(ph, [128, 128]), sbt(ph, [128, 128])
    DV(V.tensor_tensor, Ust[:, :], Uinc[:, :], ident[:, :], SUB)
    tstr = DV(V.tensor_tensor, Lst[:, :], Linc[:, :], ident[:, :], SUB)
    St = [sbt(ph, [128, 256]) for _ in range(2)]
    ysp = []
    tX, tB, gone, ytok, tz_ = {}, {}, {}, {}, {}
    h4 = [128, 4, 64]

    def hv(x):
        return x.rearrange("p (h d) -> p h d", h=4)

    small = []
    flat = (lambda x: x[:, :, :].rearrange("p a b -> p (a b)"))

    def ssm_steps():
        u = unit(W, [(2560, 32)])
        b, t = tm(u, 0, 32, list(range(8)))
        u.done()
        yield
        t = DV(V.tensor_tensor, dt_[:, :, :], b.t[:, 0:256].rearrange("p (a b) -> p a b", a=8),
               bc(dbr[:, :].unsqueeze(1), [128, 8, 32]), ADD, w=[t] + ct)
        b.w = [t]
        t1 = AC(C.activation, flat(wd), flat(dt_), ACT.Abs, w=[t])
        t1 = AC(C.activation, flat(wd), flat(wd), ACT.Exp, scale=-1.0, w=[t1])
        yield
        t1 = AC(C.activation, flat(wd), flat(wd), ACT.Ln, bias=1.0, w=[t1])
        tA = AC(C.activation, Ar[:, :], Ar[:, :], ACT.Exp, w=ct)
        t = DV(V.scalar_tensor_tensor, dt_[:, :, :], dt_[:, :, :], 0.0, wd[:, :, :], MAX, ADD, w=[t1])
        t = DV(V.scalar_tensor_tensor, dA[:, :, :], dt_[:, :, :], -1.0, bc(Ar[:, :].unsqueeze(1), [128, 8, 32]),
               MUL, MUL, w=[t, tA])
        yield
        b = PB.get()
        bvv = b.t[:, 0:256].rearrange("p (a b) -> p a b", a=8)
        mms(bvv[:, :, 0:16], [(Uinc[:, :], dA[:, :, 0:16])], b.w + [t], inc=False)
        mms(bvv[:, :, 16:32], [(Linc[:, :], dA[:, :, 16:32])], (), inc=False)
        t = mms(b.t[:, 256:512], [(ones[:, :], flat(dA))], ())
        t1 = DV(V.tensor_copy, acs[:, :, :], bvv, w=[t])
        yield
        t1 = DV(V.tensor_tensor, flat(wd), b.t[:, 256:512], flat(acs), SUB, w=[t1])
        t2 = AC(C.activation, flat(dcy), b.t[:, 256:512], ACT.Exp, w=[t1])
        b.w = [t2, t1]
        t3 = AC(C.activation, flat(wd), flat(wd), ACT.Exp, w=[t1])
        t4_ = AC(C.activation, flat(ea), flat(acs), ACT.Exp, w=[t1])
        tw = DV(V.tensor_tensor, flat(wd), flat(wd), flat(dt_), MUL, w=[t3])
        small.extend([tw, t4_, t2, t1])

    def ssm_dense(i):
        g, half = i // 2, i % 2
        xs, (BT, CT, Bt) = XS[i % 2], BC[g]
        w0 = gone.get(i - 2, [])
        for n in ([1, 0] if half == 0 else [0]):
            if n == 0:
                u = unit(W, [(1024 + i * 256, 256)])
                ms = [2 * i, 2 * i + 1]
            else:
                u = unit(W, [(2048 + g * 128, 128), (2304 + g * 128, 128)])
                ms = [8 + g, 10 + g]
            for mi, m in enumerate(ms):
                p = Pad.get()
                for th in range(2):
                    b, t = fm(u, mi * 128, th)
                    tp = AC(C.copy, p.t[:, 2 + th * 512:2 + th * 512 + 512], b.t[:, :], w=[t, pz] + p.w)
                    b.w = [tp]
                    yield
                a = Acc.get()
                t = AC(C.activation, a.t[:, :], p.t[:, 0:S], ACT.Identity, scale=pc("cw2", m), bias=pc("cb2", m),
                       w=[tp] + a.w)
                for j in range(1, 5):
                    t = DV(V.scalar_tensor_tensor, a.t[:, :], p.t[:, j:j + S], pc("cw2", 12 * j + m), a.t[:, :],
                           MUL, ADD, w=[t])
                    yield
                p.w = [t]
                dst = a.t if m < 8 else (BT if m == 8 + g else CT)
                t = AC(C.activation, dst[:, :], a.t[:, :], ACT.Silu, w=[t] + w0)
                tB.setdefault(g, []).append(t)
                last = t
                if m != 10 + g:
                    for th in range(2):
                        b = PB.get()
                        for j in range(4):
                            tt = th * 4 + j
                            last = PE(T.transpose, b.t[:, j * 128:(j + 1) * 128], dst[:, tt * 128:(tt + 1) * 128],
                                      ident[:, :], w=b.w + [t], inc=(j == 3))
                        o = xs[:, th * 4:th * 4 + 4, (m % 2) * 128:(m % 2) * 128 + 128] if m < 8 else \
                            Bt[:, th * 4:th * 4 + 4, :]
                        t2 = AC(C.copy, o, b.t[:, :].rearrange("p (a c) -> p a c", a=4), w=[last] + w0)
                        b.w = [t2]
                        (tX.setdefault(i, []) if m < 8 else tB[g]).append(t2)
                        yield
                a.w = [last]
            u.done()

    def ssm_skip(i):
        g, half = i // 2, i % 2
        xs = XS[i % 2]
        for tt in range(NT):
            ytok[tt] = PO(G.tensor_tensor, hv(y[:, tt, half * 256:half * 256 + 256]), hv(xs[:, tt, :]),
                          bc(Dr[:, i * 4:i * 4 + 4].unsqueeze(2), h4), MUL, w=tX[i] + [ct[4]] + gone.get("y", []))

    def ssm_scan(i, d):
        g, half = i // 2, i % 2
        xs, (BT, CT, Bt) = XS[i % 2], BC[g]
        S_ = St[d]
        tri, strict = (Uinc, Lst) if d == 0 else (Linc, Ust)
        h0 = d * 16 + i * 4
        hs = slice(h0, h0 + 4)
        order = list(range(8)) if d == 0 else list(range(7, -1, -1))
        ts, tz = None, gone.get("s%d" % d)

        def scaled(tt):
            e = Er.get()
            for j in range(4):
                te = AC(C.mul, e.t[:, j, :], strict[:, :], dA[:, tt, h0 + j:h0 + j + 1], w=small + e.w + [tstr])
            return tt, e, te

        def front(tt, e, te):
            sl = slice(tt * 128, tt * 128 + 128)
            b = PB.get()
            t = mms(b.t[:, 0:128], [(BT[:, sl], CT[:, sl])], b.w + tB[g])
            cb = Cb.get()
            tcb = DV(V.tensor_tensor, cb.t[:, :], b.t[:, 0:128], tri[:, :], MUL, w=[t] + cb.w)
            b.w = [tcb]
            b = PB.get()
            for j in range(4):
                t = mms(b.t[:, j * 128:(j + 1) * 128], [(e.t[:, j, :], tri[:, :])], b.w + [te], inc=(j == 3))
            te = AC(C.activation, e.t[:, :, :], b.t[:, :].rearrange("p (a c) -> p a c", a=4), ACT.Exp, w=[t])
            b.w = [te]
            return tt, cb, tcb, e, te

        pend = front(*scaled(order[0]))
        yield
        for n, tt in enumerate(order):
            _, cb, tcb, e, te = pend
            sl = slice(tt * 128, tt * 128 + 128)
            Y = PD.get()
            if n > 0:
                t = mms(Y.t[:, 256:512], [(CT[:, sl], S_[:, :])], Y.w + [ts] + tB[g], inc=False)
            if n < 7:
                xw = Xw.get()
                txw = PO(G.tensor_tensor, hv(xw.t[:, :]), hv(xs[:, tt, :]), bc(wd[:, tt, hs].unsqueeze(2), h4),
                         MUL, w=tX[i] + small + xw.w)
            for j in range(4):
                tg = DV(V.scalar_tensor_tensor, e.t[:, j, :], e.t[:, j, :], dt_[:, tt, h0 + j:h0 + j + 1],
                        cb.t[:, :], MUL, MUL, w=[te, tcb])
            cb.w = [tg]
            if n < 7:
                nxt = scaled(order[n + 1])
            yield
            if n < 7:
                pend = front(*nxt)
            yield
            for j in range(4):
                t = mms(Y.t[:, j * 64:j * 64 + 64], [(e.t[:, j, :], xs[:, tt, j * 64:j * 64 + 64])],
                        Y.w + [tg] + tX[i], inc=(j == 3))
            tz = [t]
            e.w = [t]
            yv = y[:, tt, half * 256:half * 256 + 256]
            ty = DV(V.tensor_tensor, yv, Y.t[:, 0:256], yv, ADD, w=[t, ytok[tt]])
            if n > 0:
                tr = Tr.get()
                t = DV(V.tensor_tensor, hv(tr.t[:, 0:256]), hv(Y.t[:, 256:512]), bc(ea[:, tt, hs].unsqueeze(2), h4),
                       MUL, w=small + tr.w)
                ty = DV(V.tensor_tensor, yv, yv, tr.t[:, 0:256], ADD, w=[t, ty])
                tr.w = [ty]
                Y.w = [t]
            else:
                Y.w = [ty]
            ytok[tt] = ty
            yield
            if n < 7:
                b = PB.get()
                t = mms(b.t[:, 0:256], [(Bt[:, tt, :], xw.t[:, :])], b.w + [txw] + tB[g])
                xw.w = [t]
                if n == 0:
                    ts = DV(V.tensor_copy, S_[:, :], b.t[:, 0:256], w=[t] + (tz if tz else []))
                else:
                    t1 = DV(V.tensor_tensor, hv(S_[:, :]), hv(S_[:, :]), bc(dcy[:, tt, hs].unsqueeze(2), h4),
                            MUL, w=tz + [ts])
                    ts = DV(V.tensor_tensor, S_[:, :], b.t[:, 0:256], S_[:, :], ADD, w=[t, t1])
                b.w = [ts]
            yield

    def ssm_gate(i):
        u = unit(W, [(i * 256, 256)])
        for n in range(2):
            a = Acc.get()
            for th in range(2):
                t4 = 2 * n + th
                b, t = tm(u, 0, 256, [2 * t4, 2 * t4 + 1])
                t = AC(C.activation, a.t[:, th * 512:th * 512 + 512], b.t[:, :], ACT.Silu, w=[t] + a.w)
                b.w = [t]
                if th == 1:
                    tz_[i, n] = dma(SP, ZS[i * 2 + n], a.t[:, :], w=[t])
                    a.w = [tz_[i, n]]
                yield
        u.done()

    def ssm_fetch(i):
        for n in range(2):
            a = Acc.get()
            tz_[i, n] = a, dma(SP, a.t[:, :], ZS[i * 2 + n], w=a.w + [tz_[i, n]])

    def ssm_mul(i):
        half = i % 2
        for n in range(2):
            a, td = tz_[i, n]
            o = y[:, 4 * n:4 * n + 4, half * 256:(half + 1) * 256]
            t = DV(V.tensor_tensor, o, o, a.t[:, :].rearrange("p (a c) -> p a c", a=4), MUL,
                   w=[td] + [ytok[4 * n + j] for j in range(4)])
            for j in range(4):
                ytok[4 * n + j] = t
            a.w = [t]

    def ssm_out(g):
        for tt in range(8):
            tr = Tr.get()
            t = AC(C.activation, tr.t[:, :], y[:, tt, :], ACT.Square, accum_out=ss[:, tt:tt + 1],
                   w=[ytok[tt]] + tr.w)
            tr.w = [t]
        t = rsqrt(st[:, 0:8], ss[:, 0:8], 1.0 / 512, 1e-5, [t])
        t = DV(V.tensor_tensor, y[:, :, :], y[:, :, :], bc(st[:, 0:8].unsqueeze(2), [128, 8, 512]), MUL, w=[t])
        for m in range(4):
            a = Acc.get()
            for th in range(2):
                b = PB.get()
                for j in range(4):
                    t_ = PE(T.transpose, b.t[:, j * 128:(j + 1) * 128], y[:, th * 4 + j, m * 128:(m + 1) * 128],
                            ident[:, :], w=b.w + [t], inc=(j == 3))
                ty = AC(C.mul, a.t[:, th * 512:th * 512 + 512], b.t[:, :], pc("ssm_g", g * 4 + m), w=[t_] + a.w)
                b.w = [ty]
            r = (g * 4 + m) * 128
            ysp.append(dma(SP, YM[r:r + 128, :], a.t[:, :], w=[ty]))
            a.w = [ysp[-1]]
            yield
        gone["y"] = [PE.now()]

    def ssm_side(i):
        if i != 1:
            yield from ssm_gate(i)
        if i < 3:
            yield from ssm_dense(i + 1)
        if i == 0:
            yield from ssm_gate(1)
        ssm_fetch(i)

    weave((ssm_steps(), 30), (ssm_dense(0), 30))
    for i in range(4):
        ssm_skip(i)
        parts = [(ssm_scan(i, 0), 33), (ssm_scan(i, 1), 33)]
        parts.append((ssm_side(i), [24, 26, 20, 4][i]))
        weave(*parts)
        ssm_mul(i)
        gone[i] = [PE.now(), DV.now(), PO.now()]
        if i % 2 == 1:
            steps(ssm_out(i // 2))
            gone[i] = [PE.now(), DV.now(), PO.now()]
    fence()
    ph.close()

    ph = ExitStack()
    WD = 1920
    bias = sbt(ph, [128, WD])
    HB = [[sbt(ph, [128, S]) for _ in range(3)] + [sbt(ph, [128, NT, 128])] for _ in range(2)]
    vT = sbt(ph, [128, S])
    SR = Ring([sbt(ph, [128, 2, S]) for _ in range(3)])
    WT = Ring([sbt(ph, [128, 8, 512])])
    tmp = Ring([sbt(ph, [128, 512]) for _ in range(2)])
    sm = Ring([sbt(ph, [128, 8]) for _ in range(4)])
    o128 = sbt(ph, [128, 128])
    epsc = sbt(ph, [128, 1])
    to128 = DV(V.memset, o128[:, :], 1.0 / 128)
    teps = DV(V.memset, epsc[:, :], 1e-5)
    PQ = [Slot(PQt[0]), Slot(PQt[1])]
    t = PO(G.iota, bias[:, :], pattern=[[-1, WD]], base=896, channel_multiplier=1,
           allow_small_or_imprecise_dtypes=True)
    tbias = [AC(C.activation, bias[:, :], bias[:, :], ACT.Abs, w=[t])]
    tD, hgone = {}, {}

    def att_dense(h):
        qT, kT, gT, vt = HB[h % 2]
        w0 = hgone.get(h - 2, [])
        u = unit(W, [(2592 + h * 128, 128), (3616 + h * 128, 128)])
        tD[h] = []
        for m, dst in enumerate((qT, kT)):
            for th in range(2):
                b, t = fm(u, m * 128, th)
                t = AC(C.copy, dst[:, th * 512:th * 512 + 512], b.t[:, :], w=[t] + w0)
                b.w = [t]
                tD[h].append(t)
                yield
        u.done()
        u = unit(W, [(4640 + h * 128, 128), (5664 + h * 128, 128)])
        for th in range(2):
            b, t = fm(u, 0, th)
            t = AC(C.copy, vT[:, th * 512:th * 512 + 512], b.t[:, :], w=[t] + hgone.get("vT", []))
            b.w = [t]
            yield
        for th in range(2):
            b = PD.get()
            for j in range(4):
                tt = th * 4 + j
                t_ = PE(T.transpose, b.t[:, j * 128:(j + 1) * 128], vT[:, tt * 128:(tt + 1) * 128],
                        ident[:, :], w=b.w + [t], inc=(j == 3))
            t2 = AC(C.copy, vt[:, th * 4:th * 4 + 4, :], b.t[:, :].rearrange("p (a c) -> p a c", a=4), w=[t_] + w0)
            b.w = [t2]
            tD[h].append(t2)
            yield
        hgone["vT"] = [t_]
        for th in range(2):
            b, t = fm(u, 128, th)
            t = AC(C.activation, gT[:, th * 512:th * 512 + 512], b.t[:, :], ACT.Silu, w=[t] + w0)
            b.w = [t]
            tD[h].append(t)
            yield
        u.done()

    def att(h):
        qT, kT, gT, vt = HB[h % 2]
        tbias[0] = AC(C.mul, bias[:, :], bias[:, :], -4.0 if h == 0 else 0.5, w=[tbias[0], DV.now()])
        tb = tbias[0]

        def scores(tt):
            s, x = SR.get(), sm.get()
            qk = []
            for sh in range(2):
                for r in range(2):
                    rows = slice(64 * r, 64 * r + 64)
                    qk.append(mms(PQ[r].t[:, sh * 512:sh * 512 + 512],
                                  [(qT[rows, tt * 128:tt * 128 + 128], kT[rows, sh * 512:sh * 512 + 512])],
                                  PQ[r].w + tD[h]))
            for r in range(2):
                t = DV(V.tensor_tensor_reduce, out=s.t[:, r, :], in0=PQ[r].t[:, :],
                       in1=bias[:, 896 - 128 * tt:896 - 128 * tt + 1024], scale=0.125, scalar=-3.0e38,
                       op0=ADD, op1=MAX, accum_out=x.t[:, r:r + 1], w=[qk[2 + r], tb] + s.w + x.w)
                PQ[r].w = [t]
            t = DV(V.tensor_scalar, x.t[:, 2:4], x.t[:, 0:2], -1.0, None, MUL, w=[t])
            for r in range(2):
                t2 = AC(C.activation, s.t[:, r, :], s.t[:, r, :], ACT.Exp, bias=x.t[:, 2 + r:3 + r],
                        accum_out=x.t[:, 4 + r:5 + r], w=[t])
            return tt, s, x, t2

        def mixed(tt, s, x, t2):
            t = DV(V.reciprocal, x.t[:, 6:8], x.t[:, 4:6], w=[t2])
            t0 = AC(C.mul, s.t[:, 0, :], s.t[:, 0, :], x.t[:, 6:7], w=[t])
            t = DV(V.tensor_tensor, x.t[:, 5:6], x.t[:, 7:8], lam[:, 3:4], MUL, w=[t])
            t = DV(V.scalar_tensor_tensor, s.t[:, 0, :], s.t[:, 1, :], x.t[:, 5:6], s.t[:, 0, :], MUL, ADD,
                   w=[t, t0])
            x.w = [t]
            return t

        wt, wtoks = None, []
        pend = [scores(0)]
        yield
        pend.append(scores(1))
        yield
        for tt in range(NT):
            if tt % 4 == 0:
                wt, wtoks = WT.get(), []
            _, s, x, t2 = pend[0]
            t = mixed(*pend.pop(0))
            yield
            if tt < 6:
                pend.append(scores(tt + 2))
            yield
            for q2 in range(2):
                b = PD.get()
                for j in range(4):
                    t_ = PE(T.transpose, b.t[:, j * 128:(j + 1) * 128],
                            s.t[:, 0, (q2 * 4 + j) * 128:(q2 * 4 + j + 1) * 128], ident[:, :], w=b.w + [t],
                            inc=(j == 3))
                o = wt.t[:, q2 * 4:q2 * 4 + 4, (tt % 4) * 128:(tt % 4) * 128 + 128]
                i_ = b.t[:, :].rearrange("p (a c) -> p a c", a=4)
                if q2 == 0:
                    t2 = AC(C.copy, o, i_, w=[t_] + wt.w)
                else:
                    t2 = DV(V.tensor_copy, o, i_, w=[t_] + wt.w)
                b.w = [t2]
                wtoks.append(t2)
            s.w = [t_]
            yield
            if tt % 4 == 3:
                th = tt // 4
                sl = slice(th * 512, th * 512 + 512)
                b = PD.get()
                t_ = mms(b.t[:, :], [(vt[:, j, :], wt.t[:, j, :]) for j in range(8)], b.w + wtoks + tD[h])
                wt.w = [t_]
                o, q = tmp.get(), tmp.get()
                t1 = AC(C.copy, o.t[:, :], b.t[:, :], w=[t_] + o.w)
                t2 = AC(C.activation, q.t[:, :], b.t[:, :], ACT.Square, w=[t_] + q.w)
                b.w = [t2]
                b = PD.get()
                t2 = mms(b.t[:, :], [(o128[:, :], q.t[:, :])], b.w + [t2, to128])
                t2 = AC(C.activation, q.t[:, :], b.t[:, :], ACT.Ln, bias=epsc[:, 0:1], w=[t2, teps])
                b.w = [t2]
                t2 = AC(C.activation, q.t[:, :], q.t[:, :], ACT.Exp, scale=-0.5, w=[t2])
                gs = gT[:, sl]
                t1 = DV(V.scalar_tensor_tensor, gs, o.t[:, :], pc("subln"), gs, MUL, MUL, w=[t1] + tD[h])
                ty = DV(V.tensor_tensor, gs, gs, q.t[:, :], MUL, w=[t1, t2])
                o.w, q.w = [t1], [ty]
                r = (8 + h) * 128
                ysp.append(dma(SP, YM[r:r + 128, sl], gs, w=[ty]))
                yield
        hgone[h] = [PE.now(), DV.now()] + ysp[-2:]

    steps(att_dense(0))
    for h in range(8):
        if h < 7:
            weave((att(h), 27), (att_dense(h + 1), 10))
        else:
            steps(att(h))
    fence()
    ph.close()

    ph = ExitStack()
    X = sbt(ph, [128, NT, 1024])
    phs = ExitStack()
    stage = Ring([sbt(phs, [128, S]) for _ in range(8)])
    xt = load_X(X, XD)
    wX = []
    for tt in range(NT):
        wX.append(AC(C.mul, X[:, tt, :], X[:, tt, :], ALPHA, w=[xt[tt]] + stx))
    gr, t1 = row_bcast(phs, A["ln_g_2"][0])
    br, t2 = row_bcast(phs, A["ln_b_2"][0])
    wt = out_proj(X, A["w_out_2"][0], [0, 1], wX[-1:], stage, {0: ysp, 1: ysp})
    toks = layernorm(X, gr, br, wt, [t1, t2])
    if upto == 2:
        stx = store_X(X, out[0], [[x] for x in toks])
        phs.close()
        ph.close()
        finish(nc, ctx, PE, AC, DV, PO, SP, stx)
        return
    stx = store_X(X, XD, [[x] for x in toks])
    norm_HT(X, stage, [[x] for x in toks], "g3")
    fence()
    phs.close()
    ph.close()
    W = A["w_in_3"][0]
    ph = ExitStack()
    PR = [sbt(ph, [128, S + 30]) for _ in range(2)]
    for p in PR:
        pz = PO(G.memset, p[:, 0:30], 0.0)
    Pad = Ring(PR)
    Acc = Ring([sbt(ph, [128, S]) for _ in range(2)])
    Sg_ = Ring([sbt(ph, [128, S]) for _ in range(6)])
    o128 = sbt(ph, [128, 128])
    to128 = DV(V.memset, o128[:, :], 1.0 / 128)
    eps = sbt(ph, [128, 1])
    teps = DV(V.memset, eps[:, :], 1e-6)
    ycs = []

    def taps(k, g):
        return pc("cw3a", 8 * k + g) if k < 16 else pc("cw3b", 8 * (k - 16) + g)

    cin, cacc = {}, {}

    def conv_dense(g):
        u = unit(W, [(g * 128, 128), (1024 + g * 128, 128)])
        p, sg = Pad.get(), Sg_.get()
        for th in range(2):
            sl = slice(th * 512, th * 512 + 512)
            b1, t1 = fm(u, 128, th)
            t1 = AC(C.activation, sg.t[:, sl], b1.t[:, :], ACT.Sigmoid, w=[t1] + sg.w)
            b1.w = [t1]
            yield
            b2, t2 = fm(u, 0, th)
            tp = DV(V.tensor_tensor, p.t[:, 30 + th * 512:30 + th * 512 + 512], b2.t[:, :], sg.t[:, sl], MUL,
                    w=[t2, t1, pz] + p.w)
            b2.w = [tp]
            yield
        u.done()
        sg.w = [tp]
        cin[g] = (p, tp)

    def conv_light(g):
        p, tp = cin[g]
        a = Acc.get()
        t = AC(C.activation, a.t[:, :], p.t[:, 0:S], ACT.Identity, scale=taps(0, g), bias=pc("cb3", g),
               w=[tp] + a.w)
        for k in range(1, 31):
            t = DV(V.scalar_tensor_tensor, a.t[:, :], p.t[:, k:k + S], taps(k, g), a.t[:, :], MUL, ADD, w=[t])
            yield
        p.w = [t]
        cacc[g] = (a, t)

    def conv_tail(g):
        a, t = cacc[g]
        sg = Sg_.get()
        yield
        for th in range(2):
            sl = slice(th * 512, th * 512 + 512)
            b = PB.get()
            t1 = mms(b.t[:, :], [(o128[:, :], a.t[:, sl])], b.w + [t, to128])
            t1 = DV(V.tensor_tensor, a.t[:, sl], a.t[:, sl], b.t[:, :], SUB, w=[t1])
            b.w = [t1]
            yield
            t2 = AC(C.activation, sg.t[:, sl], a.t[:, sl], ACT.Square, w=[t1] + sg.w)
            b = PB.get()
            t2 = mms(b.t[:, :], [(o128[:, :], sg.t[:, sl])], b.w + [t2])
            t2 = AC(C.activation, sg.t[:, sl], b.t[:, :], ACT.Ln, bias=eps[:, 0:1], w=[t2, teps])
            b.w = [t2]
            t2 = AC(C.activation, sg.t[:, sl], sg.t[:, sl], ACT.Exp, scale=-0.5, w=[t2])
            yield
            t1 = DV(V.tensor_tensor, a.t[:, sl], a.t[:, sl], sg.t[:, sl], MUL, w=[t1, t2])
            yield
            t1 = AC(C.activation, sg.t[:, sl], a.t[:, sl], ACT.Silu, scale=pc("cng", g), bias=pc("cnb", g), w=[t1])
            yield
        a.w = [t1]
        ycs.append(dma(SP, YC[g * 128:(g + 1) * 128, :], sg.t[:, :], w=[t1]))
        sg.w = [ycs[-1]]

    zgs = []

    def gate_dense(n):
        u = unit(W, [(2048 + n * 256, 256)])
        for m in range(2):
            sg = Sg_.get()
            for th in range(2):
                b, t = fm(u, m * 128, th)
                t = AC(C.activation, sg.t[:, th * 512:th * 512 + 512], b.t[:, :], ACT.Silu, w=[t] + sg.w)
                b.w = [t]
                yield
            r = (n * 2 + m) * 128
            zgs.append(dma(SP, ZG[r:r + 128, :], sg.t[:, :], w=[t]))
            sg.w = [zgs[-1]]
        u.done()

    def conv_side(g):
        if g % 2 == 1:
            yield from gate_dense(g // 2)
        if g < 7:
            yield from conv_dense(g + 1)

    steps(conv_dense(0))
    for g in range(8):
        parts = [(conv_light(g), 31), (conv_side(g), 8 if g % 2 else 4)]
        if g > 0:
            parts.append((conv_tail(g - 1), 11))
        weave(*parts)
    steps(conv_tail(7))
    fence()
    ph.close()

    ph = ExitStack()
    M128 = sbt(ph, [128, S])
    lb, lb1 = sbt(ph, [128, 8]), sbt(ph, [128, 8])
    Mi = sbt(ph, [128, 8, 128], I32)
    Mf = sbt(ph, [128, 128])
    t = PO(G.memset, M128[:, :], 1.0)
    tM = PO(G.memset, M128[:, :].rearrange("p (c t) -> p c t", t=128)[:, :, 0:1], 0.0, w=[t])
    LV = [64, 32, 16, 8, 4, 2, 1]
    tm_ = []
    for l, w_ in enumerate(LV):
        nb = 64 // w_
        mfv = Mf[:, :].rearrange("p (b h t) -> p b h t", b=nb, h=2)
        t = PO(G.memset, Mf[:, :], 0.0, w=[DV.now(), PO.now()])
        t = PO(G.memset, mfv[:, :, 1, :], 1.0, w=[t])
        t = PO(G.affine_select, out=Mf[:, :], in_=Mf[:, :], compare_op=ALU.is_ge, fill=0.0, base=0,
               pattern=[[-2 * w_, nb], [0, 2 * w_]], channel_multiplier=1, w=[t])
        t = PO(G.affine_select, out=Mf[:, :], in_=Mf[:, :], compare_op=ALU.is_ge, fill=0.0, base=w_ - 1,
               pattern=[[2 * w_, nb], [0, 2 * w_]], channel_multiplier=-1, w=[t])
        tMi = DV(V.tensor_copy, Mi[:, l, :], Mf[:, :], w=[t])
    tMi = DV(V.tensor_copy, Mi[:, 7, :], ident[:, :])
    l0 = PC[:, col["lb0"]:col["lb0"] + 8]
    l1 = PC[:, col["lb1"]:col["lb1"] + 8]
    t = DV(V.tensor_tensor, lb1[:, :], l0, l1, MAX)
    t = DV(V.tensor_tensor, lb[:, :], l0, lb1[:, :], SUB, w=[t])
    t = DV(V.tensor_tensor, lb1[:, :], l1, lb1[:, :], SUB, w=[t])
    t = AC(C.activation, lb[:, :], lb[:, :], ACT.Exp, w=[t])
    t = AC(C.activation, lb1[:, :], lb1[:, :], ACT.Exp, w=[t])
    t = DV(V.tensor_tensor, lb1[:, :], lb[:, :], lb1[:, :], ADD, w=[t])
    t = DV(V.reciprocal, lb1[:, :], lb1[:, :], w=[t])
    t = DV(V.tensor_tensor, lb[:, :], lb[:, :], lb1[:, :], MUL, w=[t])
    tlb = DV(V.tensor_scalar, lb1[:, :], lb[:, :], -1.0, 1.0, MUL, ADD, w=[t])
    HB = [[sbt(ph, [128, S]) for _ in range(4)] + [sbt(ph, [128, NT, 128])] for _ in range(2)]
    vT = sbt(ph, [128, S])
    Dr_ = Ring([sbt(ph, [128, S]) for _ in range(3)])
    Zr = Ring([sbt(ph, [128, S]) for _ in range(3)])
    At = sbt(ph, [128, NT, 128])
    tAz = PO(G.memset, At[:, :, :], 0.0)
    kdt = sbt(ph, [128, NT, 128])
    O = sbt(ph, [128, NT, 128])
    Sr = Ring([sbt(ph, [128, 128]) for _ in range(2)])
    dec = sbt(ph, [128, 8])
    yh = []
    tD, hgone = {}, {}

    def rec_dense(h):
        qT, kT, bT, gT, vt = HB[h % 2]
        w0 = hgone.get(h - 2, [])
        tD[h] = []
        u = unit(W, [(4096 + h * 128, 128), (3072 + h * 128, 128)])
        for th in range(2):
            sl = slice(th * 512, th * 512 + 512)
            b, t = fm(u, 0, th)
            tf = AC(C.activation, bT[:, sl], b.t[:, :], ACT.Sigmoid, w=[t] + w0)
            tk = AC(C.activation, kT[:, sl], b.t[:, :], ACT.Sigmoid, scale=-1.0, w=[t] + w0)
            b.w = [tk]
            yield
        for th in range(2):
            b, t = fm(u, 128, th)
            tq = AC(C.activation, qT[:, th * 512:th * 512 + 512], b.t[:, :], ACT.Silu, w=[t] + w0)
            b.w = [tq]
            yield
        u.done()
        u = unit(W, [(5120 + h * 128, 128), (6144 + h * 128, 128)])
        for th in range(2):
            b, t = fm(u, 128, th)
            tq = AC(C.activation, gT[:, th * 512:th * 512 + 512], b.t[:, :], ACT.Silu, w=[t] + w0)
            b.w = [tq]
            yield
        for th in range(2):
            b, t = fm(u, 0, th)
            t = AC(C.copy, vT[:, th * 512:th * 512 + 512], b.t[:, :], w=[t] + hgone.get("vT", []))
            b.w = [t]
            yield
        u.done()
        for th in range(2):
            b = PD.get()
            for j in range(4):
                tt = th * 4 + j
                t_ = PE(T.transpose, b.t[:, j * 128:(j + 1) * 128], vT[:, tt * 128:(tt + 1) * 128],
                        ident[:, :], w=b.w + [t], inc=(j == 3))
            tv = AC(C.copy, vt[:, th * 4:th * 4 + 4, :], b.t[:, :].rearrange("p (a c) -> p a c", a=4),
                    w=[t_] + w0)
            b.w = [tv]
            yield
        hgone["vT"] = [t_]
        tD[h] = [tv]

    def rec(h):
        q, k, bb, gT, v = HB[h % 2]
        q, k, bb = q[:, :], k[:, :], bb[:, :]
        td = tD[h]
        ow = hgone.get(h - 1, [])
        t = DV(V.tensor_scalar, bb, bb, lb1[:, h:h + 1], lb[:, h:h + 1], MUL, ADD, w=td + [tlb])
        tk2 = DV(V.tensor_scalar, k, k, lb1[:, h:h + 1], None, MUL)
        dd = Dr_.get()
        t = DV(V.tensor_scalar, bb, bb, 2.0 ** -63, None, MAX, w=[t])
        t = AC(C.activation, dd.t[:, :], bb, ACT.Ln, w=[t] + dd.w)
        tb = DV(V.tensor_tensor_scan, bb, M128[:, :], dd.t[:, :], 0.0, op0=MUL, op1=ADD, w=[t, tM])
        dd.w = [tb]
        yield
        tAs = [tAz, tAz]

        def front(l):
            if l == 7:
                return None, tk2
            w_ = LV[l]
            nb = S // (2 * w_)
            dd, z = Dr_.get(), Zr.get()

            def v4(x):
                return x.rearrange("p (b h t) -> p b h t", h=2, t=w_)
            ref = v4(bb)[:, :, 0, w_ - 1:w_]
            DV(V.tensor_tensor, v4(dd.t[:, :])[:, :, 0, :], bc(ref, [128, nb, w_]), v4(bb)[:, :, 0, :],
               SUB, w=[tb] + dd.w)
            t1 = DV(V.tensor_tensor, v4(dd.t[:, :])[:, :, 1, :], v4(bb)[:, :, 1, :], bc(ref, [128, nb, w_]), SUB)
            t1 = AC(C.activation, dd.t[:, :], dd.t[:, :], ACT.Exp, w=[t1])
            t2 = PO(G.tensor_tensor, v4(z.t[:, :])[:, :, 0, :], v4(k)[:, :, 0, :],
                    v4(dd.t[:, :])[:, :, 0, :], MUL, w=[t1, tk2] + z.w)
            t2 = PO(G.tensor_tensor, v4(z.t[:, :])[:, :, 1, :], v4(q)[:, :, 1, :],
                    v4(dd.t[:, :])[:, :, 1, :], MUL)
            dd.w = [t2]
            return z, t2

        def back(l, z, tz):
            for th in range(2):
                b = PB.get()
                for j in range(4):
                    sl = slice((th * 4 + j) * 128, (th * 4 + j) * 128 + 128)
                    l_, r_ = (z.t[:, sl], z.t[:, sl]) if l < 7 else (k[:, sl], q[:, sl])
                    t = mms(b.t[:, j * 128:(j + 1) * 128], [(l_, r_)], b.w + [tz] + td, inc=(j == 3))
                tAs[th] = DV(V.copy_predicated, At[:, th * 4:th * 4 + 4, :],
                             bc(Mi[:, l:l + 1, :], [128, 4, 128]),
                             b.t[:, :].rearrange("p (a c) -> p a c", a=4), w=[t, tMi, tAs[th]] + ow)
                b.w = [tAs[th]]
                yield
            if l < 7:
                z.w = [t]

        pend = [front(7), front(0)]
        yield
        for l in range(8):
            if l < 6:
                pend.append(front(l + 1))
            yield
            yield from back((l + 7) % 8, *pend.pop(0))
        bv = bb.rearrange("p (c t) -> p c t", t=128)
        dd = Dr_.get()
        t1 = DV(V.tensor_tensor, dd.t[:, :].rearrange("p (c t) -> p c t", t=128),
                bc(bv[:, :, 127:128], [128, 8, 128]), bv, SUB, w=[tb] + dd.w)
        t1 = AC(C.activation, dd.t[:, :], dd.t[:, :], ACT.Exp, w=[t1])
        tkd = DV(V.tensor_tensor, dd.t[:, :], k, dd.t[:, :], MUL, w=[t1, tk2])
        tdec = AC(C.activation, dec[:, :], bv[:, :, 127], ACT.Exp, w=[tkd])
        z = Zr.get()
        t1 = AC(C.activation, z.t[:, :], bb, ACT.Exp, w=[tb] + z.w)
        tqx = DV(V.tensor_tensor, z.t[:, :], q, z.t[:, :], MUL, w=[t1])
        yield
        for th in range(2):
            b = PB.get()
            for j in range(4):
                tt = th * 4 + j
                t = PE(T.transpose, b.t[:, j * 128:(j + 1) * 128], dd.t[:, tt * 128:(tt + 1) * 128],
                       ident[:, :], w=b.w + [tkd], inc=(j == 3))
            tkt = AC(C.copy, kdt[:, th * 4:th * 4 + 4, :], b.t[:, :].rearrange("p (a c) -> p a c", a=4), w=[t])
            b.w = [tkt]
            yield
        dd.w = [t]
        so = None
        for th in range(2):
            kvb = PB.get()
            for j in range(4):
                tt = th * 4 + j
                tkv = mms(kvb.t[:, j * 128:(j + 1) * 128], [(kdt[:, tt, :], v[:, tt, :])],
                          kvb.w + [tkt] + td, inc=(j == 3))
            ob = PB.get()
            for j in range(4):
                tt = th * 4 + j
                o = ob.t[:, j * 128:(j + 1) * 128]
                t = mms(o, [(At[:, tt, :], v[:, tt, :])] +
                        ([(z.t[:, tt * 128:(tt + 1) * 128], so.t[:, :])] if so else []),
                        ob.w + tAs + td + [tqx] + ([tso] if so else []))
                if tt < 7:
                    kv = kvb.t[:, j * 128:(j + 1) * 128]
                    sn = Sr.get()
                    if so is None:
                        tso = DV(V.tensor_copy, sn.t[:, :], kv, w=[tkv] + sn.w)
                    else:
                        tso = DV(V.scalar_tensor_tensor, sn.t[:, :], so.t[:, :], dec[:, tt:tt + 1], kv, MUL,
                                 ADD, w=[tkv, tso, tdec] + sn.w)
                        so.w = [t, tso]
                    so = sn
                else:
                    so.w = [t]
                if j < 3:
                    yield
            kvb.w = [tso]
            to = AC(C.copy, O[:, th * 4:th * 4 + 4, :], ob.t[:, :].rearrange("p (a c) -> p a c", a=4),
                    w=[t] + hgone.get("O", []))
            ob.w = [to]
            yield
        z.w = [t]
        hgone[h] = [t]
        s = Dr_.get()
        t = rms_heads(O[:, :, :], 8, 128, s.t[:, :].rearrange("p (a c) -> p a c", a=8), [to] + s.w, 1e-6)
        s.w = [t]
        yield
        for th in range(2):
            b = PB.get()
            for j in range(4):
                t_ = PE(T.transpose, b.t[:, j * 128:(j + 1) * 128], O[:, th * 4 + j, :], ident[:, :],
                        w=b.w + [t], inc=(j == 3))
            gs = gT[:, th * 512:th * 512 + 512]
            ty = DV(V.scalar_tensor_tensor, gs, b.t[:, :], pc("ong", h), gs, MUL, MUL, w=[t_])
            b.w = [ty]
            yield
        hgone["O"] = [t_]
        r = (8 + h) * 128
        yh.append(dma(SP, YM[r:r + 128, :], gT[:, :], w=[ty]))
        hgone[h] = [PE.now(), AC.now(), DV.now(), PO.now()] + yh[-1:]

    steps(rec_dense(0))
    for h in range(8):
        if h < 7:
            weave((rec(h), 42), (rec_dense(h + 1), 10))
        else:
            steps(rec(h))
    fence()
    ph.close()

    ph = ExitStack()
    X = sbt(ph, [128, NT, 1024])
    ph3 = ExitStack()
    stage = Ring([sbt(ph3, [128, S]) for _ in range(8)])
    gst = Ring([sbt(ph3, [128, S]) for _ in range(3)])
    xt = load_X(X, XD)
    for k in range(8):
        s = stage.get()
        td = dma(SP, s.t[:, :], YC[k * 128:(k + 1) * 128, :], w=s.w + ycs)
        t1 = AC(C.activation, HTh[:, k, :], s.t[:, :], ACT.Copy, w=[td])
        t2 = DV(V.tensor_tensor, HTl[:, k, :], s.t[:, :], HTh[:, k, :].bitcast(F32), SUB, w=[t1, td])
        s.w = [t1, t2]
    HT.w = [t1, t2]
    yc2 = []
    for n in range(4):
        u = unit(A["w_pw2_3"][0], [(n * 256, 256)])
        for m in range(2):
            r = (n * 2 + m) * 128
            g_ = gst.get()
            td = dma(SP, g_.t[:, :], ZG[r:r + 128, :], w=g_.w + zgs)
            for th in range(2):
                b, t = fm(u, m * 128, th)
                o = g_.t[:, th * 512:th * 512 + 512]
                t = DV(V.scalar_tensor_tensor, o, b.t[:, :], pc("bpw", n * 2 + m), o, ADD, MUL, w=[t, td])
                b.w = [t]
            yc2.append(dma(SP, YM[r:r + 128, :], g_.t[:, :], w=[t]))
            g_.w = [yc2[-1]]
        u.done()
    wt = out_proj(X, A["w_out_3"][0], [1, 0], xt, stage, {1: yh, 0: yc2})
    norm_HT(X, stage, wt, "peg")
    fence()
    ph3.close()
    ph2 = ExitStack()
    pin = sbt(ph2, [128, NT, 256])
    Ph = sbt(ph2, [128, 2, S], F32R)
    Pl = sbt(ph2, [128, 2, S], F32R)
    gtr = Ring([sbt(ph2, [128, 512]) for _ in range(8)])
    fg, t1f = row_bcast(ph2, A["final_g_3"])
    tp = dma(SP, pin[:, :, :], A["p_3"][0, 0].rearrange("(t p) d -> p t d", p=128))
    for k in range(2):
        for th in range(2):
            b = PB.get()
            for j in range(4):
                t = PE(T.transpose, b.t[:, j * 128:(j + 1) * 128], pin[:, th * 4 + j, k * 128:(k + 1) * 128],
                       ident[:, :], w=b.w + [tp], inc=(j == 3))
            sl = slice(th * 512, th * 512 + 512)
            t1 = AC(C.activation, Ph[:, k, sl], b.t[:, :], ACT.Copy, w=[t])
            tP = DV(V.tensor_tensor, Pl[:, k, sl], b.t[:, :], Ph[:, k, sl].bitcast(F32), SUB, w=[t1])
            b.w = [t1, tP]
    for n in range(4):
        u = unit(A["w_pg_3"][0], [(n * 256, 256)])
        gts = []
        for t4 in range(4):
            b, t = tm(u, 0, 256, [2 * t4, 2 * t4 + 1])
            gt = gtr.get()
            t = AC(C.activation, gt.t[:, :], b.t[:, :], ACT.Sigmoid, w=[t] + gt.w)
            b.w = [t]
            gts.append((gt, t))
        u.done()
        u = unit(A["w_pp_3"][0], [(n * 256, 256)], k=2)
        for t4 in range(4):
            gt, tg = gts[t4]
            b = PD.get()
            for j in range(2):
                sl = slice((2 * t4 + j) * 128, (2 * t4 + j) * 128 + 128)
                pairs = []
                for k in range(2):
                    pairs += three(Ph[:, k, sl], Pl[:, k, sl], u.h[:, k, :], u.l[:, k, :])
                t = mms(b.t[:, j * 256:(j + 1) * 256], pairs, b.w + u.w + [tP], inc=(j == 1))
            t = DV(V.tensor_tensor, gt.t[:, :], b.t[:, :], gt.t[:, :], MUL, w=[t, tg])
            b.w = [t]
            o = X[:, 2 * t4:2 * t4 + 2, n * 256:(n + 1) * 256]
            t = PO(G.tensor_tensor, o, o, gt.t[:, :].rearrange("p (a c) -> p a c", a=2), ADD, w=[t])
            gt.w = [t]
            wt[2 * t4] = wt[2 * t4 + 1] = [t]
        u.done()
    q0 = squares(X, 0, wt)
    q1 = squares(X, 1, wt)
    toks = rms_scale(X, 0, rstd(0, q0), fg, [t1f])
    toks += rms_scale(X, 1, rstd(1, q1), fg, [t1f])
    stx = store_X(X, out[0], toks)
    ph2.close()
    ph.close()
    finish(nc, ctx, PE, AC, DV, PO, SP, stx)


def finish(nc, ctx, PE, AC, DV, PO, SP, last):
    SP.later(lambda wait: wait(last))
    block = ctx.enter_context(nc.Block())

    @block.sync
    def _(e):
        SP.emit(e)

    @block.tensor
    def _(e):
        PE.emit(e)

    @block.vector
    def _(e):
        DV.emit(e)

    @block.scalar
    def _(e):
        AC.emit(e)

    @block.gpsimd
    def _(e):
        PO.emit(e)


_INS = [
    "x", "norm_mix_g", "w_in", "w_a2_fwd", "b_a_fwd", "w_a2_bwd", "b_a_bwd", "gla_norm_g", "sgu_norm_g", "w_s",
    "b_s", "w_out", "norm_mlp_g", "w_mlp1", "w_mlp2", "final_norm_g", "ln_emb_g_2", "ln_emb_b_2", "w_in_2",
    "conv_w_2", "conv_b_2", "A_log_fwd_2", "A_log_bwd_2", "dt_bias_fwd_2", "dt_bias_bwd_2", "D_skip_2",
    "ssm_norm_g_2", "lambda_q1_2", "lambda_k1_2", "lambda_q2_2", "lambda_k2_2", "subln_g_2", "w_out_2", "ln_g_2",
    "ln_b_2", "p_3", "ln_g_3", "w_in_3", "conv_w_3", "conv_b_3", "cnorm_g_3", "cnorm_b_3", "w_pw2_3", "b_pw2_3",
    "lb_logits_3", "onorm_g_3", "w_out_3", "pe_norm_g_3", "w_pg_3", "w_pp_3", "final_g_3",
]


def kernel(**inputs):
    import numpy as _np
    import concourse.bacc as _bacc
    from concourse import mybir as _mybir
    from concourse.bass_utils import run_bass_kernel_spmd as _run

    nc = _bacc.Bacc("TRN2", target_bir_lowering=False, num_devices=1)
    arrays, args = {}, {}
    for name in _INS:
        a = _np.ascontiguousarray(inputs[name])
        arrays[f"in_{name}_dram"] = a
        args[name] = nc.dram_tensor(f"in_{name}_dram", a.shape, _mybir.dt.from_np(a.dtype),
                                    kind="ExternalInput").ap()
    o = nc.dram_tensor("out_0_dram", (1, 1024, 1024), F32, kind="ExternalOutput").ap()
    build(nc, args, o)
    r = _run(nc, [arrays], core_ids=[0])
    return r.results[0]["out_0_dram"]
```

```python
import math
from contextlib import ExitStack
from itertools import chain, islice

import numpy as np
import concourse.bass as bass
from concourse import mybir

F32 = mybir.dt.float32
F32R = mybir.dt.float32r
I32 = mybir.dt.int32
ALU = mybir.AluOpType
ACT = mybir.ActivationFunctionType
AX = mybir.AxisListType
ADD, SUB, MUL, MAX, MIN = ALU.add, ALU.subtract, ALU.mult, ALU.max, ALU.min
ALPHA = 2.0 ** 0.25
S = 1024
NT = 8


class Queue:

    def __init__(self, sem):
        self.sem, self.n, self.items = sem, 0, []

    def __call__(self, fn, *a, w=(), inc=True, **k):
        self.n += inc
        self.items.append((fn, a, k, list(w), self.sem if inc else None, 1))
        return (self.sem, self.n)

    def dma(self, fn, out, in_, sem, w=()):
        self.items.append((fn, (out, in_), {}, list(w), sem, 16))

    def later(self, fn):
        self.items.append((fn, None, None, [], None, 0))

    def now(self):
        return (self.sem, self.n)

    def emit(self, eng):
        seen = {}

        def wait(w):
            for sem, v in w:
                if v > 0 and seen.get(id(sem), 0) < v:
                    eng.wait_ge(sem, v)
                    seen[id(sem)] = v
        for fn, a, k, w, sem, by in self.items:
            if a is None:
                fn(wait)
                continue
            wait(w)
            ins = fn(*a, **k)
            if sem is not None:
                ins.then_inc(sem, by)


class Slot:

    def __init__(self, t):
        self.t, self._w, self.held = t, [], False

    @property
    def w(self):
        return self._w

    @w.setter
    def w(self, toks):
        self._w, self.held = toks, False


class Ring:
    def __init__(self, ts):
        self.s, self.i = [Slot(t) for t in ts], -1

    def get(self):
        for _ in self.s:
            self.i = (self.i + 1) % len(self.s)
            if not self.s[self.i].held:
                self.s[self.i].held = True
                return self.s[self.i]
        raise RuntimeError("no slot is free")


def weave(*parts):
    live = [[g, n, 0] for g, n in parts]
    while live:
        x = min(live, key=lambda x: (x[2] + 0.5) / x[1])
        x[2] += 1
        try:
            next(x[0])
        except StopIteration:
            live.remove(x)


def steps(g):
    for _ in g:
        pass


def bc(ap, shape):
    return ap.broadcast_to(shape)


def build(nc, A, out, upto=3):
    ctx = ExitStack()
    with ctx:
        program(nc, A, out, ctx, upto)


def program(nc, A, out, ctx, upto):
    names = [0]

    def sbt(c, shape, dt=F32):
        names[0] += 1
        return c.enter_context(nc.sbuf_tensor(f"t{names[0]}", shape, dt))

    def sem(name):
        return ctx.enter_context(nc.semaphore(name))

    PE, AC, DV, PO = (Queue(sem(n)) for n in ("s_pe", "s_ac", "s_dv", "s_po"))
    SP = Queue(sem("s_sp"))
    T, V, G, C = nc.tensor, nc.vector, nc.gpsimd, nc.scalar
    dram = nc.dram_tensor
    YM = dram("ym_scratch", [2048, S], F32, kind="Internal").ap()
    XD = dram("x_scratch", [S, 1024], F32, kind="Internal").ap()
    ZG = dram("zg_scratch", [1024, S], F32, kind="Internal").ap()
    ZS = dram("zs_scratch", [8, 128, 1024], F32, kind="Internal").ap()
    GS = dram("gs_scratch", [16, 128, 1024], F32, kind="Internal").ap()
    YC = dram("yc_scratch", [1024, S], F32, kind="Internal").ap()

    dsem = [[sem(f"s_d{i}"), 0] for i in range(24)]
    dcount = [0]
    stores = {}

    def dma(q, out_, in_, w=()):
        d = dsem[dcount[0] % len(dsem)]
        dcount[0] += 1
        before = [(d[0], d[1])] if d[1] else []
        d[1] += 16
        fn = {id(SP): nc.sync.dma_start, id(PO): G.dma_start, id(AC): C.dma_start}[id(q)]
        q.dma(fn, out_, in_, d[0], w=list(w) + before)
        return (d[0], d[1])

    HTh = sbt(ctx, [128, 8, S], F32R)
    HTl = sbt(ctx, [128, 8, S], F32R)
    WR = [sbt(ctx, [128, 2048]) for _ in range(2)]
    WH = [sbt(ctx, [128, 2048], F32R) for _ in range(2)]
    WL = [sbt(ctx, [128, 2048], F32R) for _ in range(2)]
    ident = sbt(ctx, [128, 128])
    Uinc = sbt(ctx, [128, 128])
    Linc = sbt(ctx, [128, 128])
    ones = sbt(ctx, [128, 128])
    nhalf = sbt(ctx, [128, 64])
    PC = sbt(ctx, [128, 4 * 128])
    ss = sbt(ctx, [128, 64])
    st = sbt(ctx, [128, 64])

    PD = Ring([ctx.enter_context(nc.psum_tensor(f"pd{i}", [128, 512], F32)) for i in range(4)])
    PQt = [ctx.enter_context(nc.psum_tensor(f"pq{i}", [128, 1024], F32)) for i in range(2)]
    PB = Ring([PQt[0][:, 0:512], PQt[0][:, 512:1024], PQt[1][:, 0:512], PQt[1][:, 512:1024]])

    NR = 2
    s_wr = [sem(f"s_wr{i}") for i in range(NR)]
    s_wh, s_wl = sem("s_wh"), sem("s_wl")
    units = []
    freed = []

    def load_unit(i):
        def go(wait):
            if i >= len(units):
                return
            if i >= NR:
                wait([(s_wh, i - NR + 1), (s_wl, i - NR + 1)])
            sz, pieces = units[i]
            for k, (o, src) in enumerate(pieces):
                ins = nc.sync.dma_start(o(WR[i % NR]), src)
                ins.then_inc(s_wr[i % NR], 16)
        SP.later(go)

    def need(i):
        return (s_wr[i % NR], sum(16 * len(units[j][1]) for j in range(i % NR, i + 1, NR)))

    def split_unit(i):
        def hi(wait):
            if i < len(units):
                wait([need(i)] + ([freed[i - 2]] if i >= 2 else []))
                n = units[i][0]
                C.activation(WH[i % 2][:, 0:n], WR[i % NR][:, 0:n], ACT.Copy).then_inc(s_wh, 1)

        def lo(wait):
            if i < len(units):
                wait([need(i), (s_wh, i + 1)])
                n = units[i][0]
                V.tensor_tensor(WL[i % 2][:, 0:n], WR[i % NR][:, 0:n],
                                  WH[i % 2][:, 0:n].bitcast(F32), SUB).then_inc(s_wl, 1)
        AC.later(hi)
        DV.later(lo)

    class Unit:
        def __init__(self, pieces, k, c):
            i = len(units)
            units.append((k * c, pieces))
            freed.append(None)
            if i == 0:
                for j in range(NR):
                    load_unit(j)
                split_unit(0)
            else:
                load_unit(i + NR - 1)
            split_unit(i + 1)
            self.i = i
            self.h = WH[i % 2][:, 0:k * c].rearrange("p (k c) -> p k c", k=k)
            self.l = WL[i % 2][:, 0:k * c].rearrange("p (k c) -> p k c", k=k)
            self.w = [(s_wh, i + 1), (s_wl, i + 1)]

        def done(self):
            freed[self.i] = PE.now()

    def unit(W, parts, k0=0, k=8):
        c = sum(n for _, n in parts)
        pieces, o = [], 0
        for c0, n in parts:
            src = W[k0 * 128:(k0 + k) * 128, c0:c0 + n].rearrange("(k p) c -> p k c", p=128)

            def dst(t, o=o, n=n):
                return t[:, 0:k * c].rearrange("p (k c) -> p k c", k=k)[:, :, o:o + n]
            pieces.append((dst, src))
            o += n
        return Unit(pieces, k, c)

    def mms(out_, pairs, w, first=True, last=True, inc=True, start=None, by_k=()):
        n = len(pairs)
        tok = None
        for j, (l, r) in enumerate(pairs):
            s_ = (first and j == 0) if start is None else (start and j == 0)
            tok = PE(T.matmul, out_, l, r, start=s_, stop=(last and j == n - 1),
                     skip_group_check=True, inc=(inc and j == n - 1),
                     w=(list(w) if j == 0 else []) + (by_k[j // 3] if by_k and j % 3 == 0 else []))
        return tok

    def three(lh, ll, rh, rl):
        return [(lh, rh), (lh, rl), (ll, rh)]

    HT = Slot(None)
    HT.k = []

    def fm(u, m0, th, kk=8, w=()):
        b = PD.get()
        sl = slice(th * 512, th * 512 + 512)
        pairs = []
        for k in range(kk):
            pairs += three(u.h[:, k, m0:m0 + 128], u.l[:, k, m0:m0 + 128], HTh[:, k, sl], HTl[:, k, sl])
        t = mms(b.t[:, :], pairs, b.w + u.w + ([] if HT.k else HT.w) + list(w), by_k=HT.k)
        return b, t

    def tm(u, c0, n, tts, kk=8):
        b = PD.get()
        t = None
        for j, tt in enumerate(tts):
            sl = slice(tt * 128, tt * 128 + 128)
            pairs = []
            for k in range(kk):
                pairs += three(HTh[:, k, sl], HTl[:, k, sl], u.h[:, k, c0:c0 + n], u.l[:, k, c0:c0 + n])
            t = mms(b.t[:, j * n:(j + 1) * n], pairs, b.w + u.w + ([] if HT.k else HT.w),
                    inc=(j == len(tts) - 1), by_k=HT.k)
        return b, t

    def fence(extra=()):
        w = [q.now() for q in (PE, AC, DV, PO)] + list(extra) + [(d[0], d[1]) for d in dsem if d[1]]
        for q in (PE, AC, DV, PO, SP):
            q.later(lambda wait, w=w: wait(w))

    t = PO(G.memset, ident[:, :], 0.0)
    t = PO(G.affine_select, out=ident[:, :], in_=ident[:, :], compare_op=ALU.not_equal, fill=1.0,
           base=0, pattern=[[-1, 128]], channel_multiplier=1, w=[t])
    t = PO(G.memset, ones[:, :], 1.0)
    PO(G.memset, nhalf[:, :], -0.5)
    PO(G.affine_select, out=Uinc[:, :], in_=ones[:, :], compare_op=ALU.is_ge, fill=0.0,
       base=0, pattern=[[1, 128]], channel_multiplier=-1, w=[t])
    CST = PO(G.affine_select, out=Linc[:, :], in_=ones[:, :], compare_op=ALU.is_ge, fill=0.0,
             base=0, pattern=[[-1, 128]], channel_multiplier=1)

    def rsqrt(dst, src, scale, eps, w):
        n = src.shape[-1]
        t = DV(V.tensor_scalar, dst, src, scale, eps, MUL, ADD, w=w)
        return PO(G.tensor_tensor, dst, dst, nhalf[:, 0:n], ALU.pow, w=[t])

    col = {}

    def columns(c, n0, parts):
        PR = sbt(c, [128, 128])
        z = PO(G.memset, PR[:, :], 0.0)
        r, toks = 0, []
        for name, ap in parts:
            k = ap.shape[0]
            toks.append(dma(SP, PR[r:r + k, :], ap, w=[z]))
            col[name] = n0 + r
            r += k
        assert r <= 128
        b = PB.get()
        t = PE(T.transpose, b.t[:, 0:128], PR[:, :], ident[:, :], w=b.w + toks + [CST])
        t = DV(V.tensor_copy, PC[:, n0:n0 + 128], b.t[:, 0:128], w=[t])
        b.w = [t]
        return t

    def vec(ap):
        return ap.rearrange("(k p) -> k p", p=128)

    def pc(name, i=0):
        c = col[name] + i
        return PC[:, c:c + 1]

    lam = sbt(ctx, [128, 4])
    ph = ExitStack()
    toks = []
    toks.append(columns(ph, 0, [
        ("g_mix", vec(A["norm_mix_g"][0])), ("g_mlp", vec(A["norm_mlp_g"][0])),
        ("ba0", vec(A["b_a_fwd"][0])), ("ba1", vec(A["b_a_bwd"][0])),
        ("gla_g", A["gla_norm_g"][0]), ("sgu_g", A["sgu_norm_g"][0]),
        ("cw2", A["conv_w_2"][0].rearrange("j (k p) -> (j k) p", p=128)),
        ("cb2", vec(A["conv_b_2"][0])), ("ssm_g", vec(A["ssm_norm_g_2"][0])),
        ("subln", A["subln_g_2"])]))
    toks.append(columns(ph, 128, [
        ("cw3a", A["conv_w_3"][0, 0:16, :].rearrange("j (k p) -> (j k) p", p=128))]))
    toks.append(columns(ph, 256, [
        ("cw3b", A["conv_w_3"][0, 16:31, :].rearrange("j (k p) -> (j k) p", p=128))]))
    toks.append(columns(ph, 384, [
        ("g3", vec(A["ln_g_3"][0])), ("cb3", vec(A["conv_b_3"][0])),
        ("cng", vec(A["cnorm_g_3"][0])), ("cnb", vec(A["cnorm_b_3"][0])),
        ("bpw", vec(A["b_pw2_3"][0])), ("lb0", vec(A["lb_logits_3"][0])),
        ("lb1", vec(A["lb_logits_3"][1])), ("ong", vec(A["onorm_g_3"][0])),
        ("peg", vec(A["pe_norm_g_3"][0]))]))
    PCt = toks

    lv = sbt(ph, [128, 5, 64])
    toks = [dma(SP, lv[:, i, :], A[n].partition_broadcast(128).rearrange("p a d -> p (a d)"))
            for i, n in enumerate(("lambda_q1_2", "lambda_k1_2", "lambda_q2_2", "lambda_k2_2"))]
    for i in range(2):
        t = DV(V.tensor_tensor, lv[:, 4, :], lv[:, 2 * i, :], lv[:, 2 * i + 1, :], MUL, w=toks + [DV.now()])
        t = DV(V.tensor_reduce, lam[:, i:i + 1], lv[:, 4, :], AX.X, ADD, w=[t])
    t = AC(C.activation, lam[:, 0:2], lam[:, 0:2], ACT.Exp, w=[t])
    t = DV(V.tensor_tensor, lam[:, 2:3], lam[:, 1:2], lam[:, 0:1], SUB, w=[t])
    t = DV(V.tensor_scalar, lam[:, 3:4], lam[:, 2:3], -(0.8 - 0.6 * math.exp(0.0)), None, ADD, w=[t])
    t = DV(V.tensor_scalar, pc("subln"), pc("subln"), 1.0 - (0.8 - 0.6 * math.exp(0.0)), None, MUL, w=PCt)
    PCt = PCt + [t]
    fence(PCt)
    ph.close()

    def row_bcast(c, ap):
        n = ap.shape[-1]
        r = sbt(c, [128, n])
        return r, dma(SP, r[:, :], ap.partition_broadcast(128))

    def load_X(X, src):
        v = src.rearrange("(t p) d -> p t d", p=128)
        return [dma(SP, X[:, tt, :], v[:, tt, :]) for tt in range(NT)]

    def store_X(X, dst, w):
        v = dst.rearrange("(t p) d -> p t d", p=128)
        return [dma(SP, v[:, tt, :], X[:, tt, :], w=w[tt] if isinstance(w[0], list) else w) for tt in range(NT)]

    def split_HT(k, sl, src, scale, w):
        if scale is None:
            t1 = AC(C.activation, HTh[:, k, sl], src, ACT.Copy, w=w)
            t2 = DV(V.tensor_tensor, HTl[:, k, sl], src, HTh[:, k, sl].bitcast(F32), SUB, w=[t1] + w)
        else:
            t1 = AC(C.activation, HTh[:, k, sl], src, ACT.Copy, scale=scale, w=w)
            t2 = DV(V.scalar_tensor_tensor, HTl[:, k, sl], src, scale, HTh[:, k, sl].bitcast(F32), MUL, SUB,
                    w=[t1] + w)
        return t1, t2

    def squares(X, th, wt):
        a, b = PB.s[0], PB.s[1]
        for tt in range(th * 4, th * 4 + 4):
            t = AC(C.activation, PQt[0][:, :], X[:, tt, :], ACT.Square, accum_out=ss[:, 16 + tt:17 + tt],
                   w=list(wt[tt]) + a.w + b.w + [AC.now()])
        a.w, b.w = [t], [t]
        return t

    def rstd(th, t):
        sl = slice(16 + th * 4, 20 + th * 4)
        return rsqrt(st[:, sl], ss[:, sl], 1.0 / 1024, 1e-6, [t])

    def to_HT(srcs, th, ws, gname):
        for k in range(8):
            b = PD.get()
            for j in range(4):
                t = PE(T.transpose, b.t[:, j * 128:(j + 1) * 128], srcs[j][:, k * 128:(k + 1) * 128], ident[:, :],
                       w=b.w + [ws[j]], inc=(j == 3))
            t1, t2 = split_HT(k, slice(th * 512, th * 512 + 512), b.t[:, :], pc(gname, k) if gname else None, [t])
            b.w = [t1, t2]
            yield
        HT.w, HT.k = [t1, t2], []

    def norm_HT(X, XN, wt, gname):
        rs = [rstd(0, squares(X, 0, wt))]
        tsq = squares(X, 1, wt)
        sl, tok = [XN.get() for _ in range(8)], [None] * 8

        def scaled(tt, r):
            c = 16 + tt
            tok[tt] = DV(V.tensor_scalar, sl[tt].t[:, :], X[:, tt, :], st[:, c:c + 1], None, MUL,
                         w=[r] + list(wt[tt]) + sl[tt].w)

        for tt in range(4):
            scaled(tt, rs[0])
        r1 = rstd(1, tsq)
        for k, _ in enumerate(to_HT([x.t for x in sl[0:4]], 0, tok[0:4], gname)):
            if k % 2 == 1:
                scaled(4 + k // 2, r1)
        steps(to_HT([x.t for x in sl[4:8]], 1, tok[4:8], gname))
        for x in sl:
            x.w = [PE.now()]

    def rms_heads(O, n, d, sq, w, eps, name_scale=None):
        t = AC(C.activation, sq, O, ACT.Square, w=w)
        t = DV(V.tensor_reduce, ss[:, 0:n], sq, AX.X, ADD, w=[t])
        t = rsqrt(st[:, 0:n], ss[:, 0:n], 1.0 / d, eps, [t])
        return DV(V.tensor_tensor, O, O, bc(st[:, 0:n].unsqueeze(2), [128, n, d]), MUL, w=[t])

    def load_HT(got):
        reads = [PE.now()]
        HT.k = []
        for k, (s, td) in enumerate(got):
            t1 = AC(C.activation, HTh[:, k, :], s.t[:, :], ACT.Copy, w=[td] + reads)
            t2 = DV(V.tensor_tensor, HTl[:, k, :], s.t[:, :], HTh[:, k, :].bitcast(F32), SUB, w=[t1, td] + reads)
            s.w = [t1, t2]
            HT.k.append([t1, t2])

    def fetch(stage, src, w):
        got = []
        for k in range(8):
            s = stage.get()
            got.append((s, dma(AC, s.t[:, :], src[k * 128:(k + 1) * 128, :], w=s.w + w)))
        return got

    def add_proj(X, W, kg, xt, alpha=None):
        last = [None] * NT
        for n in range(4):
            u = unit(W, [(n * 256, 256)], k0=kg * 8)
            for t4 in range(4):
                b, t = tm(u, 0, 256, [2 * t4, 2 * t4 + 1])
                o = X[:, 2 * t4:2 * t4 + 2, n * 256:(n + 1) * 256]
                bv = b.t[:, :].rearrange("p (a c) -> p a c", a=2)
                w = [t, xt[2 * t4], xt[2 * t4 + 1]]
                if alpha is None:
                    t = DV(V.tensor_tensor, o, bv, o, ADD, w=w)
                else:
                    t = DV(V.scalar_tensor_tensor, o, o, alpha, bv, MUL, ADD, w=w)
                b.w = [t]
                last[2 * t4] = last[2 * t4 + 1] = [t]
            u.done()
        return last

    x_in = A["x"][0]
    ph = ExitStack()
    X = sbt(ph, [128, NT, 1024])
    xt = load_X(X, x_in)
    norm_HT(X, Ring([sbt(ph, [128, 1024]) for _ in range(8)]), [[x] for x in xt], "g_mix")
    fence()
    ph.close()

    W = A["w_in"][0]
    ph = ExitStack()
    M64 = sbt(ph, [128, S])
    aT = sbt(ph, [32, S])
    wa = [sbt(ph, [32, 256]) for _ in range(2)]
    qT, kT, bb = sbt(ph, [128, S]), sbt(ph, [128, S]), sbt(ph, [128, S])
    DE = sbt(ph, [128, 2, S])
    qin, kin, qx = sbt(ph, [128, S]), sbt(ph, [128, S]), sbt(ph, [128, S])
    vt = sbt(ph, [128, NT, 256])
    kdt = sbt(ph, [128, NT, 128])
    Am = sbt(ph, [128, 2, NT, 128])
    Sg = sbt(ph, [128, 16, 128])
    O = sbt(ph, [128, NT, 2, 128])
    dec = sbt(ph, [128, 16])
    mk = sbt(ph, [128, 2, 64])
    t = PO(G.memset, M64[:, :], 1.0)
    t = PO(G.memset, M64[:, :].rearrange("p (c t) -> p c t", t=64)[:, :, 0:1], 0.0, w=[t])
    PO(G.memset, Am[:, :, :, :], 0.0)
    t = PO(G.memset, mk[:, :, :], 1.0)
    for half in range(2):
        r = slice(64 * half, 64 * half + 64)
        PO(G.affine_select, out=mk[r, 0, :], in_=mk[r, 0, :], compare_op=ALU.is_ge, fill=0.0,
           base=0, pattern=[[1, 64]], channel_multiplier=-1, w=[t])
        PO(G.affine_select, out=mk[r, 1, :], in_=mk[r, 1, :], compare_op=ALU.is_gt, fill=0.0,
           base=0, pattern=[[-1, 64]], channel_multiplier=1, w=[t])
    PO(G.memset, wa[0][:, :], 0.0)
    t = PO(G.memset, wa[1][:, :], 0.0)
    g0 = t
    wat = [dma(SP, wa[0][0:16, :], A["w_a2_fwd"][0], w=[t]), dma(SP, wa[1][16:32, :], A["w_a2_bwd"][0], w=[t])]
    u = unit(W, [(1536, 128)])
    for th in range(2):
        b, t = fm(u, 0, th)
        t = AC(C.copy, aT[:, th * 512:th * 512 + 512], b.t[0:32, :], w=[t])
        b.w = [t]
    u.done()
    at = t
    ysp = []
    prev = []
    stg = Ring([sbt(ph, [128, S]) for _ in range(3)])
    gs_tok = {}

    def fm_store(u, m0, name, i, **how):
        s = stg.get()
        for th in range(2):
            b, t = fm(u, m0, th)
            t = AC(C.activation, s.t[:, th * 512:th * 512 + 512], b.t[:, :], w=[t] + s.w, **how)
            b.w = [t]
            if th == 1:
                gs_tok[name] = [dma(SP, GS[i], s.t[:, :], w=[t])]
                s.w = gs_tok[name]
            yield

    def tm_store(u, name, i, **how):
        gs_tok[name] = []
        for n in range(2):
            s = stg.get()
            for h in range(2):
                t4 = 2 * n + h
                b, t = tm(u, 0, 256, [2 * t4, 2 * t4 + 1])
                t = AC(C.activation, s.t[:, h * 512:h * 512 + 512], b.t[:, :], w=[t] + s.w, **how)
                b.w = [t]
                if h == 1:
                    gs_tok[name].append(dma(SP, GS[i + n], s.t[:, :], w=[t]))
                    s.w = gs_tok[name][-1:]
                yield

    def dense_ahead(n):
        if n == 0:
            u = unit(W, [(128, 128), (384, 128)])
            yield from fm_store(u, 0, "q", 0, func=ACT.Copy, scale=0.125)
            yield from fm_store(u, 128, "k", 1, func=ACT.Copy)
            u.done()
            u = unit(W, [(768, 256)])
            yield from tm_store(u, "v", 2, func=ACT.Copy)
            u.done()
        elif n == 1:
            for pt in range(2):
                u = unit(W, [(1024 + pt * 256, 256)])
                for hh in range(2):
                    yield from fm_store(u, hh * 128, ("g", pt, hh), 4 + pt * 2 + hh, func=ACT.Silu)
                u.done()
        elif n == 2:
            for gp in range(2):
                u = unit(W, [(2080 + gp * 256, 256)])
                yield from tm_store(u, ("sv", gp), 8 + gp * 2, func=ACT.Gelu)
                u.done()
        else:
            for gp in range(2):
                u = unit(W, [(1568 + gp * 256, 256)])
                for g in range(2):
                    yield from fm_store(u, g * 128, ("su", gp, g), 12 + gp * 2 + g, func=ACT.Gelu)
                u.done()

    qkv = [[], [], []]

    def qk_first():
        u = unit(W, [(0, 128), (256, 128)])
        for th in range(2):
            sl = slice(th * 512, th * 512 + 512)
            b, t = fm(u, 0, th)
            qkv[0].append(AC(C.mul, qT[:, sl], b.t[:, :], 0.125, w=[t]))
            b.w = qkv[0][-1:]
            b, t = fm(u, 128, th)
            qkv[1].append(DV(V.tensor_copy, kT[:, sl], b.t[:, :], w=[t]))
            b.w = qkv[1][-1:]
        u.done()

    def v_first():
        u = unit(W, [(512, 256)])
        for t4 in range(4):
            b, t = tm(u, 0, 256, [2 * t4, 2 * t4 + 1])
            qkv[2].append(AC(C.copy, vt[:, 2 * t4:2 * t4 + 2, :], b.t[:, :].rearrange("p (a c) -> p a c", a=2),
                             w=[t]))
            b.w = qkv[2][-1:]
            yield
        u.done()

    def gla(pt, d, tq, tk, tv):
        D, E = DE[:, 0, :], DE[:, 1, :]
        for th in range(2):
            sl = slice(th * 512, th * 512 + 512)
            b = PB.get()
            t = mms(b.t[:, :], [(wa[d][:, pt * 128:(pt + 1) * 128], aT[:, sl])], b.w + [at] + wat)
            t = AC(C.activation, D[:, sl], b.t[:, :], ACT.Identity, bias=pc(f"ba{d}", pt), w=[t] + prev + [DV.now(), PE.now()])
            b.w = [t]
        yield
        t1 = AC(C.activation, E, D, ACT.Abs, w=[t])
        t1 = AC(C.activation, E, E, ACT.Exp, scale=-1.0, w=[t1])
        t1 = AC(C.activation, E, E, ACT.Ln, bias=1.0, w=[t1])
        t = DV(V.tensor_scalar, D, D, 0.0, 1.0 / 16, MIN, MUL, w=[t, t1])
        t = DV(V.scalar_tensor_tensor, D, E, -1.0 / 16, D, MUL, ADD, w=[t])
        yield
        if d == 0:
            t = DV(V.tensor_tensor_scan, bb[:, :], M64[:, :], D, 0.0, op0=MUL, op1=ADD, w=[t, g0])
        else:
            t = DV(V.tensor_tensor_scan, bb[:, ::-1], M64[:, :], DE[:, 0, ::-1], 0.0, op0=MUL, op1=ADD, w=[t])
        bv = bb[:, :].rearrange("p (c t) -> p c t", t=64)
        Dv = D.rearrange("p (c t) -> p c t", t=64)
        mid, end = (32, 63) if d == 0 else (31, 0)
        t = DV(V.tensor_tensor, Dv, bv, bc(bv[:, :, mid:mid + 1], [128, 16, 64]), SUB, w=[t])
        t1 = AC(C.activation, E, D, ACT.Exp, w=[t])
        t = DV(V.tensor_tensor, qin[:, :], qT[:, :], E, MUL, w=[t1] + tq)
        t2 = AC(C.activation, E, D, ACT.Exp, scale=-1.0, w=[t])
        ti = DV(V.tensor_tensor, kin[:, :], kT[:, :], E, MUL, w=[t2] + tk)
        yield
        t3 = DV(V.tensor_tensor, Dv, bc(bv[:, :, end:end + 1], [128, 16, 64]), bv, SUB, w=[t2])
        t3 = AC(C.activation, D, D, ACT.Exp, w=[t3])
        tkd = DV(V.tensor_tensor, D, kT[:, :], D, MUL, w=[t3])
        t4_ = AC(C.activation, E, bb[:, :], ACT.Exp, w=[ti])
        tdec = AC(C.activation, dec[:, :], bv[:, :, end], ACT.Exp, w=[DV.now()])
        tqx = DV(V.tensor_tensor, qx[:, :], qT[:, :], E, MUL, w=[t4_])
        yield
        for th in range(2):
            b = PB.get()
            for j in range(4):
                tt = th * 4 + j
                t = PE(T.transpose, b.t[:, j * 128:(j + 1) * 128], D[:, tt * 128:(tt + 1) * 128], ident[:, :],
                       w=b.w + [tkd], inc=(j == 3))
            tkt = AC(C.copy, kdt[:, th * 4:th * 4 + 4, :], b.t[:, :].rearrange("p (a c) -> p a c", a=4), w=[t])
            b.w = [tkt]
        yield
        banks = [PB.get(), PB.get()]
        for hh in range(2):
            r = slice(64 * hh, 64 * hh + 64)
            b = banks[hh]
            for c in range(16):
                half, cs = c % 2, slice(64 * c, 64 * c + 64)
                t = mms(b.t[64 * half:64 * half + 64, 64 * (c // 2):64 * (c // 2) + 64],
                        [(kin[r, cs], qin[r, cs])], b.w + [ti], inc=(c == 15))
            for half in range(2):
                p = slice(64 * half, 64 * half + 64)
                ta = DV(V.tensor_tensor, Am[p, hh, :, 64 * half:64 * half + 64],
                        b.t[p, :].rearrange("p (a c) -> p a c", a=8),
                        bc(mk[p, d:d + 1, :], [64, 8, 64]), MUL, w=[t, g0])
            b.w = [ta]
        yield
        order = list(range(16)) if d == 0 else list(range(15, -1, -1))
        t = DV(V.memset, Sg[:, order[0], :], 0.0, w=[PE.now()])
        ts = t
        for q4 in range(4):
            cs = order[q4 * 4:q4 * 4 + 4]
            banks = [PB.get(), PB.get()]
            for j, c in enumerate(cs):
                half, tt = c % 2, c // 2
                r = slice(64 * half, 64 * half + 64)
                for hh in range(2):
                    t = mms(banks[half].t[64 * hh:64 * hh + 64, (j // 2) * 128:(j // 2) * 128 + 128],
                            [(kdt[r, tt, 64 * hh:64 * hh + 64], vt[r, tt, hh * 128:hh * 128 + 128])],
                            banks[half].w + [tkt] + tv, inc=(j == 3 and hh == 1))
            for j, c in enumerate(cs):
                i = q4 * 4 + j
                if i < 15:
                    ts = DV(V.scalar_tensor_tensor, Sg[:, order[i + 1], :], Sg[:, c, :], dec[:, c:c + 1],
                            banks[c % 2].t[:, (j // 2) * 128:(j // 2) * 128 + 128], MUL, ADD, w=[t, ts, tdec])
            for b in banks:
                b.w = [ts]
            yield
        for hh in range(2):
            r = slice(64 * hh, 64 * hh + 64)
            for th in range(2):
                b = PB.get()
                for j in range(4):
                    tt = th * 4 + j
                    o = b.t[:, j * 128:(j + 1) * 128]
                    mms(o, [(Am[:, hh, tt, :], vt[:, tt, hh * 128:(hh + 1) * 128])], b.w + [ta, ts, tqx] + tv,
                        last=False, inc=False)
                    for half in range(2):
                        c = 2 * tt + half
                        t = mms(b.t[64 * half:64 * half + 64, j * 128:(j + 1) * 128],
                                [(qx[r, 64 * c:64 * c + 64], Sg[r, c, :])], (), first=False,
                                inc=(half == 1))
                ov = O[:, th * 4:th * 4 + 4, hh, :]
                bvw = b.t[:, :].rearrange("p (a c) -> p a c", a=4)
                if d == 0:
                    to = DV(V.tensor_copy, ov, bvw, w=[t] + prev)
                else:
                    to = DV(V.tensor_tensor, ov, bvw, ov, ADD, w=[t, DV.now()])
                b.w = [to]
                yield
        got_o.append(to)

    def gla_out(pt):
        Of = O[:, :, :, :].rearrange("p a b c -> p (a b) c")
        t = rms_heads(Of, 16, 128, Sg[:, :, :], [got_o[-1], PE.now()], 1e-6)
        for hh in range(2):
            for th in range(2):
                b = PB.get()
                for j in range(4):
                    tt_ = PE(T.transpose, b.t[:, j * 128:(j + 1) * 128], O[:, th * 4 + j, hh, :], ident[:, :],
                             w=b.w + [t], inc=(j == 3))
                gs = DE[:, hh, th * 512:th * 512 + 512]
                ty = DV(V.scalar_tensor_tensor, gs, b.t[:, :], pc("gla_g", pt * 2 + hh), gs, MUL, MUL, w=[tt_, gs_tok["g", pt, hh]])
                b.w = [ty]
                yield
            r = (pt * 2 + hh) * 128
            ysp.append(dma(SP, YM[r:r + 128, :], DE[:, hh, :], w=[ty]))

    got_o = []
    first = gla(0, 0, *qkv)
    next(first)
    next(first)
    qk_first()
    weave((first, 13), (chain(v_first(), dense_ahead(0)), 18))
    for pt in range(2):
        weave((gla(pt, 1, *qkv), 15), (dense_ahead(1 + 2 * pt), 22))
        gw = [PE.now(), AC.now(), DV.now()]
        for hh in range(2):
            tg = dma(SP, DE[:, hh, :], GS[4 + pt * 2 + hh], w=gw + gs_tok["g", pt, hh])
            gs_tok["g", pt, hh] = tg
        if pt == 0:
            qkv = [[dma(SP, qT[:, :], GS[0], w=gw + gs_tok["q"])], [dma(SP, kT[:, :], GS[1], w=gw + gs_tok["k"])],
                   [dma(SP, vt[:, 4 * n:4 * n + 4, :].rearrange("p a c -> p (a c)"), GS[2 + n],
                        w=gw + gs_tok["v"]) for n in range(2)]]
        more = dense_ahead(2) if pt == 0 else iter(())
        weave((gla_out(pt), 4), (islice(more, 3), 4))
        prev = [PE.now(), AC.now(), DV.now()] + ysp[-2:]
        if pt == 0:
            weave((gla(1, 0, *qkv), 15), (more, 15))
    fence()
    ph.close()

    ph = ExitStack()
    X = sbt(ph, [128, NT, 1024])
    hk = []
    ph2 = ExitStack()
    stage = Ring([sbt(ph2, [128, S]) for _ in range(2)])
    for k in range(4):
        s = stage.get()
        td = dma(SP, s.t[:, :], YM[k * 128:(k + 1) * 128, :], w=s.w)
        t1, t2 = split_HT(k, slice(0, S), s.t[:, :], None, [td])
        s.w = [t1, t2]
        hk.append([t1, t2])
    wsr = sbt(ph2, [128, 4, 128])
    wsT = sbt(ph2, [128, 4, 128])
    bsr, bst = row_bcast(ph2, A["b_s"][0].rearrange("g p -> (g p)"))
    wst = dma(SP, wsr[:, :, :], A["w_s"][0].rearrange("g p q -> p g q"))
    b = PB.get()
    for g in range(4):
        t = PE(T.transpose, b.t[:, g * 128:(g + 1) * 128], wsr[:, g, :], ident[:, :], w=b.w + [wst], inc=(g == 3))
    twT = AC(C.copy, wsT[:, :, :], b.t[:, :].rearrange("p (a c) -> p a c", a=4), w=[t])
    b.w = [twT]
    VS = Ring([sbt(ph2, [128, NT, 2, 128]) for _ in range(2)])
    UT = Ring([sbt(ph2, [128, 2, S]) for _ in range(2)])
    sq = sbt(ph2, [128, 16, 128])
    for gp in range(2):
        vs, ut = VS.get(), UT.get()
        tv = [dma(SP, vs.t[:, 4 * n:4 * n + 4, :, :].rearrange("p a g c -> p (a g c)"), GS[8 + gp * 2 + n])
              for n in range(2)]
        tu = [dma(SP, ut.t[:, g, :], GS[12 + gp * 2 + g]) for g in range(2)]
        tv = rms_heads(vs.t[:, :, :, :].rearrange("p a g c -> p (a g) c"), 16, 128, sq[:, :, :],
                       tv + [DV.now()], 1e-6)
        for g in range(2):
            gg = gp * 2 + g
            for th in range(2):
                b = PB.get()
                for j in range(4):
                    t = mms(b.t[:, j * 128:(j + 1) * 128], [(vs.t[:, th * 4 + j, g, :], wsT[:, gg, :])],
                            b.w + [tv, twT], inc=(j == 3))
                mixed = sq[:, 0:4, :]
                t = DV(V.scalar_tensor_tensor, mixed, b.t[:, :].rearrange("p (a c) -> p a c", a=4),
                       pc("sgu_g", gg),
                       bc(bsr[:, gg * 128:(gg + 1) * 128].unsqueeze(1), [128, 4, 128]), MUL, ADD,
                       w=[t, bst, DV.now()])
                b.w = [t]
                o = ut.t[:, g, th * 512:th * 512 + 512]
                t = DV(V.tensor_tensor, o, o, mixed.rearrange("p a c -> p (a c)"), MUL, w=[t, tu[g]])
            hk.append(split_HT(4 + gg, slice(0, S), ut.t[:, g, :], None, [t]))
    xt = load_X(X, x_in)
    HT.k = [list(x) for x in hk]
    tiles = [v.t[:, 4 * n:4 * n + 4, :, :].rearrange("p a g c -> p (a g c)") for v in VS.s for n in range(2)]
    XN = Ring(tiles + [u_.t[:, g, :] for u_ in UT.s for g in range(2)])
    for x in XN.s:
        x.w = [PE.now(), AC.now(), DV.now()]
    wt = add_proj(X, A["w_out"][0], 0, xt)
    norm_HT(X, XN, wt, "g_mlp")
    fence()
    ph2.close()
    ph2 = ExitStack()
    Uh = [sbt(ph2, [128, 2, S], F32R) for _ in range(2)]
    Ul = [sbt(ph2, [128, 2, S], F32R) for _ in range(2)]
    rr = Ring([sbt(ph2, [128, 512]) for _ in range(3)])
    qq = Ring([sbt(ph2, [128, 512]) for _ in range(3)])
    fg, t1 = row_bcast(ph2, A["final_norm_g"])
    eg, t2 = row_bcast(ph2, A["ln_emb_g_2"])
    eb, t3 = row_bcast(ph2, A["ln_emb_b_2"])
    W1, W2 = A["w_mlp1"][0], A["w_mlp2"][0]
    utok, uread = {}, {}

    def up(j):
        u = unit(W1, [(j * 256, 256)])
        toks = []
        for m in range(2):
            for th in range(2):
                sl = slice(th * 512, th * 512 + 512)
                b, t = fm(u, m * 128, th)
                r, q = rr.get(), qq.get()
                t = AC(C.activation, r.t[:, :], b.t[:, :], ACT.Relu, w=[t] + r.w)
                b.w = [t]
                tq = PO(G.tensor_tensor, q.t[:, :], r.t[:, :], r.t[:, :], MUL, w=[t] + q.w)
                th_ = AC(C.activation, Uh[j % 2][:, m, sl], r.t[:, :], ACT.Square, w=[t] + uread.get(j - 2, []))
                tl = DV(V.tensor_tensor, Ul[j % 2][:, m, sl], q.t[:, :], Uh[j % 2][:, m, sl].bitcast(F32), SUB,
                        w=[tq, th_])
                r.w, q.w = [tq, th_], [tl]
                toks += [th_, tl]
        u.done()
        utok[j] = toks

    def down(j):
        u = unit(W2, [(0, 1024)], k0=2 * j, k=2)
        last = []
        for tt in range(NT):
            sl = slice(tt * 128, tt * 128 + 128)
            for nh in range(2):
                cs = slice(nh * 512, nh * 512 + 512)
                b = PD.get()
                pairs = []
                for k in range(2):
                    pairs += three(Uh[j % 2][:, k, sl], Ul[j % 2][:, k, sl], u.h[:, k, cs], u.l[:, k, cs])
                t = mms(b.t[:, :], pairs, b.w + u.w + utok[j])
                t = DV(V.tensor_tensor, X[:, tt, cs], b.t[:, :], X[:, tt, cs], ADD, w=[t])
                b.w = [t]
            last.append([t])
        u.done()
        uread[j] = [PE.now()]
        return last

    up(0)
    for j in range(16):
        if j < 15:
            up(j + 1)
        wt = down(j)

    def ln_stats(X, th, wt):
        mv = st[:, 32:48]
        for tt in range(th * 4, th * 4 + 4):
            t1 = DV(V.bn_stats, ss[:, 0:6], X[:, tt, 0:512], w=list(wt[tt]) + [DV.now()])
            t2 = DV(V.bn_stats, ss[:, 6:12], X[:, tt, 512:1024])
            t3 = DV(V.bn_aggr, mv[:, 2 * tt:2 * tt + 2], ss[:, 0:12], w=[t2])
        var = mv.rearrange("p (t c) -> p t c", c=2)
        sl = slice(th * 4, th * 4 + 4)
        t = DV(V.tensor_scalar, st[:, sl], var[:, sl, 1], 1.0, 1e-5, MUL, ADD, w=[t3])
        return PO(G.tensor_tensor, st[:, sl], st[:, sl], nhalf[:, 0:4], ALU.pow, w=[t])

    def ln_apply(X, gr, br, th, w):
        mv = st[:, 32:48]
        toks = []
        for tt in range(th * 4, th * 4 + 4):
            t1 = DV(V.tensor_scalar, X[:, tt, :], X[:, tt, :], mv[:, 2 * tt:2 * tt + 1], st[:, tt:tt + 1],
                    SUB, MUL, w=w)
            t2 = DV(V.tensor_tensor, X[:, tt, :], X[:, tt, :], gr[:, :], MUL, w=[t1])
            toks.append(PO(G.tensor_tensor, X[:, tt, :], X[:, tt, :], br[:, :], ADD, w=[t2]))
        return toks

    def layernorm(X, gr, br, wt, w):
        a, b = ln_stats(X, 0, wt), ln_stats(X, 1, wt)
        return ln_apply(X, gr, br, 0, [a] + w) + ln_apply(X, gr, br, 1, [b] + w)

    def rms_scale(X, th, r, g, w):
        return [[DV(V.scalar_tensor_tensor, X[:, tt, :], X[:, tt, :], st[:, 16 + tt:17 + tt], g[:, :], MUL, MUL,
                    w=[r] + w)] for tt in range(th * 4, th * 4 + 4)]

    q0 = squares(X, 0, wt)
    q1 = squares(X, 1, wt)
    wt = rms_scale(X, 0, rstd(0, q0), fg, [t1])
    wt += rms_scale(X, 1, rstd(1, q1), fg, [t1])
    if upto == 1:
        stx = store_X(X, out[0], wt)
        ph2.close()
        ph.close()
        finish(nc, ctx, PE, AC, DV, PO, SP, stx)
        return
    toks = layernorm(X, eg, eb, wt, [t2, t3])
    stx = store_X(X, XD, [[x] for x in toks])
    for th in range(2):
        steps(to_HT([X[:, th * 4 + j, :] for j in range(4)], th, toks[th * 4:th * 4 + 4], None))
    fence()
    ph2.close()
    ph.close()
    W = A["w_in_2"][0]
    ph = ExitStack()
    dt_, dA, acs, wd, ea, dcy = (sbt(ph, [128, NT, 32]) for _ in range(6))
    dbr = sbt(ph, [128, 32])
    Ar = sbt(ph, [128, 32])
    Dr = sbt(ph, [128, 16])
    ct = [dma(SP, dbr[:, 0:16], A["dt_bias_fwd_2"][0].partition_broadcast(128)),
          dma(SP, dbr[:, 16:32], A["dt_bias_bwd_2"][0].partition_broadcast(128)),
          dma(SP, Ar[:, 0:16], A["A_log_fwd_2"][0].partition_broadcast(128)),
          dma(SP, Ar[:, 16:32], A["A_log_bwd_2"][0].partition_broadcast(128)),
          dma(SP, Dr[:, :], A["D_skip_2"][0].partition_broadcast(128))]
    XS = [sbt(ph, [128, NT, 256]) for _ in range(2)]
    BC = [[sbt(ph, [128, S]), sbt(ph, [128, S]), sbt(ph, [128, NT, 128])] for _ in range(2)]
    y = sbt(ph, [128, NT, 512])
    PR = [sbt(ph, [128, S + 4])]
    for p in PR:
        PO(G.memset, p[:, 0:2], 0.0)
        t = PO(G.memset, p[:, S + 2:S + 4], 0.0)
    pz = t
    Pad = Ring(PR)
    Acc = Ring([sbt(ph, [128, S]) for _ in range(2)])
    Er = Ring([sbt(ph, [128, 4, 128]) for _ in range(4)])
    Tr = Ring([sbt(ph, [128, 512]) for _ in range(1)])
    Xw = Ring([sbt(ph, [128, 256]) for _ in range(2)])
    Cb = Ring([sbt(ph, [128, 128]) for _ in range(3)])
    Ust, Lst = sbt(ph, [128, 128]), sbt(ph, [128, 128])
    DV(V.tensor_tensor, Ust[:, :], Uinc[:, :], ident[:, :], SUB)
    tstr = DV(V.tensor_tensor, Lst[:, :], Linc[:, :], ident[:, :], SUB)
    St = [sbt(ph, [128, 256]) for _ in range(2)]
    ysp = []
    tX, tB, gone, ytok, tz_ = {}, {}, {}, {}, {}
    h4 = [128, 4, 64]

    def hv(x):
        return x.rearrange("p (h d) -> p h d", h=4)

    small = []
    flat = (lambda x: x[:, :, :].rearrange("p a b -> p (a b)"))

    def ssm_steps():
        u = unit(W, [(2560, 32)])
        a, b = Acc.get(), None
        for th in range(2):
            b = PD.get()
            sl = slice(th * 512, th * 512 + 512)
            pairs = []
            for k in range(8):
                pairs += three(u.h[:, k, 0:32], u.l[:, k, 0:32], HTh[:, k, sl], HTl[:, k, sl])
            t = mms(b.t[0:32, :], pairs, b.w + u.w + HT.w)
            t = AC(C.copy, a.t[0:32, sl], b.t[0:32, :], w=[t] + a.w)
            b.w = [t]
        u.done()
        b = PB.get()
        for tt in range(8):
            t = PE(T.transpose, b.t[:, tt * 32:tt * 32 + 32], a.t[0:32, tt * 128:tt * 128 + 128],
                   ident[0:32, 0:32], w=b.w + [t], inc=(tt == 7))
        a.w = [t]
        yield
        t = DV(V.tensor_tensor, dt_[:, :, :], b.t[:, 0:256].rearrange("p (a b) -> p a b", a=8),
               bc(dbr[:, :].unsqueeze(1), [128, 8, 32]), ADD, w=[t] + ct)
        b.w = [t]
        t1 = AC(C.activation, flat(wd), flat(dt_), ACT.Abs, w=[t])
        t1 = AC(C.activation, flat(wd), flat(wd), ACT.Exp, scale=-1.0, w=[t1])
        yield
        t1 = AC(C.activation, flat(wd), flat(wd), ACT.Ln, bias=1.0, w=[t1])
        tA = AC(C.activation, Ar[:, :], Ar[:, :], ACT.Exp, w=ct)
        t = DV(V.scalar_tensor_tensor, dt_[:, :, :], dt_[:, :, :], 0.0, wd[:, :, :], MAX, ADD, w=[t1])
        t = DV(V.scalar_tensor_tensor, dA[:, :, :], dt_[:, :, :], -1.0, bc(Ar[:, :].unsqueeze(1), [128, 8, 32]),
               MUL, MUL, w=[t, tA])
        yield
        b = PB.get()
        bvv = b.t[:, 0:256].rearrange("p (a b) -> p a b", a=8)
        mms(bvv[:, :, 0:16], [(Uinc[:, :], dA[:, :, 0:16])], b.w + [t], inc=False)
        mms(bvv[:, :, 16:32], [(Linc[:, :], dA[:, :, 16:32])], (), inc=False)
        t = mms(b.t[:, 256:512], [(ones[:, :], flat(dA))], ())
        t1 = DV(V.tensor_copy, acs[:, :, :], bvv, w=[t])
        yield
        t1 = DV(V.tensor_tensor, flat(wd), b.t[:, 256:512], flat(acs), SUB, w=[t1])
        t2 = AC(C.activation, flat(dcy), b.t[:, 256:512], ACT.Exp, w=[t1])
        b.w = [t2, t1]
        t3 = AC(C.activation, flat(wd), flat(wd), ACT.Exp, w=[t1])
        t4_ = AC(C.activation, flat(ea), flat(acs), ACT.Exp, w=[t1])
        tw = DV(V.tensor_tensor, flat(wd), flat(wd), flat(dt_), MUL, w=[t3])
        small.extend([tw, t4_, t2, t1])

    def ssm_dense(i):
        g, half = i // 2, i % 2
        xs, (BT, CT, Bt) = XS[i % 2], BC[g]
        w0 = gone.get(i - 2, [])
        for n in ([1, 0] if half == 0 else [0]):
            if n == 0:
                u = unit(W, [(1024 + i * 256, 256)])
                ms = [2 * i, 2 * i + 1]
            else:
                u = unit(W, [(2048 + g * 128, 128), (2304 + g * 128, 128)])
                ms = [8 + g, 10 + g]
            for mi, m in enumerate(ms):
                p = Pad.get()
                for th in range(2):
                    b, t = fm(u, mi * 128, th)
                    tp = AC(C.copy, p.t[:, 2 + th * 512:2 + th * 512 + 512], b.t[:, :], w=[t, pz] + p.w)
                    b.w = [tp]
                    yield
                a = Acc.get()
                t = AC(C.activation, a.t[:, :], p.t[:, 0:S], ACT.Identity, scale=pc("cw2", m), bias=pc("cb2", m),
                       w=[tp] + a.w)
                for j in range(1, 5):
                    t = DV(V.scalar_tensor_tensor, a.t[:, :], p.t[:, j:j + S], pc("cw2", 12 * j + m), a.t[:, :],
                           MUL, ADD, w=[t])
                    yield
                p.w = [t]
                dst = a.t if m < 8 else (BT if m == 8 + g else CT)
                t = AC(C.activation, dst[:, :], a.t[:, :], ACT.Silu, w=[t] + w0)
                tB.setdefault(g, []).append(t)
                last = t
                if m != 10 + g:
                    for th in range(2):
                        b = PB.get()
                        for j in range(4):
                            tt = th * 4 + j
                            last = PE(T.transpose, b.t[:, j * 128:(j + 1) * 128], dst[:, tt * 128:(tt + 1) * 128],
                                      ident[:, :], w=b.w + [t], inc=(j == 3))
                        o = xs[:, th * 4:th * 4 + 4, (m % 2) * 128:(m % 2) * 128 + 128] if m < 8 else \
                            Bt[:, th * 4:th * 4 + 4, :]
                        t2 = AC(C.copy, o, b.t[:, :].rearrange("p (a c) -> p a c", a=4), w=[last] + w0)
                        b.w = [t2]
                        (tX.setdefault(i, []) if m < 8 else tB[g]).append(t2)
                        yield
                a.w = [last]
            u.done()

    def ssm_skip(i):
        g, half = i // 2, i % 2
        xs = XS[i % 2]
        for tt in range(NT):
            ytok[tt] = PO(G.tensor_tensor, hv(y[:, tt, half * 256:half * 256 + 256]), hv(xs[:, tt, :]),
                          bc(Dr[:, i * 4:i * 4 + 4].unsqueeze(2), h4), MUL, w=tX[i] + [ct[4]] + gone.get("y", []))

    def ssm_scan(i, d):
        g, half = i // 2, i % 2
        xs, (BT, CT, Bt) = XS[i % 2], BC[g]
        S_ = St[d]
        tri, strict = (Uinc, Lst) if d == 0 else (Linc, Ust)
        h0 = d * 16 + i * 4
        hs = slice(h0, h0 + 4)
        order = list(range(8)) if d == 0 else list(range(7, -1, -1))
        ts, tz = None, gone.get("s%d" % d)

        def scaled(tt):
            e = Er.get()
            for j in range(4):
                te = AC(C.mul, e.t[:, j, :], strict[:, :], dA[:, tt, h0 + j:h0 + j + 1], w=small + e.w + [tstr])
            return tt, e, te

        def front(tt, e, te):
            sl = slice(tt * 128, tt * 128 + 128)
            b = PB.get()
            t = mms(b.t[:, 0:128], [(BT[:, sl], CT[:, sl])], b.w + tB[g])
            cb = Cb.get()
            tcb = DV(V.tensor_tensor, cb.t[:, :], b.t[:, 0:128], tri[:, :], MUL, w=[t] + cb.w)
            b.w = [tcb]
            b = PB.get()
            for j in range(4):
                t = mms(b.t[:, j * 128:(j + 1) * 128], [(e.t[:, j, :], tri[:, :])], b.w + [te], inc=(j == 3))
            te = AC(C.activation, e.t[:, :, :], b.t[:, :].rearrange("p (a c) -> p a c", a=4), ACT.Exp, w=[t])
            b.w = [te]
            return tt, cb, tcb, e, te

        pend = front(*scaled(order[0]))
        yield
        for n, tt in enumerate(order):
            _, cb, tcb, e, te = pend
            sl = slice(tt * 128, tt * 128 + 128)
            Y = PD.get()
            if n > 0:
                t = mms(Y.t[:, 256:512], [(CT[:, sl], S_[:, :])], Y.w + [ts] + tB[g], inc=False)
            if n < 7:
                xw = Xw.get()
                txw = PO(G.tensor_tensor, hv(xw.t[:, :]), hv(xs[:, tt, :]), bc(wd[:, tt, hs].unsqueeze(2), h4),
                         MUL, w=tX[i] + small + xw.w)
            for j in range(4):
                tg = DV(V.scalar_tensor_tensor, e.t[:, j, :], e.t[:, j, :], dt_[:, tt, h0 + j:h0 + j + 1],
                        cb.t[:, :], MUL, MUL, w=[te, tcb])
            cb.w = [tg]
            if n < 7:
                nxt = scaled(order[n + 1])
            yield
            if n < 7:
                pend = front(*nxt)
            yield
            for j in range(4):
                t = mms(Y.t[:, j * 64:j * 64 + 64], [(e.t[:, j, :], xs[:, tt, j * 64:j * 64 + 64])],
                        Y.w + [tg] + tX[i], inc=(j == 3))
            tz = [t]
            e.w = [t]
            yv = y[:, tt, half * 256:half * 256 + 256]
            ty = DV(V.tensor_tensor, yv, Y.t[:, 0:256], yv, ADD, w=[t, ytok[tt]])
            if n > 0:
                tr = Tr.get()
                t = DV(V.tensor_tensor, hv(tr.t[:, 0:256]), hv(Y.t[:, 256:512]), bc(ea[:, tt, hs].unsqueeze(2), h4),
                       MUL, w=small + tr.w)
                ty = DV(V.tensor_tensor, yv, yv, tr.t[:, 0:256], ADD, w=[t, ty])
                tr.w = [ty]
                Y.w = [t]
            else:
                Y.w = [ty]
            ytok[tt] = ty
            yield
            if n < 7:
                b = PB.get()
                t = mms(b.t[:, 0:256], [(Bt[:, tt, :], xw.t[:, :])], b.w + [txw] + tB[g])
                xw.w = [t]
                if n == 0:
                    ts = DV(V.tensor_copy, S_[:, :], b.t[:, 0:256], w=[t] + (tz if tz else []))
                else:
                    t1 = DV(V.tensor_tensor, hv(S_[:, :]), hv(S_[:, :]), bc(dcy[:, tt, hs].unsqueeze(2), h4),
                            MUL, w=tz + [ts])
                    ts = DV(V.tensor_tensor, S_[:, :], b.t[:, 0:256], S_[:, :], ADD, w=[t, t1])
                b.w = [ts]
            yield

    def ssm_gate(i):
        u = unit(W, [(i * 256, 256)])
        for n in range(2):
            a = Acc.get()
            for th in range(2):
                t4 = 2 * n + th
                b, t = tm(u, 0, 256, [2 * t4, 2 * t4 + 1])
                t = AC(C.activation, a.t[:, th * 512:th * 512 + 512], b.t[:, :], ACT.Silu, w=[t] + a.w)
                b.w = [t]
                if th == 1:
                    tz_[i, n] = dma(SP, ZS[i * 2 + n], a.t[:, :], w=[t])
                    a.w = [tz_[i, n]]
                yield
        u.done()

    def ssm_fetch(i):
        for n in range(2):
            a = Acc.get()
            tz_[i, n] = a, dma(SP, a.t[:, :], ZS[i * 2 + n], w=a.w + [tz_[i, n]])

    def ssm_mul(i):
        half = i % 2
        for n in range(2):
            a, td = tz_[i, n]
            o = y[:, 4 * n:4 * n + 4, half * 256:(half + 1) * 256]
            t = DV(V.tensor_tensor, o, o, a.t[:, :].rearrange("p (a c) -> p a c", a=4), MUL,
                   w=[td] + [ytok[4 * n + j] for j in range(4)])
            for j in range(4):
                ytok[4 * n + j] = t
            a.w = [t]

    def ssm_out(g):
        for tt in range(8):
            tr = Tr.get()
            t = AC(C.activation, tr.t[:, :], y[:, tt, :], ACT.Square, accum_out=ss[:, tt:tt + 1],
                   w=[ytok[tt]] + tr.w)
            tr.w = [t]
        t = rsqrt(st[:, 0:8], ss[:, 0:8], 1.0 / 512, 1e-5, [t])
        t = DV(V.tensor_tensor, y[:, :, :], y[:, :, :], bc(st[:, 0:8].unsqueeze(2), [128, 8, 512]), MUL, w=[t])
        for m in range(4):
            a = Acc.get()
            for th in range(2):
                b = PB.get()
                for j in range(4):
                    t_ = PE(T.transpose, b.t[:, j * 128:(j + 1) * 128], y[:, th * 4 + j, m * 128:(m + 1) * 128],
                            ident[:, :], w=b.w + [t], inc=(j == 3))
                ty = AC(C.mul, a.t[:, th * 512:th * 512 + 512], b.t[:, :], pc("ssm_g", g * 4 + m), w=[t_] + a.w)
                b.w = [ty]
            r = (g * 4 + m) * 128
            ysp.append(dma(SP, YM[r:r + 128, :], a.t[:, :], w=[ty]))
            a.w = [ysp[-1]]
            yield
        gone["y"] = [PE.now()]

    def ssm_side(i):
        if i != 1:
            yield from ssm_gate(i)
        if i < 3:
            yield from ssm_dense(i + 1)
        if i == 0:
            yield from ssm_gate(1)
        ssm_fetch(i)

    weave((ssm_steps(), 30), (ssm_dense(0), 30))
    for i in range(4):
        ssm_skip(i)
        parts = [(ssm_scan(i, 0), 33), (ssm_scan(i, 1), 33)]
        if i != 2:
            side = ssm_side(i)
        parts.append((side, [24, 26, 16, 4][i]))
        weave(*parts)
        ssm_mul(i)
        gone[i] = [PE.now(), DV.now(), PO.now()]
        if i % 2 == 1:
            side = ssm_side(2) if i == 1 else iter(())
            weave((ssm_out(i // 2), 5), (islice(side, 4), 5))
            gone[i] = [PE.now(), DV.now(), PO.now()]
    fence()
    ph.close()

    ph = ExitStack()
    WD = 1920
    bias = sbt(ph, [128, WD])
    QS = [sbt(ph, [128, S], F32R) for _ in range(2)]
    KS = [sbt(ph, [128, S], F32R) for _ in range(2)]
    KL = sbt(ph, [128, S], F32R)
    HB = [[sbt(ph, [128, S]), sbt(ph, [128, NT, 128])] for _ in range(2)]
    SR = Ring([sbt(ph, [128, 2, S]) for _ in range(3)])
    WT = Ring([sbt(ph, [128, 8, 512])])
    tmp = Ring([sbt(ph, [128, 512]) for _ in range(2)])
    sm = Ring([sbt(ph, [128, 8]) for _ in range(4)])
    o128 = sbt(ph, [128, 128])
    epsc = sbt(ph, [128, 1])
    to128 = DV(V.memset, o128[:, :], 1.0 / 128)
    teps = DV(V.memset, epsc[:, :], 1e-5)
    PQ = [Slot(PQt[0]), Slot(PQt[1])]
    t = PO(G.iota, bias[:, :], pattern=[[-1, WD]], base=896, channel_multiplier=1,
           allow_small_or_imprecise_dtypes=True)
    tbias = [AC(C.activation, bias[:, :], bias[:, :], ACT.Abs, w=[t])]
    tD, tQ, scored, hgone = {}, {}, {}, {}

    LO, HI = slice(0, 64), slice(64, 128)

    def att_vg(h):
        gT, vt = HB[h % 2]
        w0 = hgone.get(h - 2, [])
        tD[h] = []
        u = unit(W, [(4640 + h * 128, 128), (5664 + h * 128, 128)])
        for th in range(2):
            b, t = fm(u, 0, th)
            vT = tmp.get()
            t = AC(C.copy, vT.t[:, :], b.t[:, :], w=[t] + vT.w)
            b.w = [t]
            yield
            b = PD.get()
            for j in range(4):
                t_ = PE(T.transpose, b.t[:, j * 128:(j + 1) * 128], vT.t[:, j * 128:(j + 1) * 128],
                        ident[:, :], w=b.w + [t], inc=(j == 3))
            t2 = AC(C.copy, vt[:, th * 4:th * 4 + 4, :], b.t[:, :].rearrange("p (a c) -> p a c", a=4), w=[t_] + w0)
            b.w, vT.w = [t2], [t_]
            tD[h].append(t2)
            yield
        for th in range(2):
            b, t = fm(u, 128, th)
            t = AC(C.activation, gT[:, th * 512:th * 512 + 512], b.t[:, :], ACT.Silu, w=[t] + w0)
            b.w = [t]
            tD[h].append(t)
            yield
        u.done()

    def att_qk(h):
        tQ[h] = [[], [], []]
        u = unit(W, [(2592 + h * 128, 128), (3616 + h * 128, 128)])
        for m in (1, 0):
            for th in range(2):
                sl = slice(th * 512, th * 512 + 512)
                b, t = fm(u, m * 128, th)
                w = [t] + (scored[h - 1] if h else [])
                D = QS if m == 0 else KS
                AC(C.copy, D[0][LO, sl], b.t[LO, :], w=w)
                ta = AC(C.copy, D[1][HI, sl], b.t[HI, :])
                if m == 0:
                    L0, L1 = D[0][HI, sl], D[1][LO, sl]
                else:
                    AC(C.copy, D[0][HI, sl], b.t[LO, :])
                    ta = AC(C.copy, D[1][LO, sl], b.t[HI, :])
                    L0, L1 = KL[LO, sl], KL[HI, sl]
                DV(V.tensor_tensor, L0, b.t[LO, :], D[0][LO, sl].bitcast(F32), SUB, w=w + [ta])
                te = DV(V.tensor_tensor, L1, b.t[HI, :], D[1][HI, sl].bitcast(F32), SUB)
                b.w = [te]
                tQ[h][2 if m else th] += [ta, te]
                yield
        u.done()

    def att(h):
        gT, vt = HB[h % 2]
        tbias[0] = AC(C.mul, bias[:, :], bias[:, :], -4.0 if h == 0 else 0.5, w=[tbias[0], DV.now()])
        tb = tbias[0]

        def scores(tt):
            s, x = SR.get(), sm.get()
            qk = []
            for sh in range(2):
                for r in range(2):
                    qs, ks = slice(tt * 128, tt * 128 + 128), slice(sh * 512, sh * 512 + 512)
                    rows = HI if r else LO
                    qk.append(mms(PQ[r].t[:, ks], [(QS[r][:, qs], KS[r][:, ks]), (QS[r][rows, qs], KL[rows, ks])],
                                  PQ[r].w + tQ[h][2] + tQ[h][tt // 4]))
            if tt == 7:
                scored[h] = [qk[-1]]
            for r in range(2):
                t = DV(V.tensor_tensor_reduce, out=s.t[:, r, :], in0=PQ[r].t[:, :],
                       in1=bias[:, 896 - 128 * tt:896 - 128 * tt + 1024], scale=0.125, scalar=-3.0e38,
                       op0=ADD, op1=MAX, accum_out=x.t[:, r:r + 1], w=[qk[2 + r], tb] + s.w + x.w)
                PQ[r].w = [t]
            t = DV(V.tensor_scalar, x.t[:, 2:4], x.t[:, 0:2], -1.0, None, MUL, w=[t])
            for r in range(2):
                t2 = AC(C.activation, s.t[:, r, :], s.t[:, r, :], ACT.Exp, bias=x.t[:, 2 + r:3 + r],
                        accum_out=x.t[:, 4 + r:5 + r], w=[t])
            return tt, s, x, t2

        def scaled(tt, s, x, t2):
            t = DV(V.reciprocal, x.t[:, 6:8], x.t[:, 4:6], w=[t2])
            t0 = AC(C.mul, s.t[:, 0, :], s.t[:, 0, :], x.t[:, 6:7], w=[t])
            t = DV(V.tensor_tensor, x.t[:, 5:6], x.t[:, 7:8], lam[:, 3:4], MUL, w=[t])
            return s, x, t0, t

        def mixed(s, x, t0, t):
            t = DV(V.scalar_tensor_tensor, s.t[:, 0, :], s.t[:, 1, :], x.t[:, 5:6], s.t[:, 0, :], MUL, ADD,
                   w=[t, t0])
            x.w = [t]
            return t

        wt, wtoks = None, []
        pend = [scores(0)]
        yield
        ready = scaled(*pend.pop())
        pend = [scores(1)]
        yield
        for tt in range(NT):
            if tt % 4 == 0:
                wt, wtoks = WT.get(), []
            s = ready[0]
            t = mixed(*ready)
            yield
            if tt < 7:
                ready = scaled(*pend.pop())
            if tt < 6:
                pend = [scores(tt + 2)]
            yield
            for q2 in range(2):
                b = PD.get()
                for j in range(4):
                    t_ = PE(T.transpose, b.t[:, j * 128:(j + 1) * 128],
                            s.t[:, 0, (q2 * 4 + j) * 128:(q2 * 4 + j + 1) * 128], ident[:, :], w=b.w + [t],
                            inc=(j == 3))
                o = wt.t[:, q2 * 4:q2 * 4 + 4, (tt % 4) * 128:(tt % 4) * 128 + 128]
                i_ = b.t[:, :].rearrange("p (a c) -> p a c", a=4)
                if q2 == 0:
                    t2 = AC(C.copy, o, i_, w=[t_] + wt.w)
                else:
                    t2 = DV(V.tensor_copy, o, i_, w=[t_] + wt.w)
                b.w = [t2]
                wtoks.append(t2)
            s.w = [t_]
            yield
            if tt % 4 == 3:
                th = tt // 4
                sl = slice(th * 512, th * 512 + 512)
                b = PD.get()
                t_ = mms(b.t[:, :], [(vt[:, j, :], wt.t[:, j, :]) for j in range(8)], b.w + wtoks + tD[h])
                wt.w = [t_]
                o, q = tmp.get(), tmp.get()
                t1 = AC(C.copy, o.t[:, :], b.t[:, :], w=[t_] + o.w)
                t2 = AC(C.activation, q.t[:, :], b.t[:, :], ACT.Square, w=[t_] + q.w)
                b.w = [t2]
                b = PD.get()
                t2 = mms(b.t[:, :], [(o128[:, :], q.t[:, :])], b.w + [t2, to128])
                t2 = AC(C.activation, q.t[:, :], b.t[:, :], ACT.Ln, bias=epsc[:, 0:1], w=[t2, teps])
                b.w = [t2]
                t2 = AC(C.activation, q.t[:, :], q.t[:, :], ACT.Exp, scale=-0.5, w=[t2])
                gs = gT[:, sl]
                t1 = DV(V.scalar_tensor_tensor, gs, o.t[:, :], pc("subln"), gs, MUL, MUL, w=[t1] + tD[h])
                ty = DV(V.tensor_tensor, gs, gs, q.t[:, :], MUL, w=[t1, t2])
                o.w, q.w = [t1], [ty]
                r = (8 + h) * 128
                ysp.append(dma(SP, YM[r:r + 128, sl], gs, w=[ty]))
                yield
        hgone[h] = [PE.now(), DV.now()] + ysp[-2:]

    steps(att_vg(0))
    steps(att_qk(0))
    for h in range(8):
        if h < 7:
            a = att(h)
            d = att_vg(h + 1)
            next(a)
            next(d)
            weave((islice(a, 18), 18), (d, 5))
            weave((a, 9), (att_qk(h + 1), 4))
        else:
            steps(att(h))
    fence()
    ph.close()

    ph = ExitStack()
    X = sbt(ph, [128, NT, 1024])
    phs = ExitStack()
    stage = Ring([sbt(phs, [128, S]) for _ in range(8)])
    load_HT(fetch(stage, YM[0:1024, :], ysp))
    xt = load_X(X, XD)
    gr, t1 = row_bcast(phs, A["ln_g_2"][0])
    br, t2 = row_bcast(phs, A["ln_b_2"][0])
    got = fetch(stage, YM[1024:2048, :], ysp)
    add_proj(X, A["w_out_2"][0], 0, xt, ALPHA)
    load_HT(got)
    wt = add_proj(X, A["w_out_2"][0], 1, xt)
    toks = layernorm(X, gr, br, wt, [t1, t2])
    if upto == 2:
        stx = store_X(X, out[0], [[x] for x in toks])
        phs.close()
        ph.close()
        finish(nc, ctx, PE, AC, DV, PO, SP, stx)
        return
    stx = store_X(X, XD, [[x] for x in toks])
    norm_HT(X, stage, [[x] for x in toks], "g3")
    fence()
    phs.close()
    ph.close()
    W = A["w_in_3"][0]
    ph = ExitStack()
    PR = [sbt(ph, [128, S + 30]) for _ in range(2)]
    for p in PR:
        pz = PO(G.memset, p[:, 0:30], 0.0)
    Pad = Ring(PR)
    Acc = Ring([sbt(ph, [128, S]) for _ in range(2)])
    Sg_ = Ring([sbt(ph, [128, S]) for _ in range(6)])
    o128 = sbt(ph, [128, 128])
    to128 = DV(V.memset, o128[:, :], 1.0 / 128)
    eps = sbt(ph, [128, 1])
    teps = DV(V.memset, eps[:, :], 1e-6)
    ycs = []

    def taps(k, g):
        return pc("cw3a", 8 * k + g) if k < 16 else pc("cw3b", 8 * (k - 16) + g)

    cin, cacc = {}, {}

    def conv_dense(g):
        u = unit(W, [(g * 128, 128), (1024 + g * 128, 128)])
        p, sg = Pad.get(), Sg_.get()
        for th in range(2):
            sl = slice(th * 512, th * 512 + 512)
            b1, t1 = fm(u, 128, th)
            t1 = AC(C.activation, sg.t[:, sl], b1.t[:, :], ACT.Sigmoid, w=[t1] + sg.w)
            b1.w = [t1]
            yield
            b2, t2 = fm(u, 0, th)
            tp = DV(V.tensor_tensor, p.t[:, 30 + th * 512:30 + th * 512 + 512], b2.t[:, :], sg.t[:, sl], MUL,
                    w=[t2, t1, pz] + p.w)
            b2.w = [tp]
            yield
        u.done()
        sg.w = [tp]
        cin[g] = (p, tp)

    def conv_light(g):
        p, tp = cin[g]
        a = Acc.get()
        t = AC(C.activation, a.t[:, :], p.t[:, 0:S], ACT.Identity, scale=taps(0, g), bias=pc("cb3", g),
               w=[tp] + a.w)
        for k in range(1, 31):
            t = DV(V.scalar_tensor_tensor, a.t[:, :], p.t[:, k:k + S], taps(k, g), a.t[:, :], MUL, ADD, w=[t])
            yield
        p.w = [t]
        cacc[g] = (a, t)

    def conv_tail(g):
        a, t = cacc[g]
        sg = Sg_.get()
        yield
        for th in range(2):
            sl = slice(th * 512, th * 512 + 512)
            b = PB.get()
            t1 = mms(b.t[:, :], [(o128[:, :], a.t[:, sl])], b.w + [t, to128])
            t1 = DV(V.tensor_tensor, a.t[:, sl], a.t[:, sl], b.t[:, :], SUB, w=[t1])
            b.w = [t1]
            yield
            t2 = AC(C.activation, sg.t[:, sl], a.t[:, sl], ACT.Square, w=[t1] + sg.w)
            yield
            b = PB.get()
            t2 = mms(b.t[:, :], [(o128[:, :], sg.t[:, sl])], b.w + [t2])
            t2 = AC(C.activation, sg.t[:, sl], b.t[:, :], ACT.Ln, bias=eps[:, 0:1], w=[t2, teps])
            b.w = [t2]
            t2 = AC(C.activation, sg.t[:, sl], sg.t[:, sl], ACT.Exp, scale=-0.5, w=[t2])
            yield
            t1 = DV(V.tensor_tensor, a.t[:, sl], a.t[:, sl], sg.t[:, sl], MUL, w=[t1, t2])
            yield
            t1 = AC(C.activation, sg.t[:, sl], a.t[:, sl], ACT.Silu, scale=pc("cng", g), bias=pc("cnb", g), w=[t1])
            yield
        a.w = [t1]
        ycs.append(dma(SP, YC[g * 128:(g + 1) * 128, :], sg.t[:, :], w=[t1]))
        sg.w = [ycs[-1]]

    zgs = []

    def gate_dense(n):
        u = unit(W, [(2048 + n * 256, 256)])
        for m in range(2):
            sg = Sg_.get()
            for th in range(2):
                b, t = fm(u, m * 128, th)
                t = AC(C.activation, sg.t[:, th * 512:th * 512 + 512], b.t[:, :], ACT.Silu, w=[t] + sg.w)
                b.w = [t]
                yield
            r = (n * 2 + m) * 128
            zgs.append(dma(SP, ZG[r:r + 128, :], sg.t[:, :], w=[t]))
            sg.w = [zgs[-1]]
        u.done()

    def conv_side(g):
        if g % 2 == 1:
            yield from gate_dense(g // 2)
        if g < 7:
            yield from conv_dense(g + 1)

    steps(conv_dense(0))
    for g in range(8):
        parts = [(conv_light(g), 31), (conv_side(g), 7 if g % 2 else 4)]
        if g > 0:
            parts.append((conv_tail(g - 1), 14))
        weave(*parts)
    steps(conv_tail(7))
    fence()
    ph.close()

    ph = ExitStack()
    M128 = sbt(ph, [128, S])
    lb, lb1 = sbt(ph, [128, 8]), sbt(ph, [128, 8])
    Mi = sbt(ph, [128, 8, 128], I32)
    Mf = sbt(ph, [128, 128])
    t = PO(G.memset, M128[:, :], 1.0)
    tM = PO(G.memset, M128[:, :].rearrange("p (c t) -> p c t", t=128)[:, :, 0:1], 0.0, w=[t])
    LV = [64, 32, 16, 8, 4, 2, 1]
    tm_ = []
    for l, w_ in enumerate(LV):
        nb = 64 // w_
        mfv = Mf[:, :].rearrange("p (b h t) -> p b h t", b=nb, h=2)
        t = PO(G.memset, Mf[:, :], 0.0, w=[DV.now(), PO.now()])
        t = PO(G.memset, mfv[:, :, 1, :], 1.0, w=[t])
        t = PO(G.affine_select, out=Mf[:, :], in_=Mf[:, :], compare_op=ALU.is_ge, fill=0.0, base=0,
               pattern=[[-2 * w_, nb], [0, 2 * w_]], channel_multiplier=1, w=[t])
        t = PO(G.affine_select, out=Mf[:, :], in_=Mf[:, :], compare_op=ALU.is_ge, fill=0.0, base=w_ - 1,
               pattern=[[2 * w_, nb], [0, 2 * w_]], channel_multiplier=-1, w=[t])
        tMi = DV(V.tensor_copy, Mi[:, l, :], Mf[:, :], w=[t])
    tMi = DV(V.tensor_copy, Mi[:, 7, :], ident[:, :])
    l0 = PC[:, col["lb0"]:col["lb0"] + 8]
    l1 = PC[:, col["lb1"]:col["lb1"] + 8]
    t = DV(V.tensor_tensor, lb1[:, :], l0, l1, MAX)
    t = DV(V.tensor_tensor, lb[:, :], l0, lb1[:, :], SUB, w=[t])
    t = DV(V.tensor_tensor, lb1[:, :], l1, lb1[:, :], SUB, w=[t])
    t = AC(C.activation, lb[:, :], lb[:, :], ACT.Exp, w=[t])
    t = AC(C.activation, lb1[:, :], lb1[:, :], ACT.Exp, w=[t])
    t = DV(V.tensor_tensor, lb1[:, :], lb[:, :], lb1[:, :], ADD, w=[t])
    t = DV(V.reciprocal, lb1[:, :], lb1[:, :], w=[t])
    t = DV(V.tensor_tensor, lb[:, :], lb[:, :], lb1[:, :], MUL, w=[t])
    tlb = DV(V.tensor_scalar, lb1[:, :], lb[:, :], -1.0, 1.0, MUL, ADD, w=[t])
    HB = [[sbt(ph, [128, S]) for _ in range(4)] + [sbt(ph, [128, NT, 128])] for _ in range(2)]
    vT = sbt(ph, [128, S])
    Dr_ = Ring([sbt(ph, [128, S]) for _ in range(3)])
    Zr = Ring([sbt(ph, [128, S]) for _ in range(3)])
    At = sbt(ph, [128, NT, 128])
    tAz = PO(G.memset, At[:, :, :], 0.0)
    kdt = sbt(ph, [128, NT, 128])
    O = sbt(ph, [128, NT, 128])
    Sr = Ring([sbt(ph, [128, 128]) for _ in range(2)])
    dec = sbt(ph, [128, 8])
    yh = []
    tD, rout, hgone = {}, {}, {}

    def rec_dense(h):
        qT, kT, bT, gT, vt = HB[h % 2]
        w0 = hgone.get(h - 2, [])
        tD[h] = []
        u = unit(W, [(4096 + h * 128, 128), (3072 + h * 128, 128)])
        for th in range(2):
            sl = slice(th * 512, th * 512 + 512)
            b, t = fm(u, 0, th)
            tf = AC(C.activation, bT[:, sl], b.t[:, :], ACT.Sigmoid, w=[t] + w0)
            tk = AC(C.activation, kT[:, sl], b.t[:, :], ACT.Sigmoid, scale=-1.0, w=[t] + w0)
            b.w = [tk]
            yield
        for th in range(2):
            b, t = fm(u, 128, th)
            tq = AC(C.activation, qT[:, th * 512:th * 512 + 512], b.t[:, :], ACT.Silu, w=[t] + w0)
            b.w = [tq]
            yield
        u.done()
        u = unit(W, [(5120 + h * 128, 128), (6144 + h * 128, 128)])
        for th in range(2):
            b, t = fm(u, 128, th)
            tq = AC(C.activation, gT[:, th * 512:th * 512 + 512], b.t[:, :], ACT.Silu,
                    w=[t] + w0 + (hgone["g", h - 2] if h > 1 else []))
            b.w = [tq]
            yield
        for th in range(2):
            b, t = fm(u, 0, th)
            t = AC(C.copy, vT[:, th * 512:th * 512 + 512], b.t[:, :], w=[t] + hgone.get("vT", []))
            b.w = [t]
            yield
        u.done()
        for th in range(2):
            b = PD.get()
            for j in range(4):
                tt = th * 4 + j
                t_ = PE(T.transpose, b.t[:, j * 128:(j + 1) * 128], vT[:, tt * 128:(tt + 1) * 128],
                        ident[:, :], w=b.w + [t], inc=(j == 3))
            tv = AC(C.copy, vt[:, th * 4:th * 4 + 4, :], b.t[:, :].rearrange("p (a c) -> p a c", a=4),
                    w=[t_] + w0)
            b.w = [tv]
            yield
        hgone["vT"] = [t_]
        tD[h] = [tv]

    def rec(h):
        q, k, bb, gT, v = HB[h % 2]
        q, k, bb = q[:, :], k[:, :], bb[:, :]
        td = tD[h]
        ow = hgone.get(h - 1, [])
        t = DV(V.tensor_scalar, bb, bb, lb1[:, h:h + 1], lb[:, h:h + 1], MUL, ADD, w=td + [tlb])
        tk2 = DV(V.tensor_scalar, k, k, lb1[:, h:h + 1], None, MUL)
        dd = Dr_.get()
        t = DV(V.tensor_scalar, bb, bb, 2.0 ** -63, None, MAX, w=[t])
        t = AC(C.activation, dd.t[:, :], bb, ACT.Ln, w=[t] + dd.w)
        tb = DV(V.tensor_tensor_scan, bb, M128[:, :], dd.t[:, :], 0.0, op0=MUL, op1=ADD, w=[t, tM])
        dd.w = [tb]
        yield
        tAs = [tAz, tAz]

        def front(l):
            if l == 7:
                return None, tk2
            w_ = LV[l]
            nb = S // (2 * w_)
            dd, z = Dr_.get(), Zr.get()

            def v4(x):
                return x.rearrange("p (b h t) -> p b h t", h=2, t=w_)
            ref = v4(bb)[:, :, 0, w_ - 1:w_]
            DV(V.tensor_tensor, v4(dd.t[:, :])[:, :, 0, :], bc(ref, [128, nb, w_]), v4(bb)[:, :, 0, :],
               SUB, w=[tb] + dd.w)
            t1 = DV(V.tensor_tensor, v4(dd.t[:, :])[:, :, 1, :], v4(bb)[:, :, 1, :], bc(ref, [128, nb, w_]), SUB)
            t1 = AC(C.activation, dd.t[:, :], dd.t[:, :], ACT.Exp, w=[t1])
            t2 = PO(G.tensor_tensor, v4(z.t[:, :])[:, :, 0, :], v4(k)[:, :, 0, :],
                    v4(dd.t[:, :])[:, :, 0, :], MUL, w=[t1, tk2] + z.w)
            t2 = PO(G.tensor_tensor, v4(z.t[:, :])[:, :, 1, :], v4(q)[:, :, 1, :],
                    v4(dd.t[:, :])[:, :, 1, :], MUL)
            dd.w = [t2]
            return z, t2

        def back(l, z, tz):
            for th in range(2):
                b = PB.get()
                for j in range(4):
                    sl = slice((th * 4 + j) * 128, (th * 4 + j) * 128 + 128)
                    l_, r_ = (z.t[:, sl], z.t[:, sl]) if l < 7 else (k[:, sl], q[:, sl])
                    t = mms(b.t[:, j * 128:(j + 1) * 128], [(l_, r_)], b.w + [tz] + td, inc=(j == 3))
                tAs[th] = DV(V.copy_predicated, At[:, th * 4:th * 4 + 4, :],
                             bc(Mi[:, l:l + 1, :], [128, 4, 128]),
                             b.t[:, :].rearrange("p (a c) -> p a c", a=4), w=[t, tMi, tAs[th]] + ow)
                b.w = [tAs[th]]
                yield
            if l < 7:
                z.w = [t]

        pend = [front(7), front(0)]
        yield
        for l in range(8):
            if l < 6:
                pend.append(front(l + 1))
            yield
            yield from back((l + 7) % 8, *pend.pop(0))
        bv = bb.rearrange("p (c t) -> p c t", t=128)
        dd = Dr_.get()
        t1 = DV(V.tensor_tensor, dd.t[:, :].rearrange("p (c t) -> p c t", t=128),
                bc(bv[:, :, 127:128], [128, 8, 128]), bv, SUB, w=[tb] + dd.w)
        t1 = AC(C.activation, dd.t[:, :], dd.t[:, :], ACT.Exp, w=[t1])
        tkd = DV(V.tensor_tensor, dd.t[:, :], k, dd.t[:, :], MUL, w=[t1, tk2])
        tdec = AC(C.activation, dec[:, :], bv[:, :, 127], ACT.Exp, w=[tkd])
        z = Zr.get()
        t1 = AC(C.activation, z.t[:, :], bb, ACT.Exp, w=[tb] + z.w)
        tqx = DV(V.tensor_tensor, z.t[:, :], q, z.t[:, :], MUL, w=[t1])
        yield
        for th in range(2):
            b = PB.get()
            for j in range(4):
                tt = th * 4 + j
                t = PE(T.transpose, b.t[:, j * 128:(j + 1) * 128], dd.t[:, tt * 128:(tt + 1) * 128],
                       ident[:, :], w=b.w + [tkd], inc=(j == 3))
            tkt = AC(C.copy, kdt[:, th * 4:th * 4 + 4, :], b.t[:, :].rearrange("p (a c) -> p a c", a=4), w=[t])
            b.w = [tkt]
            yield
        dd.w = [t]
        so = None
        for th in range(2):
            kvb = PB.get()
            for j in range(4):
                tt = th * 4 + j
                tkv = mms(kvb.t[:, j * 128:(j + 1) * 128], [(kdt[:, tt, :], v[:, tt, :])],
                          kvb.w + [tkt] + td, inc=(j == 3))
            ob = PB.get()
            for j in range(4):
                tt = th * 4 + j
                o = ob.t[:, j * 128:(j + 1) * 128]
                t = mms(o, [(At[:, tt, :], v[:, tt, :])] +
                        ([(z.t[:, tt * 128:(tt + 1) * 128], so.t[:, :])] if so else []),
                        ob.w + tAs + td + [tqx] + ([tso] if so else []))
                if tt < 7:
                    kv = kvb.t[:, j * 128:(j + 1) * 128]
                    sn = Sr.get()
                    if so is None:
                        tso = DV(V.tensor_copy, sn.t[:, :], kv, w=[tkv] + sn.w)
                    else:
                        tso = DV(V.scalar_tensor_tensor, sn.t[:, :], so.t[:, :], dec[:, tt:tt + 1], kv, MUL,
                                 ADD, w=[tkv, tso, tdec] + sn.w)
                        so.w = [t, tso]
                    so = sn
                else:
                    so.w = [t]
                if j < 3:
                    yield
            kvb.w = [tso]
            to = AC(C.copy, O[:, th * 4:th * 4 + 4, :], ob.t[:, :].rearrange("p (a c) -> p a c", a=4),
                    w=[t] + hgone.get("O", []))
            ob.w = [to]
            yield
        z.w = [t]
        rout[h] = to
        hgone[h] = [PE.now(), AC.now(), DV.now(), PO.now()]

    def rec_out(h):
        gT, to = HB[h % 2][3], rout[h]
        yield
        s = Dr_.get()
        t = rms_heads(O[:, :, :], 8, 128, s.t[:, :].rearrange("p (a c) -> p a c", a=8), [to] + s.w, 1e-6)
        s.w = [t]
        yield
        yield
        for th in range(2):
            b = PB.get()
            for j in range(4):
                t_ = PE(T.transpose, b.t[:, j * 128:(j + 1) * 128], O[:, th * 4 + j, :], ident[:, :],
                        w=b.w + [t], inc=(j == 3))
            gs = gT[:, th * 512:th * 512 + 512]
            ty = DV(V.scalar_tensor_tensor, gs, b.t[:, :], pc("ong", h), gs, MUL, MUL, w=[t_])
            b.w = [ty]
            yield
        hgone["O"] = [t_]
        r = (8 + h) * 128
        yh.append(dma(SP, YM[r:r + 128, :], gT[:, :], w=[ty]))
        hgone["g", h] = yh[-1:]

    steps(rec_dense(0))
    for h in range(8):
        parts = [(rec(h), 42)]
        if h > 0:
            parts.append((rec_out(h - 1), 18))
        if h < 7:
            parts.append((rec_dense(h + 1), 10))
        weave(*parts)
    steps(rec_out(7))
    fence()
    ph.close()

    ph = ExitStack()
    X = sbt(ph, [128, NT, 1024])
    ph3 = ExitStack()
    stage = Ring([sbt(ph3, [128, S]) for _ in range(8)])
    load_HT(fetch(stage, YC, ycs))
    got = fetch(stage, ZG, zgs)
    xt = load_X(X, XD)
    for n in range(4):
        u = unit(A["w_pw2_3"][0], [(n * 256, 256)])
        for m in range(2):
            g_, t = got[n * 2 + m]
            for th in range(2):
                b, t1 = fm(u, m * 128, th)
                o = g_.t[:, th * 512:th * 512 + 512]
                t = DV(V.scalar_tensor_tensor, o, b.t[:, :], pc("bpw", n * 2 + m), o, ADD, MUL, w=[t, t1])
                b.w = [t]
            got[n * 2 + m] = g_, t
        u.done()
    load_HT(got)
    got = fetch(stage, YM[1024:2048, :], yh)
    add_proj(X, A["w_out_3"][0], 0, xt)
    load_HT(got)
    wt = add_proj(X, A["w_out_3"][0], 1, xt)
    norm_HT(X, stage, wt, "peg")
    fence()
    ph3.close()
    ph2 = ExitStack()
    pin = sbt(ph2, [128, NT, 256])
    Ph = sbt(ph2, [128, 2, S], F32R)
    Pl = sbt(ph2, [128, 2, S], F32R)
    gtr = Ring([sbt(ph2, [128, 512]) for _ in range(8)])
    fg, t1f = row_bcast(ph2, A["final_g_3"])
    tp = dma(SP, pin[:, :, :], A["p_3"][0, 0].rearrange("(t p) d -> p t d", p=128))
    for k in range(2):
        for th in range(2):
            b = PB.get()
            for j in range(4):
                t = PE(T.transpose, b.t[:, j * 128:(j + 1) * 128], pin[:, th * 4 + j, k * 128:(k + 1) * 128],
                       ident[:, :], w=b.w + [tp], inc=(j == 3))
            sl = slice(th * 512, th * 512 + 512)
            t1 = AC(C.activation, Ph[:, k, sl], b.t[:, :], ACT.Copy, w=[t])
            tP = DV(V.tensor_tensor, Pl[:, k, sl], b.t[:, :], Ph[:, k, sl].bitcast(F32), SUB, w=[t1])
            b.w = [t1, tP]
    for n in range(4):
        u = unit(A["w_pg_3"][0], [(n * 256, 256)])
        gts = []
        for t4 in range(4):
            b, t = tm(u, 0, 256, [2 * t4, 2 * t4 + 1])
            gt = gtr.get()
            t = AC(C.activation, gt.t[:, :], b.t[:, :], ACT.Sigmoid, w=[t] + gt.w)
            b.w = [t]
            gts.append((gt, t))
        u.done()
        u = unit(A["w_pp_3"][0], [(n * 256, 256)], k=2)
        for t4 in range(4):
            gt, tg = gts[t4]
            b = PD.get()
            for j in range(2):
                sl = slice((2 * t4 + j) * 128, (2 * t4 + j) * 128 + 128)
                pairs = []
                for k in range(2):
                    pairs += three(Ph[:, k, sl], Pl[:, k, sl], u.h[:, k, :], u.l[:, k, :])
                t = mms(b.t[:, j * 256:(j + 1) * 256], pairs, b.w + u.w + [tP], inc=(j == 1))
            t = DV(V.tensor_tensor, gt.t[:, :], b.t[:, :], gt.t[:, :], MUL, w=[t, tg])
            b.w = [t]
            o = X[:, 2 * t4:2 * t4 + 2, n * 256:(n + 1) * 256]
            t = PO(G.tensor_tensor, o, o, gt.t[:, :].rearrange("p (a c) -> p a c", a=2), ADD, w=[t])
            gt.w = [t]
            wt[2 * t4] = wt[2 * t4 + 1] = [t]
        u.done()
    q0 = squares(X, 0, wt)
    q1 = squares(X, 1, wt)
    toks = rms_scale(X, 0, rstd(0, q0), fg, [t1f])
    toks += rms_scale(X, 1, rstd(1, q1), fg, [t1f])
    stx = store_X(X, out[0], toks)
    ph2.close()
    ph.close()
    finish(nc, ctx, PE, AC, DV, PO, SP, stx)


def finish(nc, ctx, PE, AC, DV, PO, SP, last):
    SP.later(lambda wait: wait(last))
    block = ctx.enter_context(nc.Block())

    @block.sync
    def _(e):
        SP.emit(e)

    @block.tensor
    def _(e):
        PE.emit(e)

    @block.vector
    def _(e):
        DV.emit(e)

    @block.scalar
    def _(e):
        AC.emit(e)

    @block.gpsimd
    def _(e):
        PO.emit(e)


_INS = [
    "x", "norm_mix_g", "w_in", "w_a2_fwd", "b_a_fwd", "w_a2_bwd", "b_a_bwd", "gla_norm_g", "sgu_norm_g", "w_s",
    "b_s", "w_out", "norm_mlp_g", "w_mlp1", "w_mlp2", "final_norm_g", "ln_emb_g_2", "ln_emb_b_2", "w_in_2",
    "conv_w_2", "conv_b_2", "A_log_fwd_2", "A_log_bwd_2", "dt_bias_fwd_2", "dt_bias_bwd_2", "D_skip_2",
    "ssm_norm_g_2", "lambda_q1_2", "lambda_k1_2", "lambda_q2_2", "lambda_k2_2", "subln_g_2", "w_out_2", "ln_g_2",
    "ln_b_2", "p_3", "ln_g_3", "w_in_3", "conv_w_3", "conv_b_3", "cnorm_g_3", "cnorm_b_3", "w_pw2_3", "b_pw2_3",
    "lb_logits_3", "onorm_g_3", "w_out_3", "pe_norm_g_3", "w_pg_3", "w_pp_3", "final_g_3",
]


def kernel(**inputs):
    import numpy as _np
    import concourse.bacc as _bacc
    from concourse import mybir as _mybir
    from concourse.bass_utils import run_bass_kernel_spmd as _run

    nc = _bacc.Bacc("TRN2", target_bir_lowering=False, num_devices=1)
    arrays, args = {}, {}
    for name in _INS:
        a = _np.ascontiguousarray(inputs[name])
        arrays[f"in_{name}_dram"] = a
        args[name] = nc.dram_tensor(f"in_{name}_dram", a.shape, _mybir.dt.from_np(a.dtype),
                                    kind="ExternalInput").ap()
    o = nc.dram_tensor("out_0_dram", (1, 1024, 1024), F32, kind="ExternalOutput").ap()
    build(nc, args, o)
    r = _run(nc, [arrays], core_ids=[0])
    return r.results[0]["out_0_dram"]
```
